# Optimizing a Trainium2 kernel written in Bass

```python
import jax, jax.numpy as jnp
from jax import lax
import numpy as np
import math

D_MODEL = 1024
BATCH = 1
SEQ = 512
DEPTH = 1

CHUNK = 64
GROUP_W = 512
N_GROUPS = 3
D_MIX = N_GROUPS * GROUP_W
H_A = 4
DH_A = GROUP_W // H_A
CONV_K = 4
POOL_WINDOWS = (2, 4, 8, 16)
N_POOL = len(POOL_WINDOWS)
DC_B = GROUP_W // N_POOL
H_C = 4
DH_C = GROUP_W // H_C
N_MEM = 256
EPS = 1e-6

_SIZES = (2 * GROUP_W, GROUP_W, GROUP_W, GROUP_W, 2 * H_A, GROUP_W, GROUP_W, GROUP_W, GROUP_W)
N_IN = sum(_SIZES)
_OFFS = tuple(int(v) for v in np.cumsum(_SIZES)[:-1])


def rmsnorm(x, g):
    xf = x.astype(jnp.float32)
    y = xf * lax.rsqrt(jnp.mean(xf * xf, axis=-1, keepdims=True) + EPS)
    return (y * g.astype(jnp.float32)).astype(x.dtype)

def causal_dwconv(x, w, b):
    S = x.shape[1]
    xp = jnp.pad(x, ((0, 0), (CONV_K - 1, 0), (0, 0)))
    return b + sum(xp[:, j:j + S] * w[j] for j in range(CONV_K))

def mlstm_chunkwise(q, k, v, ig, logf):
    B, S, H, D = q.shape
    NC, L = S // CHUNK, CHUNK
    to_c = lambda a: a.reshape(B, NC, L, H, D).transpose(0, 3, 1, 2, 4)
    q, k, v = to_c(q), to_c(k), to_c(v)
    ig = ig.reshape(B, NC, L, H).transpose(0, 3, 1, 2)
    logf = logf.reshape(B, NC, L, H).transpose(0, 3, 1, 2)
    b = jnp.cumsum(logf, axis=-1)
    bL = b[..., -1]
    g = bL[..., None] - b + ig
    gmax = jnp.max(g, axis=-1)
    w = jnp.exp(g - gmax[..., None])
    kv_loc = jnp.einsum('bhcld,bhcle->bhcde', k * w[..., None], v)
    n_loc = jnp.einsum('bhcld,bhcl->bhcd', k, w)

    def step(carry, inp):
        C, n, m = carry
        kv_c, n_c, bL_c, gmax_c = inp
        m_new = jnp.maximum(bL_c + m, gmax_c)
        a = jnp.exp(bL_c + m - m_new)
        bc = jnp.exp(gmax_c - m_new)
        C_new = a[..., None, None] * C + bc[..., None, None] * kv_c
        n_new = a[..., None] * n + bc[..., None] * n_c
        return (C_new, n_new, m_new), (C, n, m)

    init = (jnp.zeros((B, H, D, D), jnp.float32), jnp.zeros((B, H, D), jnp.float32),
            jnp.zeros((B, H), jnp.float32))
    mv = lambda a: jnp.moveaxis(a, 2, 0)
    _, (C_prev, n_prev, m_prev) = lax.scan(step, init, (mv(kv_loc), mv(n_loc), mv(bL), mv(gmax)))
    C_prev = jnp.moveaxis(C_prev, 0, 2)
    n_prev = jnp.moveaxis(n_prev, 0, 2)
    m_prev = jnp.moveaxis(m_prev, 0, 2)

    causal = jnp.tril(jnp.ones((L, L), dtype=bool))
    dmat = jnp.where(causal, b[..., :, None] - b[..., None, :] + ig[..., None, :], -jnp.inf)
    inter = b + m_prev[..., None]
    m_t = jnp.maximum(inter, jnp.max(dmat, axis=-1))
    s = jnp.einsum('bhcld,bhcsd->bhcls', q, k) * jnp.exp(dmat - m_t[..., None])
    a_t = jnp.exp(inter - m_t)
    num = a_t[..., None] * jnp.einsum('bhcld,bhcde->bhcle', q, C_prev) + jnp.einsum('bhcls,bhcse->bhcle', s, v)
    den = a_t * jnp.einsum('bhcld,bhcd->bhcl', q, n_prev) + jnp.sum(s, axis=-1)
    h = num / jnp.maximum(jnp.abs(den), jnp.exp(-m_t))[..., None]
    return h.transpose(0, 2, 3, 1, 4).reshape(B, S, H, D)

def mlstm_branch(qk_raw, v, o, ig, fg, conv_w, conv_b, norm_g):
    B, S, _ = v.shape
    f32 = jnp.float32
    qk = jax.nn.silu(causal_dwconv(qk_raw, conv_w, conv_b))
    q, k = jnp.split(qk, 2, axis=-1)
    q = q.astype(f32).reshape(B, S, H_A, DH_A)
    k = k.astype(f32).reshape(B, S, H_A, DH_A) * (DH_A ** -0.5)
    vh = v.astype(f32).reshape(B, S, H_A, DH_A)
    h = mlstm_chunkwise(q, k, vh, ig.astype(f32), jax.nn.log_sigmoid(fg.astype(f32)))
    h = jax.nn.sigmoid(o.astype(f32)).reshape(B, S, H_A, DH_A) * h
    h = h * lax.rsqrt(jnp.mean(h * h, axis=-1, keepdims=True) + EPS)
    h = h * norm_g.astype(f32).reshape(H_A, DH_A)
    return h.reshape(B, S, GROUP_W).astype(v.dtype)

def pool_branch(u, w, scale):
    B, S, _ = u.shape
    uf = u.astype(jnp.float32).reshape(B, S, N_POOL, DC_B)
    cs = jnp.cumsum(uf, axis=1)
    t1 = jnp.arange(1, S + 1, dtype=jnp.float32)
    pooled = []
    for gi, win in enumerate(POOL_WINDOWS):
        c = cs[:, :, gi]
        lo = jnp.pad(c, ((0, 0), (win, 0), (0, 0)))[:, :S]
        cnt = jnp.minimum(t1, float(win))[None, :, None]
        pooled.append((c - lo) / cnt)
    p = (jnp.stack(pooled, axis=2) - uf).astype(u.dtype)
    y = jnp.einsum('bsgc,gcd->bsgd', p, w).reshape(B, S, GROUP_W)
    return y * scale

def mem_attn_branch(qc, mem, mem_norm_g, w_kv):
    B, S, _ = qc.shape
    mn = rmsnorm(mem, mem_norm_g)
    kv = mn @ w_kv
    km, vm = jnp.split(kv, 2, axis=-1)
    km = km.reshape(B, N_MEM, H_C, DH_C)
    vm = vm.reshape(B, N_MEM, H_C, DH_C)
    q = qc.reshape(B, S, H_C, DH_C)
    s = jnp.einsum('bshd,bmhd->bhsm', q, km).astype(jnp.float32) * (DH_C ** -0.5)
    p = jax.nn.softmax(s, axis=-1).astype(vm.dtype)
    return jnp.einsum('bhsm,bmhd->bshd', p, vm).reshape(B, S, GROUP_W)

def first_inputs(seed: int = 0) -> dict:
    key = jax.random.key(seed)
    ks = jax.random.split(key, 16)
    nrm = jax.random.normal
    f32 = jnp.float32
    x = nrm(ks[0], (BATCH, SEQ, D_MODEL), f32)
    mem = nrm(ks[1], (BATCH, N_MEM, D_MODEL), f32)
    norm_g = 1.0 + 0.1 * nrm(ks[2], (DEPTH, D_MODEL), f32)
    w_in = nrm(ks[3], (DEPTH, D_MODEL, N_IN), f32) * D_MODEL ** -0.5
    b_i = 0.1 * nrm(ks[4], (DEPTH, H_A), f32)
    b_f = jnp.linspace(3.0, 6.0, H_A, dtype=f32)[None, :] + 0.1 * nrm(ks[5], (DEPTH, H_A), f32)
    b_gates = jnp.concatenate([b_i, b_f], axis=-1)
    conv_w = nrm(ks[6], (DEPTH, CONV_K, 2 * GROUP_W), f32) * CONV_K ** -0.5
    conv_b = 0.02 * nrm(ks[7], (DEPTH, 2 * GROUP_W), f32)
    mlstm_norm_g = 1.0 + 0.1 * nrm(ks[8], (DEPTH, GROUP_W), f32)
    pool_w = nrm(ks[9], (DEPTH, N_POOL, DC_B, DC_B), f32) * DC_B ** -0.5
    pool_scale = 1.0 + 0.1 * nrm(ks[10], (DEPTH, GROUP_W), f32)
    mem_norm_g = 1.0 + 0.1 * nrm(ks[11], (DEPTH, D_MODEL), f32)
    w_mem_kv = nrm(ks[12], (DEPTH, D_MODEL, 2 * GROUP_W), f32) * D_MODEL ** -0.5
    w_out = nrm(ks[13], (DEPTH, D_MIX, D_MODEL), f32) * D_MIX ** -0.5
    final_norm_g = 1.0 + 0.1 * nrm(ks[14], (D_MODEL,), f32)
    return {"x": x, "mem": mem, "norm_g": norm_g, "w_in": w_in, "b_gates": b_gates,
            "conv_w": conv_w, "conv_b": conv_b, "mlstm_norm_g": mlstm_norm_g,
            "pool_w": pool_w, "pool_scale": pool_scale, "mem_norm_g": mem_norm_g,
            "w_mem_kv": w_mem_kv, "w_out": w_out, "final_norm_g": final_norm_g}

def first_block(x, mem, norm_g, w_in, b_gates, conv_w, conv_b, mlstm_norm_g, pool_w, pool_scale,
              mem_norm_g, w_mem_kv, w_out, final_norm_g):
    for l in range(DEPTH):
        h = rmsnorm(x, norm_g[l])
        proj = h @ w_in[l]
        qk_raw, v, o, z_a, gates, u, z_b, qc, z_c = jnp.split(proj, _OFFS, axis=-1)
        gates = gates + b_gates[l]
        ig, fg = gates[..., :H_A], gates[..., H_A:]
        y_a = mlstm_branch(qk_raw, v, o, ig, fg, conv_w[l], conv_b[l], mlstm_norm_g[l]) * jax.nn.silu(z_a)
        y_b = pool_branch(u, pool_w[l], pool_scale[l]) * jax.nn.silu(z_b)
        y_c = mem_attn_branch(qc, mem, mem_norm_g[l], w_mem_kv[l]) * jax.nn.silu(z_c)
        x = x + jnp.concatenate([y_a, y_b, y_c], axis=-1) @ w_out[l]
    return rmsnorm(x, final_norm_g)


SG_CHUNK = 128
SG_WIDTH = D_MODEL
SG_GROUPS = 8
SG_GROUP_DIM = SG_WIDTH // SG_GROUPS
GLA_HEADS = 4
GLA_KEY_DIM = D_MODEL // 2
GLA_VAL_DIM = D_MODEL
GLA_HEAD_K = GLA_KEY_DIM // GLA_HEADS
GLA_HEAD_V = GLA_VAL_DIM // GLA_HEADS
GLA_GATE_RANK = 16
GLA_GATE_TEMP = 16.0
GLA_CHUNK = 64
D_FF = 4 * D_MODEL
LN_EPS = 1e-5
DEEPNORM_ALPHA = (2.0 * DEPTH) ** 0.25
DEEPNORM_BETA = (8.0 * DEPTH) ** -0.25
SPLITS = (SG_WIDTH, SG_WIDTH, GLA_KEY_DIM, GLA_KEY_DIM, GLA_VAL_DIM, GLA_VAL_DIM,
          GLA_GATE_RANK, D_MODEL, D_MODEL)
D_IN = sum(SPLITS)
SPLIT_POINTS = [int(s) for s in np.cumsum(SPLITS)[:-1]]


def layer_norm(x, g, b):
    xf = x.astype(jnp.float32)
    mu = jnp.mean(xf, axis=-1, keepdims=True)
    var = jnp.mean(jnp.square(xf - mu), axis=-1, keepdims=True)
    y = (xf - mu) * lax.rsqrt(var + LN_EPS) * g.astype(jnp.float32) + b.astype(jnp.float32)
    return y.astype(x.dtype)

def spatial_gating(u, v, ln_g, ln_b, w_s, b_s):
    bsz, t, _ = v.shape
    n = t // SG_CHUNK
    u = jax.nn.gelu(u)
    v = layer_norm(jax.nn.gelu(v), ln_g, ln_b)
    vc = v.reshape(bsz, n, SG_CHUNK, SG_GROUPS, SG_GROUP_DIM)
    causal = jnp.tril(jnp.ones((SG_CHUNK, SG_CHUNK), dtype=bool))
    ws = jnp.where(causal[None], w_s, jnp.zeros_like(w_s))
    mixed = jnp.einsum('gts,bnsgd->bntgd', ws, vc) + jnp.transpose(b_s)[:, :, None]
    return u * mixed.reshape(bsz, t, SG_WIDTH)

def gla_chunked(q, k, v, log_f):
    bsz, t, h, dk = q.shape
    dv = v.shape[-1]
    n = t // GLA_CHUNK

    def to_chunks(a):
        return a.astype(jnp.float32).reshape(bsz, n, GLA_CHUNK, h, a.shape[-1]).transpose(1, 0, 3, 2, 4)

    qc, kc, vc, gc = to_chunks(q * (GLA_HEAD_K ** -0.5)), to_chunks(k), to_chunks(v), to_chunks(log_f)
    causal = jnp.tril(jnp.ones((GLA_CHUNK, GLA_CHUNK), dtype=bool))[:, :, None]

    def step(state, inp):
        qb, kb, vb, gb = inp
        cum = jnp.cumsum(gb, axis=-2)
        diff = cum[..., :, None, :] - cum[..., None, :, :]
        decay = jnp.exp(jnp.where(causal, diff, -jnp.inf))
        scores = jnp.einsum('bhtd,bhsd,bhtsd->bhts', qb, kb, decay)
        o_intra = jnp.einsum('bhts,bhsv->bhtv', scores, vb)
        o_inter = jnp.einsum('bhtd,bhdv->bhtv', qb * jnp.exp(cum), state)
        total = cum[..., -1, :]
        k_dec = kb * jnp.exp(total[..., None, :] - cum)
        new_state = jnp.exp(total)[..., None] * state + jnp.einsum('bhsd,bhsv->bhdv', k_dec, vb)
        return new_state, o_intra + o_inter

    s0 = jnp.zeros((bsz, h, dk, dv), dtype=jnp.float32)
    _, out = lax.scan(step, s0, (qc, kc, vc, gc))
    return out.transpose(1, 0, 3, 2, 4).reshape(bsz, t, h, dv)

def second_inputs(seed: int = 0) -> dict:
    key = jax.random.key(seed)
    ks = jax.random.split(key, 20)
    f32 = jnp.float32
    x = jax.random.normal(ks[0], (BATCH, SEQ, D_MODEL), f32)
    w_in = jax.random.normal(ks[1], (DEPTH, D_MODEL, D_IN), f32) * D_MODEL ** -0.5
    col_scale = np.ones((D_IN,), np.float32)
    col_scale[:2 * SG_WIDTH] = DEEPNORM_BETA
    v0 = 2 * SG_WIDTH + 2 * GLA_KEY_DIM
    col_scale[v0:v0 + GLA_VAL_DIM] = DEEPNORM_BETA
    w_in = w_in * jnp.asarray(col_scale)
    b_in = 0.02 * jax.random.normal(ks[2], (DEPTH, D_IN), f32)
    sg_ln_g = 1.0 + 0.05 * jax.random.normal(ks[3], (DEPTH, SG_WIDTH), f32)
    sg_ln_b = 0.02 * jax.random.normal(ks[4], (DEPTH, SG_WIDTH), f32)
    sg_w_s = 0.5 * jax.random.normal(ks[5], (DEPTH, SG_GROUPS, SG_CHUNK, SG_CHUNK), f32) * SG_CHUNK ** -0.5
    sg_b_s = 1.0 + 0.1 * jax.random.normal(ks[6], (DEPTH, SG_GROUPS, SG_CHUNK), f32)
    gla_w_gate2 = jax.random.normal(ks[7], (DEPTH, GLA_GATE_RANK, GLA_KEY_DIM), f32) * GLA_GATE_RANK ** -0.5
    gla_b_gate = 0.1 * jax.random.normal(ks[8], (DEPTH, GLA_KEY_DIM), f32)
    gla_norm_g = 1.0 + 0.05 * jax.random.normal(ks[9], (DEPTH, GLA_VAL_DIM), f32)
    w_out = jax.random.normal(ks[10], (DEPTH, D_MODEL, D_MODEL), f32) * (D_MODEL ** -0.5 * DEEPNORM_BETA)
    ln1_g = 1.0 + 0.05 * jax.random.normal(ks[11], (DEPTH, D_MODEL), f32)
    ln1_b = 0.02 * jax.random.normal(ks[12], (DEPTH, D_MODEL), f32)
    w_ff1 = jax.random.normal(ks[13], (DEPTH, D_MODEL, D_FF), f32) * (D_MODEL ** -0.5 * DEEPNORM_BETA)
    w_ff2 = jax.random.normal(ks[14], (DEPTH, D_FF, D_MODEL), f32) * (D_FF ** -0.5 * DEEPNORM_BETA)
    ln2_g = 1.0 + 0.05 * jax.random.normal(ks[15], (DEPTH, D_MODEL), f32)
    ln2_b = 0.02 * jax.random.normal(ks[16], (DEPTH, D_MODEL), f32)
    return {'x': x, 'w_in': w_in, 'b_in': b_in, 'sg_ln_g': sg_ln_g, 'sg_ln_b': sg_ln_b,
            'sg_w_s': sg_w_s, 'sg_b_s': sg_b_s, 'gla_w_gate2': gla_w_gate2, 'gla_b_gate': gla_b_gate,
            'gla_norm_g': gla_norm_g, 'w_out': w_out, 'ln1_g': ln1_g, 'ln1_b': ln1_b,
            'w_ff1': w_ff1, 'w_ff2': w_ff2, 'ln2_g': ln2_g, 'ln2_b': ln2_b}

def second_block(x, w_in, b_in, sg_ln_g, sg_ln_b, sg_w_s, sg_b_s, gla_w_gate2, gla_b_gate,
              gla_norm_g, w_out, ln1_g, ln1_b, w_ff1, w_ff2, ln2_g, ln2_b):
    bsz, t, _ = x.shape
    h = x
    for l in range(DEPTH):
        p = jnp.einsum('btd,de->bte', h, w_in[l]) + b_in[l]
        a_u, a_v, q, k, v, r, a_low, g_a, g_b = jnp.split(p, SPLIT_POINTS, axis=-1)
        y_a = spatial_gating(a_u, a_v, sg_ln_g[l], sg_ln_b[l], sg_w_s[l], sg_b_s[l])
        log_f = jax.nn.log_sigmoid((a_low @ gla_w_gate2[l] + gla_b_gate[l]).astype(jnp.float32)) / GLA_GATE_TEMP
        o = gla_chunked(q.reshape(bsz, t, GLA_HEADS, GLA_HEAD_K),
                        k.reshape(bsz, t, GLA_HEADS, GLA_HEAD_K),
                        v.reshape(bsz, t, GLA_HEADS, GLA_HEAD_V),
                        log_f.reshape(bsz, t, GLA_HEADS, GLA_HEAD_K))
        o = o * lax.rsqrt(jnp.mean(jnp.square(o), axis=-1, keepdims=True) + LN_EPS)
        y_b = (o.reshape(bsz, t, GLA_VAL_DIM) * gla_norm_g[l].astype(jnp.float32)).astype(h.dtype) * jax.nn.silu(r)
        m = jax.nn.sigmoid(g_a) * y_a + jax.nn.sigmoid(g_b) * y_b
        h = layer_norm(DEEPNORM_ALPHA * h + m @ w_out[l], ln1_g[l], ln1_b[l])
        f = jnp.square(jax.nn.relu(h @ w_ff1[l])) @ w_ff2[l]
        h = layer_norm(DEEPNORM_ALPHA * h + f, ln2_g[l], ln2_b[l])
    return h


def setup_inputs(seed=0):
    out = dict(first_inputs(seed))
    for name, value in second_inputs(seed + 1).items():
        if name != "x":
            out[name + "_2"] = value
    return out


def reference(
    x, mem, norm_g, w_in, b_gates, conv_w, conv_b, mlstm_norm_g, pool_w, pool_scale, mem_norm_g,
    w_mem_kv, w_out, final_norm_g, w_in_2, b_in_2, sg_ln_g_2, sg_ln_b_2, sg_w_s_2, sg_b_s_2,
    gla_w_gate2_2, gla_b_gate_2, gla_norm_g_2, w_out_2, ln1_g_2, ln1_b_2, w_ff1_2, w_ff2_2,
    ln2_g_2, ln2_b_2,
):
    x = first_block(
        x, mem, norm_g, w_in, b_gates, conv_w, conv_b, mlstm_norm_g, pool_w, pool_scale,
        mem_norm_g, w_mem_kv, w_out, final_norm_g,
    )
    return second_block(
        x, w_in_2, b_in_2, sg_ln_g_2, sg_ln_b_2, sg_w_s_2, sg_b_s_2, gla_w_gate2_2,
        gla_b_gate_2, gla_norm_g_2, w_out_2, ln1_g_2, ln1_b_2, w_ff1_2, w_ff2_2, ln2_g_2,
        ln2_b_2,
    )


_drawn_inputs = setup_inputs


def setup_inputs(seed=0):
    import zlib

    import numpy as np

    out = dict(_drawn_inputs(seed))
    spreads = {}
    factors = {'conv_b': 8.0,
     'mem_norm_g': 8.0,
     'b_in_2': 6.169,
     'sg_ln_g_2': 53.465,
     'sg_ln_b_2': 200.0,
     'sg_b_s_2': 6.223,
     'gla_w_gate2_2': 3.219,
     'gla_b_gate_2': 7.963,
     'gla_norm_g_2': 6.806,
     'ln1_b_2': 2.818,
     'ln2_b_2': 2.738,
     'pool_scale': 2.736,
     'mlstm_norm_g': 2.744}
    for name, (base, spread) in spreads.items():
        noise = np.random.default_rng([zlib.crc32(name.encode()), seed]).standard_normal(out[name].shape)
        drawn = base * np.exp(spread * noise) if base else spread * noise
        out[name] = __import__('jax').numpy.asarray(drawn.astype(out[name].dtype))
    for name, factor in factors.items():
        out[name] = (out[name] * factor).astype(out[name].dtype)
    return out
```

```python
import numpy as np


P = 128
S = 512
D = 1024
TT = S // P
KC = D // P
NMEM = 256
MT = NMEM // P
H = 4
GW = 512
RMS_EPS = 1e-6
LN_EPS = 1e-5
SCALE = float(P) ** -0.5
ALPHA = 2.0 ** 0.25
LEVELS = 7
WINDOWS = (2, 4, 8, 16)
K1 = 1024
DV = 256
PAD = 8
ML_OFF = (0, 512, 896, 1152)


def block_list(a):
    w_in, w_kv, w_out = a["w_in"][0], a["w_mem_kv"][0], a["w_out"][0]
    w_in2, w_out2, w_ff1, w_ff2 = a["w_in_2"][0], a["w_out_2"][0], a["w_ff1_2"][0], a["w_ff2_2"][0]

    def chunks(w):
        return w.rearrange("(k p) n -> p k n", p=P)

    blocks = []

    def fm(name, w, c0, width):
        for c in range(c0, c0 + width, 256):
            blocks.append(("fm", name, chunks(w)[:, :, c:c + 256]))

    def tm(name, w, c0, width, groups):
        for c in range(c0, c0 + width, 512):
            for g in groups:
                blocks.append(("tm", name, chunks(w)[:, 4 * g:4 * g + 4, c:c + 512]))

    fm("km", w_kv, 0, GW)
    tm("vm", w_kv, GW, GW, (0, 1))
    fm("q", w_in, 0, GW)
    fm("k", w_in, GW, GW)
    tm("v", w_in, 2 * GW, GW, (0, 1))
    tm("o", w_in, 3 * GW, GW, (0, 1))
    z_a = 4 * GW
    u = 5 * GW + 2 * H
    fm("qc", w_in, u + 2 * GW, GW)
    fm("z_a", w_in, z_a, GW)
    fm("z_c", w_in, u + 3 * GW, GW)
    fm("u", w_in, u, GW)
    fm("z_b", w_in, u + GW, GW)
    tm("w_out", w_out, 0, D, (0, 2, 1))
    low = 5 * D
    blocks.append(("fm", "low", chunks(w_in2)[:, :, low:low + P]))
    fm("q2", w_in2, 2 * D, D // 2)
    fm("k2", w_in2, 2 * D + D // 2, D // 2)
    tm("v2", w_in2, 3 * D, D, (0, 1))
    tm("a_v", w_in2, D, D, (0, 1))
    fm("a_u", w_in2, 0, D)
    fm("g_a", w_in2, low + 16, D)
    fm("r", w_in2, 4 * D, D)
    fm("g_b", w_in2, low + 16 + D, D)
    tm("w_out2", w_out2, 0, D, (0, 1))
    fm("ff1", w_ff1, 0, 4 * D)
    tm("ff2", w_ff2, 0, D, range(8))
    return blocks


def two_blocks(nc, a, out, x1_spill):
    from concourse import mybir
    from contextlib import ExitStack

    f32 = mybir.dt.float32
    f32r = mybir.dt.float32r
    u8 = mybir.dt.uint8
    ALU = mybir.AluOpType
    ACT = mybir.ActivationFunctionType
    AX = mybir.AxisListType

    blocks = block_list(a)
    N = len(blocks)
    first = {}
    for n, (_, name, _) in enumerate(blocks):
        first.setdefault(name, n)

    def name_of(n):
        return blocks[n][1], n - first[blocks[n][1]]

    base = 16512
    top = [base]

    def at(name, shape, offset, dt=f32):
        return nc.alloc_sbuf_tensor_at(name, shape, dt, offset=offset)

    def place(name, shape, dt=f32, size=4):
        n = int(np.prod(shape[1:])) * size
        t = at(name, shape, top[0], dt)
        top[0] += (n + 31) // 32 * 32
        return t

    RAW = [place(f"w_raw{i}", [P, 2048]) for i in range(2)]
    WH = [place(f"w_hi{i}", [P, 2048], f32r) for i in range(2)]
    WL = [place(f"w_lo{i}", [P, 2048], f32r) for i in range(2)]
    XS = top[0]
    top[0] += 32 * K1
    TH = place("act_t_hi", [P, KC, S], f32r)
    TL = place("act_t_lo", [P, KC, S], f32r)
    A = top[0]
    top[0] += 88 * K1

    IDENT = place("ident", [P, P])
    TRIU = place("triu", [P, P])
    TRI16 = place("triu_16th", [P, P])
    ONES = place("ones", [P, P])
    MASK = place("level_masks", [P, LEVELS + 1, P], u8, 1)
    VC = place("vector_columns", [P, P])
    WG = place("w_gates", [P, KC, 2 * H])
    WGH = place("w_gates_hi", [P, KC, 2 * H], f32r)
    WGL = place("w_gates_lo", [P, KC, 2 * H], f32r)
    BG = place("b_gates_all", [P, 2 * H])
    PINV = place("pool_edge", [P, 4, 16])
    LOWB = place("low_bias", [16, 1])
    NHALF = place("minus_half", [P, 16])
    SSQ = place("mean_squares", [P, 16])
    RST = place("rstd", [P, 16])
    RTMP = place("rstd_tmp", [P, 16])
    G8 = place("gates", [P, TT, 2 * H])
    LF = place("log_f", [P, TT, H])
    GT1 = place("gate_tmp", [P, TT, H])
    GG = place("i_minus_F", [P, TT, H])
    FS = place("F", [P, TT, H])
    FLOOR = place("den_floor", [P, TT, H])
    RDEN = place("den", [P, TT])
    SMX = place("neg_max", [P, H])
    SSUM = place("row_sum", [P, H])
    BN = place("bn", [P, 2, 6])
    MV = place("mean_var", [P, TT, 2])
    ETOT = place("exp_total", [P, H * TT])
    assert top[0] <= 229344, top[0]

    XH = [at(f"x_hi{i}", [P, 2048], XS + 8 * K1 * i, f32r) for i in range(2)]
    XL = [at(f"x_lo{i}", [P, 2048], XS + 16 * K1 + 8 * K1 * i, f32r) for i in range(2)]
    MEMH = at("mem_t_hi", [P, KC, NMEM], XS, f32r)
    MEML = at("mem_t_lo", [P, KC, NMEM], XS + 8 * K1, f32r)
    MEM = at("mem", [P, MT, D], XS + 16 * K1)
    VR = [at(f"vector_rows{i}", [64, P], XS + 24 * K1 + 512 * i) for i in range(2)]
    MASKF = at("level_masks_loaded", [P, LEVELS + 1, P], XS + 26 * K1)
    GROW = at("g_rows", [H, S], XS + 16 * K1)
    MROW = at("m_rows", [H, S], XS + 18 * K1)
    MB = at("minus_m_all", [P, H, S], XS)
    PP = [at(f"mlstm_p{i}", [P, 1280], XS + 8 * K1 + 5 * K1 * i) for i in range(2)]
    HM = [at(f"mlstm_h{i}", [P, TT, P], XS + 18 * K1 + 2 * K1 * i) for i in range(2)]
    SQ = at("mlstm_sq", [P, TT, P], XS + 22 * K1)
    QC = at("q_c", [P, H, S], XS + 24 * K1)
    PT = [at(f"probs_t{i}", [P, 2 * H, P], XS + 8 * K1 + 4 * K1 * i) for i in range(2)]
    LF2 = at("log_f2", [P, TT, S], XS)
    EE = at("decay", [P, H * S], XS)
    KDT = at("k_dec_t", [P, H, TT, P], XS)
    QE = at("q_decayed", [P, H * S], XS + 8 * K1)
    KE = at("k_decayed", [P, H * S], XS + 16 * K1)
    SC = at("gla_scores", [P, H * TT, P], XS + 24 * K1)

    RES = at("residual", [P, TT, D], A)
    XN = at("x_normed", [P, TT, D], A + 16 * K1)
    Y = at("y", [P, 12, S], A + 16 * K1)
    QK = at("qk", [P, 8, S], A + 40 * K1)
    V = at("v", [P, TT, GW], A + 56 * K1)
    O = at("o_gate", [P, TT, GW], A + 64 * K1)
    KM = at("k_mem", [P, H, NMEM], A + 72 * K1)
    VM = at("v_mem", [P, MT, GW], A + 76 * K1)
    FG = at("final_g_all", [P, D], A + 80 * K1)
    WG2 = at("w_gate2_and_bias", [17, S], A + 84 * K1)
    NSEL = at("minus_head_rows", [H, H, P], A + 86 * K1)
    PROB = [at(f"probs{i}", [P, H, NMEM], A + 56 * K1 + 4 * K1 * i) for i in range(2)]
    UP = at("u_padded", [P, 4, PAD + S], A + 40 * K1)
    PW = [at(f"pool_sum{i}", [P, PAD + S], A + 49 * K1 + 2560 * i) for i in range(2)]
    POOLW = at("pool_w_sb", [P, 4, P], A + 64 * K1)
    SINK = at("squares_sink", [P, D], A + 68 * K1)
    U = at("u_gelu", [P, KC, S], A)
    WSR = at("w_s_rows", [P, 8, P], A)
    Q2 = at("q2", [P, H * S], A + 16 * K1)
    K2 = at("k2", [P, H * S], A + 24 * K1)
    CUM = at("cum", [P, H * S], A + 32 * K1)
    V2 = at("v2", [P, TT, D], A + 40 * K1)
    VH = at("v_hat", [P, TT, D], A + 56 * K1)
    R = at("r_silu", [P, KC, S], A + 56 * K1)
    BV = at("b_v_all", [P, D], A + 72 * K1)
    WST = at("w_s_t", [P, 8, P], A + 72 * K1)
    BAV = at("b_av_all", [P, D], A + 76 * K1)
    BS = at("b_s_all", [P, 8, P], A + 76 * K1)
    ALT = at("a_low_t", [32, S], A + 86 * K1)
    SGG = at("sg_g_all", [P, D], A + 80 * K1)
    SGB = at("sg_b_all", [P, D], A + 84 * K1)
    STATE = at("gla_state", [P, H, 256], A + 80 * K1)
    OJ = at("gla_o", [P, D], A + 84 * K1)
    L1G = at("ln1_g_all", [P, D], A + 72 * K1)
    L1B = at("ln1_b_all", [P, D], A + 76 * K1)
    L2G = at("ln2_g_all", [P, D], A + 80 * K1)
    L2B = at("ln2_b_all", [P, D], A + 84 * K1)
    F1 = at("ff_hidden", [P, 8, 2048], A + 16 * K1)

    C_NORM, C_MEMN, C_CW, C_CB, C_MN, C_PS = 0, 8, 16, 48, 56, 60
    C_B2, C_B2G, C_GN = 64, 64 + 40, 64 + 56

    def col(c):
        return VC[:, c:c + 1]

    ctx = ExitStack()
    with ctx:
        bank = [ctx.enter_context(nc.psum_tensor(f"bank{b}", [P, 512], f32)) for b in range(8)]

        def sem(name):
            return ctx.enter_context(nc.semaphore(name))

        w_loaded = [sem(f"w_loaded{i}") for i in range(2)]
        w_hi, w_lo, w_used = sem("w_hi_done"), sem("w_lo_done"), sem("w_block_used")
        x_hi, x_lo = sem("x_hi_done"), sem("x_lo_done")
        bank_full = [sem(f"bank_full{b}") for b in range(8)]
        bank_free = [sem(f"bank_free{b}") for b in range(8)]
        consts_in, rows_in, mem_in, wg_in, fg_in, wg2_in = (sem(s + "_in") for s in
                                                            ("consts", "rows", "mem", "wg", "fg", "wg2"))
        x_in = [sem(f"x_in{j}") for j in range(TT)]
        poolw_in, bv_in, ws_in, sg_in, bs_in, ln1_in, ln2_in = (sem(s + "_in") for s in
                                                                ("poolw", "bv", "ws", "sg", "bs", "ln1", "ln2"))
        x1_spilled, x1_back, stored = sem("x1_spilled"), sem("x1_back"), sem("stored")
        ones_set, alt_set, zeros_set, masks_set = (sem(s) for s in ("ones_set", "alt_set", "zeros_set", "masks_set"))
        squared, rstd_done = sem("squares_summed"), sem("rstd_done")
        mem_normed, x_normed, t_hi, wg_hi, wg_lo = (sem(s) for s in ("mem_normed", "x_normed", "turned_hi", "wg_hi", "wg_lo"))
        softplus_done, logf_done, g_done, m_done, floor_done = (sem(s) for s in
                                                                ("softplus_done", "logf_done", "g_done", "m_done", "floor_done"))
        conv_first, qk_done = sem("conv_first_tap"), sem("qk_done")
        ml_arg, ml_exp, ml_ss, ml_h = sem("mlstm_arg"), sem("mlstm_exp"), sem("mlstm_ss"), sem("mlstm_h_done")
        max_done, probs_done = sem("softmax_max"), sem("probs_normed")
        pooled, yb_done, x1_done = sem("pooled"), sem("yb_done"), sem("x1_done")
        lg_min, lg_softplus = sem("logit_min"), sem("logit_softplus")
        lv_arg, lv_exp, lv_qk = sem("level_arg"), sem("level_exp"), sem("level_operands")
        av_gelu, vhat_done, vh_ready, ga_sig, gb_sig = (sem(s) for s in
                                                        ("av_gelu", "vhat_done", "vh_ready", "ga_sigmoid", "gb_sigmoid"))
        qc_exp, qcum_done, kd_arg, kd_exp, kd_done, etot_done = (sem("gla_" + s) for s in
                                                                ("qcum_exp", "qcum", "kdec_arg", "kdec_exp", "kdec", "exp_total"))
        m_ready = sem("m_ready")
        ln_var, h1_done, h2_done, f1_done = sem("ln_var"), sem("h1_done"), sem("h2_done"), sem("f1_done")
        pool_chain, dve_chain, act_chain = sem("pool_chain"), sem("dve_chain"), sem("act_chain")

        block = ctx.enter_context(nc.Block())

        turn, uses, block_done = {}, [0] * 8, {}

        def full(eng, key):
            b, u = turn[key]
            eng.wait_ge(bank_full[b], u + 1)
            return bank[b]

        def free(ins, key):
            ins.then_inc(bank_free[turn[key][0]], 1)

        def drained(eng, key):
            b, u = turn[key]
            eng.wait_ge(bank_free[b], u + 1)

        def quarters(t):
            return t.rearrange("p (a b) -> p a b", a=4)

        def weights(n, pair):
            k, c = blocks[n][2].shape[1:]
            return tuple(t[n % 2][:, 0:k * c].rearrange("p (k c) -> p k c", c=c) for t in pair)

        def tile_of(j):
            return slice(j * P, j * P + P)

        ff1_0, ff2_0 = first["ff1"], first["ff2"]
        WO, WO2 = first["w_out"], first["w_out2"]
        WO_GROUPS = (0, 2, 1)
        ML = first["qc"]
        AT = ML + 4
        LG = first["low"] + 1
        LV = first["v2"]
        GO = LV + 2 * LEVELS + 4
        SG = first["a_u"] + 3
        E_WO2 = 6
        E_FF2 = E_WO2 + 4

        def fm_key(name, c):
            return ("fm", first[name] + c // 2, c % 2)

        @block.tensor
        def _(pe):
            n_used = [0]

            def take(b, key):
                turn[key] = (b, uses[b])
                if uses[b]:
                    pe.wait_ge(bank_free[b], uses[b])
                uses[b] += 1
                return bank[b]

            def give(ins, key):
                ins.then_inc(bank_full[turn[key][0]], 1)

            def three(dst, lh, ll, rh, rl, start, stop):
                pe.matmul(dst, lh, rh, start=start, stop=False)
                pe.matmul(dst, lh, rl, start=False, stop=False)
                return pe.matmul(dst, ll, rh, start=False, stop=stop)

            def fm_block(n, xh, xl, tokens=S):
                wh, wlo = weights(n, (WH, WL))
                pe.wait_ge(w_lo, n + 1)
                for t in range(wh.shape[2] // P):
                    key = ("fm", n, t)
                    dst = take(t, key)[:, 0:tokens]
                    for k in range(KC):
                        last = three(dst, wh[:, k, tile_of(t)], wlo[:, k, tile_of(t)], xh[:, k, :], xl[:, k, :],
                                     k == 0, k == KC - 1)
                    give(last, key)
                b, u = turn[key]
                block_done[n] = (bank_full[b], u + 1)

            def tm_block(n, g, groups, lhs, tiles=TT):
                wh, wlo = weights(n, (WH, WL))
                pe.wait_ge(w_lo, n + 1)
                for j in range(tiles):
                    key = ("tm", n - g, j)
                    if g == 0:
                        take(2 + j, key)
                    for kk in range(4):
                        xh, xl = lhs(kk)
                        last = three(bank[2 + j][:, :], xh[:, tile_of(j)], xl[:, tile_of(j)], wh[:, kk, :], wlo[:, kk, :],
                                     g == 0 and kk == 0, g == groups - 1 and kk == 3)
                    if g == groups - 1:
                        give(last, key)
                if g == groups - 1:
                    b, u = turn[key]
                    block_done[n] = (bank_full[b], u + 1)
                else:
                    n_used[0] += 1
                    last.then_inc(w_used, 1)
                    block_done[n] = (w_used, n_used[0])

            def staged(slot):
                h, l = quarters(XH[slot][:, :]), quarters(XL[slot][:, :])
                return lambda kk: (h[:, kk, :], l[:, kk, :])

            def resident(h, l, g):
                return lambda kk: (h[:, 4 * g + kk, :], l[:, 4 * g + kk, :])

            def turn_four(src, b, key):
                dst = take(b, key)
                for i in range(4):
                    last = pe.transpose(dst[:, tile_of(i)], src(i), IDENT[:, :])
                give(last, key)

            def turn_vectors():
                pe.wait_ge(consts_in, 16 * 6)
                pe.wait_ge(rows_in, 16 * 10)
                dst = take(0, "vectors")
                pe.transpose(dst[:, 0:64], VR[0][:, :], IDENT[0:64, 0:64])
                give(pe.transpose(dst[:, 64:128], VR[1][:, :], IDENT[0:64, 0:64]), "vectors")

            def turn_mem():
                pe.wait_ge(mem_normed, MT)
                for c in range(KC):
                    b, key = 4 + c // 2, ("memT", c // 2)
                    if c % 2 == 0:
                        take(b, key)
                    for j in range(MT):
                        q = (c % 2) * NMEM + j * P
                        last = pe.transpose(bank[b][:, q:q + P], MEM[:, j, tile_of(c)], IDENT[:, :])
                    if c % 2:
                        give(last, key)

            def turn_x():
                pe.wait_ge(x_normed, TT)
                for c in range(KC):
                    turn_four(lambda j: XN[:, j, tile_of(c)], 4 + c % 4, ("xT", c))

            def gates():
                for c in range(4, KC):
                    drained(pe, ("xT", c))
                pe.wait_ge(wg_lo, 1)
                dst = take(6, "gates")
                for j in range(TT):
                    for k in range(KC):
                        last = three(dst[:, 2 * H * j:2 * H * (j + 1)], TH[:, k, tile_of(j)], TL[:, k, tile_of(j)],
                                     WGH[:, k, :], WGL[:, k, :], k == 0, k == KC - 1)
                give(last, "gates")

            def sum_f():
                pe.wait_ge(logf_done, 1)
                pe.wait_ge(ones_set, 1)
                dst = take(6, "F")
                for j in range(TT):
                    for i in range(j + 1):
                        last = pe.matmul(dst[:, H * j:H * j + H], (TRIU if i == j else ONES)[:, :], LF[:, i, :],
                                         start=i == 0, stop=i == j)
                give(last, "F")

            def g_rows():
                pe.wait_ge(g_done, 1)
                dst = take(7, "g_rows")
                for j in range(TT):
                    last = pe.transpose(dst[0:H, tile_of(j)], GG[:, j, :], IDENT[:, :])
                give(last, "g_rows")

            def m_all(h, b):
                pe.wait_ge(m_done, 1)
                dst = take(b, ("m_all", h))
                give(pe.matmul(dst[:, :], NSEL[:, h, :], MROW[:, :], start=True, stop=True), ("m_all", h))

            def m_columns():
                dst = take(7, "m_columns")
                for j in range(TT):
                    last = pe.transpose(dst[:, H * j:H * j + H], MROW[:, tile_of(j)], IDENT[0:H, 0:H])
                give(last, "m_columns")

            def mlstm_scores(h):
                pe.wait_ge(qk_done, 8)
                for i, b, c0 in ((0, 2, 0), (1, 3, 0), (3, 3, 384), (2, 4, 0)):
                    key = ("ms", h, b)
                    if i != 3:
                        take(b, key)
                    last = pe.matmul(bank[b][:, c0:c0 + S - i * P], QK[:, 4 + h, tile_of(i)], QK[:, h, i * P:S],
                                     start=True, stop=True)
                    if i != 1:
                        give(last, key)

            def mlstm_sums(h):
                for b in (2, 3, 4):
                    drained(pe, ("ms", h, b))
                if h == 0:
                    for j in range(TT):
                        drained(pe, ("tm", first["v"], j))
                num, den = take(5, ("num", h)), take(6, ("den", h))
                for dst, key in ((num, ("num", h)), (den, ("den", h))):
                    for j in range(TT):
                        for i in range(j + 1):
                            c = ML_OFF[i] + (j - i) * P
                            w = PP[h % 2][:, c:c + P]
                            if key[0] == "num":
                                last = pe.matmul(dst[:, tile_of(j)], w, V[:, i, tile_of(h)], start=i == 0, stop=i == j)
                            else:
                                last = pe.matmul(dst[:, j:j + 1], w, ONES[:, 0:1], start=i == 0, stop=i == j)
                    give(last, key)

            def mlstm_turn(h):
                pe.wait_ge(ml_h, h + 1)
                turn_four(lambda j: HM[h % 2][:, j, :], 7, ("hT", h))

            def mem_scores(j):
                if j == 0:
                    for c in range(H):
                        drained(pe, fm_key("qc", c))
                        drained(pe, fm_key("km", c))
                for i in range(2):
                    dst = take(2 + i, ("cs", j, i))
                    for h in (2 * i, 2 * i + 1):
                        q = (h % 2) * NMEM
                        last = pe.matmul(dst[:, q:q + NMEM], QC[:, h, tile_of(j)], KM[:, h, :], start=True, stop=True)
                    give(last, ("cs", j, i))

            def probs_turn(j):
                pe.wait_ge(probs_done, j + 1)
                for i in range(2):
                    turn_four(lambda q: PROB[j % 2][:, 2 * i + q // 2, tile_of(q % 2)], 4 + i, ("pT", j, i))

            def mem_values(j):
                for i in range(2):
                    drained(pe, ("pT", j, i))
                    drained(pe, ("tm", first["vm"], i))
                dst = take(6, ("yc", j))
                for h in range(H):
                    for m in range(MT):
                        last = pe.matmul(dst[:, tile_of(h)], VM[:, m, tile_of(h)], PT[j % 2][:, 2 * h + m, :],
                                         start=m == 0, stop=m == MT - 1)
                give(last, ("yc", j))

            def pool_mix():
                pe.wait_ge(poolw_in, 16)
                for g in range(4):
                    pe.wait_ge(pooled, g + 1)
                    dst = take(2 + g, ("pool", g))
                    give(pe.matmul(dst[:, :], POOLW[:, g, :], UP[:, g, PAD:PAD + S], start=True, stop=True), ("pool", g))

            def gate_logits():
                drained(pe, ("fm", first["low"], 0))
                pe.wait_ge(wg2_in, 32)
                for j in range(TT):
                    dst = take(2 + j, ("lg", j))
                    give(pe.matmul(dst[:, :], ALT[0:17, tile_of(j)], WG2[:, :], start=True, stop=True), ("lg", j))

            def cum_sums():
                for j in range(TT):
                    drained(pe, ("lg", j))
                for h in range(H):
                    dst = take(2 + h, ("cum", h))
                    for j in range(TT):
                        last = pe.matmul(dst[:, tile_of(j)], LF2[:, j, tile_of(h)], TRI16[:, :], start=True, stop=True)
                    give(last, ("cum", h))

            def gla_pairs(level, half):
                if level >= 0:
                    pe.wait_ge(lv_qk, 2 * (level + 1))
                elif half == 0:
                    for c in range(H):
                        drained(pe, fm_key("q2", c))
                        drained(pe, fm_key("k2", c))
                kk, qq = (K2, Q2) if level < 0 else (KE, QE)
                for h in (2 * half, 2 * half + 1):
                    dst = take(6 + h % 2, ("lv", level, h))
                    for j in range(TT):
                        c = slice(h * S + j * P, h * S + j * P + P)
                        last = pe.matmul(dst[:, tile_of(j)], kk[:, c], qq[:, c], start=True, stop=True)
                    give(last, ("lv", level, h))

            def kdec_turn():
                pe.wait_ge(kd_done, 1)
                for h in range(H):
                    turn_four(lambda j: KE[:, h * S + j * P:h * S + j * P + P], 2 + h, ("kdT", h))

            def gla_out(j):
                if j == 0:
                    for h in range(H):
                        drained(pe, ("lv", LEVELS - 1, h))
                        drained(pe, ("kdT", h))
                        for half in range(2):
                            drained(pe, ("tm", first["v2"] + 2 * half, h))
                    pe.wait_ge(qcum_done, 1)
                else:
                    drained(pe, ("kv", j - 1, 0))
                    drained(pe, ("kv", j - 1, 1))
                for i in range(2):
                    dst = take(2 + i, ("o2", j, i))
                    for h in (2 * i, 2 * i + 1):
                        c, v = slice((h % 2) * DV, (h % 2 + 1) * DV), slice(h * DV, h * DV + DV)
                        last = pe.matmul(dst[:, c], SC[:, h * TT + j, :], V2[:, j, v], start=True, stop=j == 0)
                        if j:
                            last = pe.matmul(dst[:, c], QE[:, h * S + j * P:h * S + j * P + P], STATE[:, h, :],
                                             start=False, stop=True)
                    give(last, ("o2", j, i))
                if j < TT - 1:
                    for i in range(2):
                        dst = take(4 + i, ("kv", j, i))
                        for h in (2 * i, 2 * i + 1):
                            c, v = slice((h % 2) * DV, (h % 2 + 1) * DV), slice(h * DV, h * DV + DV)
                            last = pe.matmul(dst[:, c], KDT[:, h, j, :], V2[:, j, v], start=True, stop=True)
                        give(last, ("kv", j, i))

            def gla_turn(j):
                for i in range(2):
                    drained(pe, ("o2", j, i))
                for i in range(2):
                    turn_four(lambda c: OJ[:, tile_of(4 * i + c)], 6 + i, ("oT", j, i))

            def ws_turn():
                pe.wait_ge(ws_in, 16)
                for i in range(2):
                    turn_four(lambda g: WSR[:, 4 * i + g, :], 6 + i, ("wsT", i))

            def sg_mix(i):
                if i == 0:
                    pe.wait_ge(vh_ready, TT)
                    drained(pe, ("wsT", 0))
                    drained(pe, ("wsT", 1))
                for g in (2 * i, 2 * i + 1):
                    dst = take(2 + g % 2, ("sg", g))
                    for j in range(TT):
                        last = pe.matmul(dst[:, tile_of(j)], VH[:, j, tile_of(g)], WST[:, g, :], start=True, stop=True)
                    give(last, ("sg", g))

            def turn_rows(name, done):
                for j in range(TT):
                    pe.wait_ge(done, j + 1)
                    for i in range(2):
                        turn_four(lambda c: RES[:, j, tile_of(4 * i + c)], 6 + i, (name, j, i))
                drained(pe, (name, TT - 1, 0))
                drained(pe, (name, TT - 1, 1))

            def side(n):
                if n == 4: turn_x(); gates()
                if n == 5: sum_f()
                if n == 6: g_rows()
                if n == 7: m_all(0, 6); m_columns()
                if n == 8: m_all(1, 6); m_all(2, 7)
                if n == 9: m_all(3, 6)
                if 0 <= n - ML - 3 < H: mlstm_turn(n - ML - 3)
                if 0 <= n - ML - 1 < H: mlstm_sums(n - ML - 1)
                if 0 <= n - ML < H: mlstm_scores(n - ML)
                if 0 <= n - AT - 2 < TT: mem_values(n - AT - 2)
                if 0 <= n - AT - 1 < TT: probs_turn(n - AT - 1)
                if 0 <= n - AT < TT: mem_scores(n - AT)
                if n == WO - 1: pool_mix()
                if n == first["low"]: turn_rows("x1T", x1_done)
                if n == LG: gate_logits()
                if n == LG + 2: cum_sums()
                if n == LV + 4: ws_turn()
                if 0 <= n - LV < 2 * (LEVELS + 1): gla_pairs((n - LV) // 2 - 1, (n - LV) % 2)
                if 0 <= n - SG < 4: sg_mix(n - SG)
                if n == GO - 1: kdec_turn()
                if 0 <= n - GO - 1 < TT: gla_turn(n - GO - 1)
                if 0 <= n - GO < TT: gla_out(n - GO)

            turn_vectors()
            turn_mem()
            for i in range(4):
                drained(pe, ("memT", i))
            for n in range(ff1_0):
                name, i = name_of(n)
                side(n)
                if name == "km":
                    fm_block(n, MEMH, MEML, NMEM)
                elif name == "vm":
                    tm_block(n, i, 2, resident(MEMH, MEML, i), MT)
                elif name in ("w_out", "w_out2"):
                    g = len(WO_GROUPS) if name == "w_out" else 2
                    pe.wait_ge(x_lo, i + 1 + (0 if name == "w_out" else E_WO2))
                    tm_block(n, i % g, g, staged(i % 2))
                elif blocks[n][0] == "tm":
                    tm_block(n, i % 2, 2, resident(TH, TL, i % 2))
                else:
                    fm_block(n, TH, TL)

            turn_rows("h1T", h1_done)
            u0 = list(uses)
            with pe.Fori(0, 8) as i:
                for b in range(2):
                    n = ff1_0 + b
                    wh, wlo = weights(n, (WH, WL))
                    pe.wait_ge(w_lo, i * 2 + (n + 1))
                    for t in range(2):
                        pe.wait_ge(bank_free[t], i * 2 + (u0[t] + b))
                        for k in range(KC):
                            last = three(bank[t][:, :], wh[:, k, tile_of(t)], wlo[:, k, tile_of(t)], TH[:, k, :], TL[:, k, :],
                                         k == 0, k == KC - 1)
                        last.then_inc(bank_full[t], 1)
            for n in range(16):
                for t in range(2):
                    turn["fm", ff1_0 + n, t] = (t, u0[t] + n)
                block_done[ff1_0 + n] = (bank_full[1], u0[1] + n + 1)
            uses[0] += 16
            uses[1] += 16

            for half in range(2):
                n0, e0, used0 = ff2_0 + 8 * half, E_FF2 + 8 * half, n_used[0]

                def group(g, more=0):
                    wh, wlo = weights(n0 + g, (WH, WL))
                    lhs = staged(g % 2)
                    pe.wait_ge(w_lo, more + (n0 + g + 1))
                    pe.wait_ge(x_lo, more + (e0 + g + 1))
                    for j in range(TT):
                        key = ("tm", n0, j)
                        if g == 0:
                            take(2 + j, key)
                        for kk in range(4):
                            h, l = lhs(kk)
                            last = three(bank[2 + j][:, :], h[:, tile_of(j)], l[:, tile_of(j)], wh[:, kk, :], wlo[:, kk, :],
                                         g == 0 and kk == 0, g == 7 and kk == 3)
                        if g == 7:
                            give(last, key)
                    if g < 7:
                        last.then_inc(w_used, 1)

                group(0)
                group(1)
                with pe.Fori(0, 2) as i:
                    group(2, i * 2)
                    group(3, i * 2)
                group(6)
                group(7)
                for g in range(7):
                    block_done[n0 + g] = (w_used, used0 + g + 1)
                n_used[0] += 7
                block_done[n0 + 7] = (bank_full[5], turn["tm", n0, 3][1] + 1)

        f0 = [turn["fm", ff1_0, t][1] for t in range(2)]

        @block.scalar
        def _(act):
            links = [0]

            def link(ins):
                links[0] += 1
                ins.then_inc(act_chain, 1)
                act.wait_ge(act_chain, links[0])

            def split(n, loads=0, more=0):
                w = blocks[n][2].shape[1] * blocks[n][2].shape[2]
                act.wait_ge(w_loaded[n % 2], loads + 16 * (n // 2 + 1))
                if n >= 2:
                    s, v = block_done[n - 2]
                    act.wait_ge(s, more + v)
                act.activation(WH[n % 2][:, 0:w], RAW[n % 2][:, 0:w], ACT.Copy).then_inc(w_hi, 1)

            def split_x(slot, src):
                act.activation(XH[slot][:, :], src, ACT.Copy).then_inc(x_hi, 1)

            def load_constants():
                def rows(slot, r0, v):
                    v = v.rearrange("(c p) -> c p", p=P)
                    act.dma_start(VR[slot][r0:r0 + v.shape[0], :], v).then_inc(rows_in, 16)

                act.dma_start(IDENT[:, :], a["c_ident"]).then_inc(consts_in, 16)
                rows(0, C_NORM, a["norm_g"][0])
                rows(0, C_MEMN, a["mem_norm_g"][0])
                rows(0, C_CW, a["conv_w"][0].rearrange("j c -> (j c)"))
                rows(0, C_CB, a["conv_b"][0])
                rows(0, C_MN, a["mlstm_norm_g"][0])
                rows(0, C_PS, a["pool_scale"][0])
                rows(1, C_B2 - 64, a["b_in_2"][0, 0:5 * D])
                rows(1, C_B2G - 64, a["b_in_2"][0, 5 * D + 16:7 * D + 16])
                rows(1, C_GN - 64, a["gla_norm_g_2"][0])
                act.dma_start(LOWB[:, :], a["b_in_2"][0, 5 * D:5 * D + 16].rearrange("(p o) -> p o", o=1)).then_inc(rows_in, 16)
                act.dma_start(TRIU[:, :], a["c_triu"]).then_inc(consts_in, 16)
                act.dma_start(TRI16[:, :], a["c_triu16"]).then_inc(consts_in, 16)
                act.dma_start(MASKF[:, :, :], a["c_masks"]).then_inc(consts_in, 16)
                act.dma_start(NSEL[:, :, :], a["c_nsel"]).then_inc(consts_in, 16)
                act.dma_start(PINV[:, :, :], a["c_pool_edge"].partition_broadcast(P)).then_inc(consts_in, 16)
                act.dma_start(WG[:, :, :], a["w_in"][0].rearrange("(k p) n -> p k n", p=P)[:, :, 5 * GW:5 * GW + 2 * H]).then_inc(wg_in, 16)
                act.dma_start(BG[:, :], a["b_gates"][0].partition_broadcast(P)).then_inc(wg_in, 16)
                act.dma_start(FG[:, :], a["final_norm_g"].partition_broadcast(P)).then_inc(fg_in, 16)
                act.dma_start(WG2[0:16, :], a["gla_w_gate2_2"][0]).then_inc(wg2_in, 16)
                act.dma_start(WG2[16:17, :], a["gla_b_gate_2"]).then_inc(wg2_in, 16)

            def mean_squares(dst, src, c, before=0):
                if before:
                    act.wait_ge(squared, before)
                act.activation(dst, src, ACT.Square, scale=1 / 32, accum_out=SSQ[:, c:c + 1]).then_inc(squared, 1)

            def gates_softplus():
                drained(act, "gates")
                link(act.activation(GT1[:, :, :], G8[:, :, H:2 * H], ACT.Abs))
                link(act.activation(GT1[:, :, :], GT1[:, :, :], ACT.Exp, scale=-1.0))
                act.activation(GT1[:, :, :], GT1[:, :, :], ACT.Ln, bias=1.0).then_inc(softplus_done, 1)

            def copy_m(h):
                b = full(act, ("m_all", h))
                free(act.activation(MB[:, h, :], b[:, :], ACT.Copy), ("m_all", h))

            def den_floor():
                drained(act, "m_columns")
                act.activation(FLOOR[:, :, :], FLOOR[:, :, :], ACT.Exp, scale=-1.0).then_inc(floor_done, 1)

            def mlstm_exp(h):
                act.wait_ge(ml_arg, h + 1)
                act.activation(PP[h % 2][:, :], PP[h % 2][:, :], ACT.Exp).then_inc(ml_exp, 1)

            def softmax_exp(j):
                act.wait_ge(max_done, j + 1)
                for h in range(H):
                    b = full(act, ("cs", j, h // 2))
                    ins = act.activation(PROB[j % 2][:, h, :], b[:, (h % 2) * NMEM:(h % 2 + 1) * NMEM], ACT.Exp,
                                         bias=SMX[:, h:h + 1], scale=SCALE, accum_out=SSUM[:, h:h + 1])
                    if h % 2:
                        free(ins, ("cs", j, h // 2))

            def probs_copy(j):
                for i in range(2):
                    b = full(act, ("pT", j, i))
                    free(act.activation(PT[j % 2][:, 4 * i:4 * i + 4, :], quarters(b[:, :]), ACT.Copy), ("pT", j, i))

            def logits_softplus():
                for f, kw in ((ACT.Abs, {}), (ACT.Exp, {"scale": -1.0}), (ACT.Ln, {"bias": 1.0})):
                    for j in range(TT):
                        b = full(act, ("lg", j))
                        if f == ACT.Abs:
                            act.wait_ge(lg_min, j + 1)
                        ins = act.activation(b[:, :], b[:, :], f, **kw)
                        if f == ACT.Ln:
                            ins.then_inc(lg_softplus, 1)
                    if f != ACT.Ln:
                        link(ins)

            def copy_cum():
                for h in range(H):
                    b = full(act, ("cum", h))
                    free(act.activation(CUM[:, h * S:h * S + S], b[:, :], ACT.Copy), ("cum", h))

            def level_exp(l):
                act.wait_ge(lv_arg, 2 * (l + 1))
                act.activation(EE[:, :], EE[:, :], ACT.Exp).then_inc(lv_exp, 1)

            def squares_o(j):
                if j:
                    full(act, ("oT", j - 1, 1))
                for h in range(H):
                    b = full(act, ("o2", j, h // 2))
                    act.activation(OJ[:, h * DV:h * DV + DV], b[:, (h % 2) * DV:(h % 2 + 1) * DV], ACT.Square,
                                   scale=1 / 16, accum_out=SSQ[:, 10 + h:11 + h]).then_inc(squared, 1)

            def rows_hi(name, j):
                for i in range(2):
                    b = full(act, (name, j, i))
                    act.activation(TH[:, 4 * i:4 * i + 4, tile_of(j)], quarters(b[:, :]), ACT.Copy).then_inc(t_hi, 1)

            def side(n):
                if n == 0:
                    for j in range(TT):
                        act.wait_ge(x_in[j], 16)
                        mean_squares(XN[:, j, :], RES[:, j, :], MT + j)
                    act.wait_ge(wg_in, 32)
                    act.activation(WGH[:, :, :], WG[:, :, :], ACT.Copy).then_inc(wg_hi, 1)
                if n == 4:
                    for c in range(KC):
                        b = full(act, ("xT", c))
                        act.activation(TH[:, c, :], b[:, :], ACT.Copy, scale=col(C_NORM + c)).then_inc(t_hi, 1)
                    gates_softplus()
                if n == 7: copy_m(0)
                if n == 8: copy_m(1); copy_m(2); den_floor()
                if n == 9: copy_m(3)
                if 0 <= n - ML < H: mlstm_exp(n - ML)
                if 0 <= n - AT - 1 < TT: probs_copy(n - AT - 1)
                if 0 <= n - AT < TT: softmax_exp(n - AT)
                if n == LG: logits_softplus()
                if n == LG + 2: copy_cum()
                if 0 < n - LV <= 2 * LEVELS and (n - LV) % 2: level_exp((n - LV) // 2)
                if n == GO - 3:
                    act.wait_ge(lv_qk, 2 * LEVELS)
                    act.activation(ETOT[:, :], CUM[:, :].rearrange("p (c t) -> p c t", t=P)[:, :, P - 1], ACT.Exp).then_inc(etot_done, 1)
                    act.activation(EE[:, :], CUM[:, :], ACT.Exp).then_inc(qc_exp, 1)
                if n == GO - 2:
                    act.wait_ge(kd_arg, 1)
                    act.activation(EE[:, :], EE[:, :], ACT.Exp).then_inc(kd_exp, 1)
                if n == GO - 1:
                    act.wait_ge(kd_done, 1)
                    for h in range(H):
                        b = full(act, ("kdT", h))
                        free(act.activation(KDT[:, h, :, :], quarters(b[:, :]), ACT.Copy), ("kdT", h))
                if 0 <= n - GO < TT: squares_o(n - GO)

            def drain(n):
                name, i = name_of(n)
                fm = [(("fm", n, t), 2 * i + t) for t in range(2)]
                if name == "km":
                    for key, c in fm:
                        b = full(act, key)
                        free(act.activation(KM[:, c, :], b[:, 0:NMEM], ACT.Copy), key)
                if name in ("vm", "v", "o") and i == 1:
                    dst, f = {"vm": (VM, ACT.Copy), "v": (V, ACT.Copy), "o": (O, ACT.Sigmoid)}[name]
                    for j in range(MT if name == "vm" else TT):
                        b = full(act, ("tm", n - 1, j))
                        free(act.activation(dst[:, j, :], b[:, :], f), ("tm", n - 1, j))
                if name in ("q", "k"):
                    c0 = 4 if name == "k" else 0
                    for key, c in fm:
                        b = full(act, key)
                        act.activation(QK[:, c0 + c, :], b[:, :], ACT.Identity, bias=col(C_CB + c0 + c),
                                       scale=col(C_CW + 24 + c0 + c)).then_inc(conv_first, 1)
                    for key, c in fm:
                        drained(act, key)
                        act.activation(QK[:, c0 + c, :], QK[:, c0 + c, :], ACT.Silu).then_inc(qk_done, 1)
                to = {"qc": lambda c: QC[:, c, :], "u": lambda c: UP[:, c, PAD:PAD + S], "z_a": lambda c: Y[:, c, :],
                      "z_b": lambda c: Y[:, 4 + c, :], "z_c": lambda c: Y[:, 8 + c, :]}.get(name)
                if to:
                    for key, c in fm:
                        b = full(act, key)
                        free(act.activation(to(c), b[:, :], ACT.Silu if name[0] == "z" else ACT.Copy), key)
                if name == "w_out" and i == 5:
                    for j in range(TT + 1):
                        if j < TT:
                            drained(act, ("tm", n - 2, j))
                            mean_squares(SINK[:, :], RES[:, j, :], 6 + j, MT + TT + j)
                        if j:
                            rows_hi("x1T", j - 1)
                if name == "a_v" and i % 2:
                    h = slice(i // 2 * 512, i // 2 * 512 + 512)
                    for j in range(TT):
                        drained(act, ("tm", n - 1, j))
                        act.activation(VH[:, j, h], VH[:, j, h], ACT.Gelu_apprx_tanh).then_inc(av_gelu, 1)
                if name in ("a_u", "g_a", "r", "g_b"):
                    for key, c in fm:
                        b = full(act, key)
                        if name == "a_u":
                            free(act.activation(U[:, c, :], b[:, :], ACT.Gelu_apprx_tanh, bias=col(C_B2 + c)), key)
                        if name == "g_a":
                            act.activation(b[:, :], b[:, :], ACT.Sigmoid, bias=col(C_B2G + c)).then_inc(ga_sig, 1)
                        if name == "r":
                            if c == 0:
                                full(act, ("sg", 7))
                            free(act.activation(R[:, c, :], b[:, :], ACT.Silu, bias=col(C_B2 + 32 + c)), key)
                        if name == "g_b":
                            act.activation(b[:, :], b[:, :], ACT.Sigmoid, bias=col(C_B2G + 8 + c)).then_inc(gb_sig, 1)
                if name == "w_out2" and i == 3:
                    for j in range(TT):
                        rows_hi("h1T", j)

            def stage(n):
                if n + 1 >= ff1_0:
                    return
                name, i = name_of(n + 1)
                if name == "w_out":
                    if i == 0: drained(act, ("hT", H - 1))
                    if i == 1: drained(act, ("yc", TT - 1))
                    if i == 2: act.wait_ge(yb_done, 4)
                    g, src = WO_GROUPS[i % 3], Y
                elif name == "w_out2":
                    act.wait_ge(m_ready, 4 if i == 0 else 8)
                    g, src = i % 2, R
                else:
                    return
                if i >= 2:
                    act.wait_ge(*block_done[n - 1])
                split_x(i % 2, src[:, 4 * g:4 * g + 4, :].rearrange("p a b -> p (a b)"))

            load_constants()
            act.wait_ge(mem_in, 16)
            for j in range(MT):
                mean_squares(SINK[:, :], MEM[:, j, :], j, j)
            full(act, "vectors")
            free(act.activation(VC[:, :], bank[0][:, 0:P], ACT.Copy), "vectors")
            drained(act, "vectors")
            split(0)
            for c in range(KC):
                full(act, ("memT", c // 2))
                q = (c % 2) * NMEM
                act.activation(MEMH[:, c, :], bank[4 + c // 2][:, q:q + NMEM], ACT.Copy, scale=col(C_MEMN + c)).then_inc(t_hi, 1)
            for n in range(ff1_0):
                split(n + 1)
                side(n)
                stage(n)
                drain(n)

            def relus(m, group, more=0):
                for t in range(2):
                    act.wait_ge(bank_full[t], more + (f0[t] + m + 1))
                    q = (2 * m + t) % 4 * S
                    act.activation(F1[:, group, q:q + S], bank[t][:, :], ACT.Relu).then_inc(bank_free[t], 1)

            split(ff1_0 + 1)
            relus(0, 0)
            with act.Fori(0, 7) as i:
                split(ff1_0 + 2, i * 16, i * 2)
                relus(1, i, i * 2)
                split(ff1_0 + 3, i * 16, i * 2)
                relus(2, i + 1, i * 2)
            split(ff2_0)
            act.wait_ge(f1_done, 4)
            act.wait_ge(*block_done[WO2 + 2])
            split_x(0, F1[:, 0, :])
            relus(15, 7)

            act.wait_ge(f1_done, 32)
            for half in range(2):
                n0 = ff2_0 + 8 * half
                for g in (1, 2):
                    split(n0 + g)
                    if n0 + g == ff2_0 + 1:
                        act.wait_ge(*block_done[WO2 + 3])
                    split_x(g % 2, F1[:, g, :])
                with act.Fori(0, 2) as i:
                    for g in (3, 4):
                        split(n0 + g, i * 16, i * 2)
                        split_x(g % 2, F1[:, i * 2 + g, :])
                split(n0 + 7)
                split_x(1, F1[:, 7, :])
                if half == 0:
                    split(n0 + 8)
                    split_x(0, F1[:, 0, :])

        @block.vector
        def _(dve):
            links = [0]

            def link(ins):
                links[0] += 1
                ins.then_inc(dve_chain, 1)
                dve.wait_ge(dve_chain, links[0])

            def lower(dst, src, hi):
                return dve.tensor_tensor(dst, src, hi.bitcast(f32), ALU.subtract)

            def split(n, more=0):
                w = blocks[n][2].shape[1] * blocks[n][2].shape[2]
                dve.wait_ge(w_hi, more + (n + 1))
                lower(WL[n % 2][:, 0:w], RAW[n % 2][:, 0:w], WH[n % 2][:, 0:w]).then_inc(w_lo, 1)

            def split_x(slot, e, src, more=0):
                dve.wait_ge(x_hi, more + (e + 1))
                lower(XL[slot][:, :], src, XH[slot][:, :]).then_inc(x_lo, 1)

            def gates_logf():
                b = full(dve, "gates")
                free(dve.tensor_tensor(G8[:, :, :], b[:, 0:TT * 2 * H].rearrange("p (a b) -> p a b", a=TT),
                                       BG[:, :].unsqueeze(1).to_broadcast([P, TT, 2 * H]), ALU.add), "gates")
                drained(dve, "gates")
                link(dve.tensor_scalar(LF[:, :, :], G8[:, :, H:2 * H], 0.0, None, ALU.min))
                dve.wait_ge(softplus_done, 1)
                dve.tensor_tensor(LF[:, :, :], LF[:, :, :], GT1[:, :, :], ALU.subtract).then_inc(logf_done, 1)

            def gates_g():
                b = full(dve, "F")
                free(dve.tensor_copy(FS[:, :, :], b[:, 0:TT * H].rearrange("p (a b) -> p a b", a=TT)), "F")
                drained(dve, "F")
                dve.tensor_tensor(GG[:, :, :], G8[:, :, 0:H], FS[:, :, :], ALU.subtract).then_inc(g_done, 1)

            def running_max():
                b = full(dve, "g_rows")
                free(dve.tensor_copy(GROW[:, :], b[0:H, :]), "g_rows")
                drained(dve, "g_rows")
                dve.tensor_tensor_scan(MROW[:, :], GROW[:, :], GROW[:, :], 0.0, ALU.max, ALU.max).then_inc(m_done, 1)

            def m_sum():
                b = full(dve, "m_columns")
                free(dve.tensor_tensor(FLOOR[:, :, :], FS[:, :, :], b[:, 0:TT * H].rearrange("p (a b) -> p a b", a=TT),
                                       ALU.add), "m_columns")

            def conv_taps(c, key):
                dve.wait_ge(conv_first, c + 1)
                b = full(dve, key)
                for back in (1, 2, 3):
                    ins = dve.scalar_tensor_tensor(QK[:, c, back:S], b[:, 0:S - back], col(C_CW + 8 * (3 - back) + c),
                                                   QK[:, c, back:S], ALU.mult, ALU.add)
                    if back < 3:
                        link(ins)
                free(ins, key)

            def mlstm_weights(h):
                p = PP[h % 2]
                drained(dve, ("m_all", h))
                for i in range(TT):
                    w = S - i * P
                    ins = dve.tensor_scalar(p[:, ML_OFF[i]:ML_OFF[i] + w], MB[:, h, i * P:S], GG[:, i, h:h + 1], 0.0,
                                            ALU.add, ALU.min)
                ins.then_inc(ml_arg, 1)
                dve.wait_ge(ml_exp, h + 1)
                for i in range(TT):
                    c = slice(ML_OFF[i], ML_OFF[i] + P)
                    ins = dve.tensor_tensor(p[:, c], p[:, c], TRIU[:, :], ALU.mult)
                link(ins)
                for i, b, c0 in ((0, 2, 0), (1, 3, 0), (3, 3, 384), (2, 4, 0)):
                    full(dve, ("ms", h, b))
                    w = S - i * P
                    c = slice(ML_OFF[i], ML_OFF[i] + w)
                    ins = dve.scalar_tensor_tensor(p[:, c], bank[b][:, c0:c0 + w], SCALE, p[:, c], ALU.mult, ALU.mult)
                    if i != 1:
                        free(ins, ("ms", h, b))

            def mlstm_out(h):
                hm = HM[h % 2]
                if h == 0:
                    dve.wait_ge(floor_done, 1)
                    for j in range(TT):
                        drained(dve, ("tm", first["o"], j))
                num, den = full(dve, ("num", h)), full(dve, ("den", h))
                link(dve.tensor_scalar(RDEN[:, :], den[:, 0:TT], -1.0, None, ALU.mult))
                free(dve.tensor_tensor(RDEN[:, :], den[:, 0:TT], RDEN[:, :], ALU.max), ("den", h))
                drained(dve, ("den", h))
                link(dve.tensor_tensor(RDEN[:, :], RDEN[:, :], FLOOR[:, :, h], ALU.max))
                link(dve.reciprocal(RDEN[:, :], RDEN[:, :]))
                free(dve.tensor_tensor(hm[:, :, :], quarters(num[:, :]), RDEN[:, :].unsqueeze(2).to_broadcast([P, TT, P]),
                                       ALU.mult), ("num", h))
                drained(dve, ("num", h))
                link(dve.tensor_tensor(hm[:, :, :], hm[:, :, :], O[:, :, tile_of(h)], ALU.mult))
                link(dve.tensor_tensor(SQ[:, :, :], hm[:, :, :], hm[:, :, :], ALU.mult))
                dve.tensor_reduce(SSQ[:, 10:14], SQ[:, :, :], AX.X, ALU.add).then_inc(ml_ss, 1)
                dve.wait_ge(rstd_done, MT + TT + h + 1)
                dve.tensor_tensor(hm[:, :, :], hm[:, :, :], RST[:, 10:14].unsqueeze(2).to_broadcast([P, TT, P]),
                                  ALU.mult).then_inc(ml_h, 1)

            def mlstm_y(h):
                b = full(dve, ("hT", h))
                drained(dve, fm_key("z_a", h))
                free(dve.scalar_tensor_tensor(Y[:, h, :], b[:, :], col(C_MN + h), Y[:, h, :], ALU.mult, ALU.mult), ("hT", h))

            def softmax(j):
                for i in range(2):
                    b = full(dve, ("cs", j, i))
                    ins = dve.tensor_reduce(SMX[:, 2 * i:2 * i + 2], b[:, :].rearrange("p (a b) -> p a b", a=2), AX.X,
                                            ALU.max, negate=True)
                link(ins)
                dve.tensor_scalar(SMX[:, :], SMX[:, :], SCALE, None, ALU.mult).then_inc(max_done, 1)
                drained(dve, ("cs", j, 0))
                drained(dve, ("cs", j, 1))
                link(dve.reciprocal(SSUM[:, :], SSUM[:, :]))
                dve.tensor_tensor(PROB[j % 2][:, :, :], PROB[j % 2][:, :, :],
                                  SSUM[:, :].unsqueeze(2).to_broadcast([P, H, NMEM]), ALU.mult).then_inc(probs_done, 1)

            def mem_y(j):
                if j == 0:
                    for c in range(H):
                        drained(dve, fm_key("z_c", c))
                b = full(dve, ("yc", j))
                y = Y[:, 8:12, tile_of(j)]
                free(dve.tensor_tensor(y, quarters(b[:, :]), y, ALU.mult), ("yc", j))

            def pool_window(g):
                drained(dve, fm_key("u", g))
                if g:
                    dve.wait_ge(pooled, g)
                src, w = UP[:, g, :], 1
                while w < WINDOWS[g]:
                    dst = PW[w.bit_length() % 2][:, :]
                    link(dve.tensor_tensor(dst[:, PAD:], src[:, PAD:], src[:, PAD - w:PAD + S - w], ALU.add))
                    src, w = dst, 2 * w
                edge, rest = slice(PAD, PAD + 16), slice(PAD + 16, PAD + S)
                link(dve.tensor_tensor(src[:, edge], src[:, edge], PINV[:, g, :], ALU.mult))
                link(dve.tensor_tensor(UP[:, g, edge], src[:, edge], UP[:, g, edge], ALU.subtract))
                dve.scalar_tensor_tensor(UP[:, g, rest], src[:, rest], 1 / w, UP[:, g, rest], ALU.mult,
                                         ALU.subtract).then_inc(pooled, 1)

            def pool_scaled():
                for g in range(4):
                    b = full(dve, ("pool", g))
                    free(dve.tensor_scalar(UP[:, g, PAD:PAD + S], b[:, :], col(C_PS + g), None, ALU.mult), ("pool", g))

            def pool_y():
                for g in range(4):
                    drained(dve, ("pool", g))
                    drained(dve, fm_key("z_b", g))
                    dve.tensor_tensor(Y[:, 4 + g, :], Y[:, 4 + g, :], UP[:, g, PAD:PAD + S], ALU.mult).then_inc(yb_done, 1)

            def logits_logf():
                for j in range(TT):
                    b = full(dve, ("lg", j))
                    dve.tensor_scalar(LF2[:, j, :], b[:, :], 0.0, None, ALU.min).then_inc(lg_min, 1)
                for j in range(TT):
                    dve.wait_ge(lg_softplus, j + 1)
                    free(dve.tensor_tensor(LF2[:, j, :], LF2[:, j, :], bank[turn["lg", j][0]][:, :], ALU.subtract), ("lg", j))

            def level_operands(l):
                half = P >> (l + 1)

                def view(t):
                    return t[:, :].rearrange("p (b t) -> p b t", t=2 * half)

                cum, ee = view(CUM), view(EE)
                left, right = slice(0, half), slice(half, 2 * half)
                nb = H * S // (2 * half)
                mid = cum[:, :, half - 1:half].to_broadcast([P, nb, half])
                if l == 0:
                    for h in range(H):
                        drained(dve, ("cum", h))
                    dve.wait_ge(zeros_set, 3)
                dve.tensor_tensor(ee[:, :, right], cum[:, :, right], mid, ALU.subtract).then_inc(lv_arg, 1)
                dve.tensor_tensor(ee[:, :, left], mid, cum[:, :, left], ALU.subtract).then_inc(lv_arg, 1)
                dve.wait_ge(lv_exp, l + 1)
                dve.tensor_tensor(view(QE)[:, :, right], view(Q2)[:, :, right], ee[:, :, right], ALU.mult).then_inc(lv_qk, 1)
                dve.tensor_tensor(view(KE)[:, :, left], view(K2)[:, :, left], ee[:, :, left], ALU.mult).then_inc(lv_qk, 1)

            def level_merge(l, half):
                if l < 0:
                    dve.wait_ge(masks_set, 1)
                    dve.wait_ge(zeros_set, 3)
                mask = MASK[:, LEVELS if l < 0 else l, :].unsqueeze(1).to_broadcast([P, TT, P])
                for h in (2 * half, 2 * half + 1):
                    b = full(dve, ("lv", l, h))
                    free(dve.copy_predicated(SC[:, h * TT:h * TT + TT, :], mask, quarters(b[:, :])), ("lv", l, h))

            def q_cum():
                dve.wait_ge(qc_exp, 1)
                dve.tensor_tensor(QE[:, :], Q2[:, :], EE[:, :], ALU.mult).then_inc(qcum_done, 1)

            def k_dec():
                dve.wait_ge(qcum_done, 1)
                cum = CUM[:, :].rearrange("p (c t) -> p c t", t=P)
                dve.tensor_tensor(EE[:, :].rearrange("p (c t) -> p c t", t=P), cum[:, :, P - 1:P].to_broadcast([P, H * TT, P]),
                                  cum, ALU.subtract).then_inc(kd_arg, 1)
                dve.wait_ge(kd_exp, 1)
                dve.tensor_tensor(KE[:, :], K2[:, :], EE[:, :], ALU.mult).then_inc(kd_done, 1)

            def gla_norm(j):
                dve.wait_ge(rstd_done, MT + TT + H + TT + TT + j + 1)
                for i in range(2):
                    b = full(dve, ("o2", j, i))
                    free(dve.tensor_tensor(OJ[:, 512 * i:512 * i + 512].rearrange("p (a b) -> p a b", a=2),
                                           b[:, :].rearrange("p (a b) -> p a b", a=2),
                                           RST[:, 10 + 2 * i:12 + 2 * i].unsqueeze(2).to_broadcast([P, 2, DV]),
                                           ALU.mult), ("o2", j, i))
                if j < TT - 1:
                    dve.wait_ge(etot_done, 1)
                    for h in range(H):
                        b = full(dve, ("kv", j, h // 2))
                        src = b[:, (h % 2) * DV:(h % 2 + 1) * DV]
                        if j == 0:
                            ins = dve.tensor_copy(STATE[:, h, :], src)
                        else:
                            ins = dve.scalar_tensor_tensor(STATE[:, h, :], STATE[:, h, :], ETOT[:, h * TT + j:h * TT + j + 1],
                                                           src, ALU.mult, ALU.add)
                        if h % 2:
                            free(ins, ("kv", j, h // 2))

            def gla_y(j, i):
                b = full(dve, ("oT", j, i))
                if GO + 1 + j > first["g_b"]:
                    drained(dve, ("fm", GO + j, 1))
                for cc in range(4):
                    c = 4 * i + cc
                    if j == 0:
                        drained(dve, fm_key("r", c))
                    r = R[:, c, tile_of(j)]
                    ins = dve.scalar_tensor_tensor(r, b[:, tile_of(cc)], col(C_GN + c), r, ALU.mult, ALU.mult)
                free(ins, ("oT", j, i))

            def add_branches(c0, c1):
                drained(dve, ("oT", TT - 1, 0))
                drained(dve, ("oT", TT - 1, 1))
                for c in range(c0, c1):
                    drained(dve, fm_key("g_b", c))
                    dve.tensor_tensor(R[:, c, :], R[:, c, :], U[:, c, :], ALU.add).then_inc(m_ready, 1)

            def layer_stats(src, j, var):
                for i in range(2):
                    link(dve.bn_stats(BN[:, i, :], src[:, j, 512 * i:512 * i + 512]))
                dve.bn_aggr(MV[:, j, :], BN[:, :, :].rearrange("p a b -> p (a b)")).then_inc(ln_var, 1)

            def layer_scale(dst, j, r):
                dve.wait_ge(rstd_done, r)
                return dve.tensor_scalar(dst[:, j, :], dst[:, j, :], MV[:, j, 0:1], RST[:, j:j + 1], ALU.subtract, ALU.mult)

            def v_norm(j):
                dve.wait_ge(av_gelu, TT + j + 1)
                layer_stats(VH, j, j)
                layer_scale(VH, j, MT + TT + H + TT + j + 1).then_inc(vhat_done, 1)

            def w_s_lower():
                for j in range(TT):
                    drained(dve, ("tm", first["v2"] + 2, j))
                for i in range(2):
                    b = full(dve, ("wsT", i))
                    free(dve.tensor_tensor(WST[:, 4 * i:4 * i + 4, :], quarters(b[:, :]),
                                           TRIU[:, :].unsqueeze(1).to_broadcast([P, 4, P]), ALU.mult), ("wsT", i))

            def sg_gate(i):
                if i == 0:
                    dve.wait_ge(bs_in, 16)
                for g in (2 * i, 2 * i + 1):
                    drained(dve, fm_key("a_u", g))
                    b = full(dve, ("sg", g))
                    link(dve.tensor_tensor(quarters(b[:, :]), quarters(b[:, :]),
                                           BS[:, g, :].unsqueeze(1).to_broadcast([P, TT, P]), ALU.add))
                    free(dve.tensor_tensor(U[:, g, :], U[:, g, :], b[:, :], ALU.mult), ("sg", g))

            def side(n):
                if n == 0:
                    for j in range(TT):
                        dve.wait_ge(rstd_done, MT + j + 1)
                        dve.tensor_scalar(XN[:, j, :], RES[:, j, :], RST[:, MT + j:MT + j + 1], None, ALU.mult).then_inc(x_normed, 1)
                    dve.wait_ge(wg_hi, 1)
                    lower(WGL[:, :, :], WG[:, :, :], WGH[:, :, :]).then_inc(wg_lo, 1)
                if n == 4:
                    for c in range(KC):
                        dve.wait_ge(t_hi, KC + c + 1)
                        free(dve.scalar_tensor_tensor(TL[:, c, :], bank[4 + c % 4][:, :], col(C_NORM + c),
                                                      TH[:, c, :].bitcast(f32), ALU.mult, ALU.subtract), ("xT", c))
                    gates_logf()
                if n == 5: gates_g()
                if n == 6: running_max()
                if n == 7: m_sum()
                if 0 <= n - ML - 3 < H: mlstm_y(n - ML - 3)
                if 0 <= n - ML - 1 < H: mlstm_out(n - ML - 1)
                if 0 <= n - ML < H: mlstm_weights(n - ML)
                if n == AT:
                    dve.memset(UP[:, :, 0:PAD], 0.0)
                    for i in range(2):
                        dve.memset(PW[i][:, 0:PAD], 0.0)
                if 0 <= n - AT - 2 < TT: mem_y(n - AT - 2)
                if 0 <= n - AT < TT: softmax(n - AT)
                if n == first["u"] + 1: pool_window(0); pool_window(1)
                if n == first["u"] + 2: pool_window(2); pool_window(3)
                if n == WO - 1: pool_scaled()
                if n == LG: logits_logf()
                if n == LV + 4: w_s_lower()
                if 0 <= n - LV < 2 * (LEVELS + 1): level_merge((n - LV) // 2 - 1, (n - LV) % 2)
                if 0 < n - LV <= 2 * LEVELS and (n - LV) % 2: level_operands((n - LV) // 2)
                if n in (first["a_u"], first["a_u"] + 1):
                    v_norm(2 * (n - first["a_u"]))
                    v_norm(2 * (n - first["a_u"]) + 1)
                if 0 <= n - SG < 4: sg_gate(n - SG)
                if n == GO - 3: q_cum()
                if n == GO - 2: k_dec()
                if 0 <= n - GO < TT: gla_norm(n - GO)
                if 0 <= n - GO - 1 < TT:
                    gla_y(n - GO - 1, 0)
                    if n > GO + 1:
                        gla_y(n - GO - 1, 1)
                if n == WO2 - 1: add_branches(4, 6)

            def add_half(n0, half, scale, j):
                key = ("tm", n0, j)
                b = full(dve, key)
                r = RES[:, j, 512 * half:512 * half + 512]
                free(dve.scalar_tensor_tensor(r, r, scale, b[:, :], ALU.mult, ALU.add), key)
                drained(dve, key)

            def rows_lo(name, j, t0):
                for i in range(2):
                    dve.wait_ge(t_hi, t0 + 2 * j + i + 1)
                    free(lower(TL[:, 4 * i:4 * i + 4, tile_of(j)], quarters(bank[6 + i][:, :]),
                               TH[:, 4 * i:4 * i + 4, tile_of(j)]), (name, j, i))

            def norm_rows(j, r, g, b, done):
                link(layer_scale(RES, j, r))
                link(dve.tensor_tensor(RES[:, j, :], RES[:, j, :], g[:, :], ALU.mult))
                dve.tensor_tensor(RES[:, j, :], RES[:, j, :], b[:, :], ALU.add).then_inc(done, 1)

            def drain(n):
                name, i = name_of(n)
                fm = [(("fm", n, t), 2 * i + t) for t in range(2)]
                if name in ("q", "k"):
                    for key, c in fm:
                        conv_taps(c + (4 if name == "k" else 0), key)
                if name == "z_b" and i == 1:
                    pool_y()
                if name == "w_out" and i == 2:
                    for j in range(TT):
                        add_half(n - 2, 0, 1.0, j)
                if name == "w_out" and i == 5:
                    dve.wait_ge(fg_in, 16)
                    for j in range(TT + 2):
                        if j < TT:
                            add_half(n - 2, 1, 1.0, j)
                        if 1 <= j <= TT:
                            dve.wait_ge(rstd_done, MT + TT + H + j)
                            r = RES[:, j - 1, :]
                            dve.scalar_tensor_tensor(r, r, RST[:, 5 + j:6 + j], FG[:, :], ALU.mult, ALU.mult).then_inc(x1_done, 1)
                        if j >= 2:
                            rows_lo("x1T", j - 2, 2 * KC)
                if name == "low":
                    key = ("fm", n, 0)
                    dve.wait_ge(alt_set, 1)
                    b = full(dve, key)
                    free(dve.tensor_scalar(ALT[0:16, :], b[0:16, :], LOWB[:, :], None, ALU.add), key)
                if name in ("q2", "k2"):
                    for key, c in fm:
                        b = full(dve, key)
                        if name == "q2":
                            ins = dve.tensor_scalar(Q2[:, c * S:c * S + S], b[:, :], col(C_B2 + 16 + c), SCALE, ALU.add, ALU.mult)
                        else:
                            ins = dve.tensor_scalar(K2[:, c * S:c * S + S], b[:, :], col(C_B2 + 20 + c), None, ALU.add)
                        free(ins, key)
                if name in ("v2", "a_v") and i % 2:
                    dst, bias = (V2, BV) if name == "v2" else (VH, BAV)
                    h = slice(i // 2 * 512, i // 2 * 512 + 512)
                    dve.wait_ge(bv_in, 32)
                    for j in range(TT):
                        key = ("tm", n - 1, j)
                        b = full(dve, key)
                        free(dve.tensor_tensor(dst[:, j, h], b[:, :], bias[:, h], ALU.add), key)
                if name == "g_a":
                    for key, c in fm:
                        dve.wait_ge(ga_sig, c + 1)
                        b = full(dve, key)
                        free(dve.tensor_tensor(U[:, c, :], U[:, c, :], b[:, :], ALU.mult), key)
                if n == GO + 1:
                    gla_y(0, 1)
                if name == "g_b":
                    for half in range(2):
                        drained(dve, ("oT", min(n - GO - 1, TT - 1), half))
                    for key, c in fm:
                        dve.wait_ge(gb_sig, c + 1)
                        b = full(dve, key)
                        free(dve.tensor_tensor(R[:, c, :], R[:, c, :], b[:, :], ALU.mult), key)
                    if i == 2:
                        add_branches(0, 4)
                    if i == 3:
                        add_branches(6, 8)
                if name == "w_out2" and i == 1:
                    dve.wait_ge(x1_back, 16)
                    for j in range(TT):
                        add_half(n - 1, 0, ALPHA, j)
                if name == "w_out2" and i == 3:
                    dve.wait_ge(ln1_in, 32)
                    r0 = MT + TT + H + 3 * TT
                    for j in range(TT + 2):
                        if j < TT:
                            add_half(n - 1, 1, ALPHA, j)
                            layer_stats(RES, j, j)
                        if 1 <= j <= TT:
                            norm_rows(j - 1, r0 + j, L1G, L1B, h1_done)
                        if j >= 2:
                            rows_lo("h1T", j - 2, 2 * KC + 2 * TT)

            def stage(n):
                if n + 1 >= ff1_0:
                    return
                name, i = name_of(n + 1)
                if name == "w_out":
                    g = WO_GROUPS[i % 3]
                    split_x(i % 2, i, Y[:, 4 * g:4 * g + 4, :].rearrange("p a b -> p (a b)"))
                if name == "w_out2":
                    g = i % 2
                    split_x(i % 2, E_WO2 + i, R[:, 4 * g:4 * g + 4, :].rearrange("p a b -> p (a b)"))

            dve.wait_ge(consts_in, 16 * 6)
            dve.tensor_copy(MASK[:, :, :], MASKF[:, :, :]).then_inc(masks_set, 1)
            for j in range(MT):
                dve.wait_ge(rstd_done, j + 1)
                dve.tensor_scalar(MEM[:, j, :], MEM[:, j, :], RST[:, j:j + 1], None, ALU.mult).then_inc(mem_normed, 1)
            split(0)
            drained(dve, "vectors")
            for c in range(KC):
                dve.wait_ge(t_hi, (c | 1) + 1)
                q = (c % 2) * NMEM
                ins = dve.scalar_tensor_tensor(MEML[:, c, :], bank[4 + c // 2][:, q:q + NMEM], col(C_MEMN + c),
                                               MEMH[:, c, :].bitcast(f32), ALU.mult, ALU.subtract)
                if c % 2:
                    free(ins, ("memT", c // 2))
            for n in range(ff1_0):
                split(n + 1)
                side(n)
                stage(n)
                drain(n)

            def squares(m, group, more=0):
                for t in range(2):
                    dve.wait_ge(bank_free[t], more + (f0[t] + m + 1))
                    q = (2 * m + t) % 4 * S
                    f = F1[:, group, q:q + S]
                    dve.tensor_tensor(f, f, f, ALU.mult).then_inc(f1_done, 1)

            split(ff1_0 + 1)
            squares(0, 0)
            with dve.Fori(0, 7) as i:
                split(ff1_0 + 2, i * 2)
                squares(1, i, i * 2)
                split(ff1_0 + 3, i * 2)
                squares(2, i + 1, i * 2)
            split(ff2_0)
            split_x(0, E_FF2, F1[:, 0, :])
            squares(15, 7)

            for half in range(2):
                n0, e0 = ff2_0 + 8 * half, E_FF2 + 8 * half
                for g in (1, 2):
                    split(n0 + g)
                    split_x(g % 2, e0 + g, F1[:, g, :])
                with dve.Fori(0, 2) as i:
                    for g in (3, 4):
                        split(n0 + g, i * 2)
                        split_x(g % 2, e0 + g, F1[:, i * 2 + g, :], i * 2)
                split(n0 + 7)
                split_x(1, e0 + 7, F1[:, 7, :])
                if half == 0:
                    split(n0 + 8)
                    split_x(0, e0 + 8, F1[:, 0, :])
                    for j in range(TT):
                        add_half(n0, 0, ALPHA, j)
            dve.wait_ge(ln2_in, 32)
            r0 = MT + TT + H + 4 * TT
            for j in range(TT + 1):
                if j < TT:
                    add_half(ff2_0 + 8, 1, ALPHA, j)
                    layer_stats(RES, j, j)
                if j:
                    norm_rows(j - 1, r0 + j, L2G, L2B, h2_done)

        @block.gpsimd
        def _(pool):
            links, roots = [0], [0]

            def link(ins):
                links[0] += 1
                ins.then_inc(pool_chain, 1)
                pool.wait_ge(pool_chain, links[0])

            def rstd(dst, src, w, mean, eps):
                if roots[0]:
                    pool.wait_ge(rstd_done, roots[0])
                roots[0] += 1
                link(pool.tensor_scalar(RTMP[:, 0:w], src, mean, eps, ALU.mult, ALU.add))
                pool.tensor_tensor(dst, RTMP[:, 0:w], NHALF[:, 0:w], ALU.pow).then_inc(rstd_done, 1)

            def load_all(dst, src, s):
                pool.dma_start(dst, src.partition_broadcast(P)).then_inc(s, 16)

            pool.memset(ONES[:, :], 1.0).then_inc(ones_set, 1)
            link(pool.memset(NHALF[:, :], -0.5))
            for c in range(MT + TT):
                pool.wait_ge(squared, c + 1)
                rstd(RST[:, c:c + 1], SSQ[:, c:c + 1], 1, 1.0, RMS_EPS)
            full(pool, ("m_all", H - 1))
            pool.memset(ALT[:, :], 1.0).then_inc(alt_set, 1)
            for h in range(H):
                pool.wait_ge(ml_ss, h + 1)
                rstd(RST[:, 10:14], SSQ[:, 10:14], 4, 1 / P, RMS_EPS)
            pool.wait_ge(ml_h, H)
            pool.dma_start(POOLW[:, :, :], a["pool_w"][0].rearrange("g c d -> c g d")).then_inc(poolw_in, 16)
            full(pool, ("yc", TT - 1))
            load_all(BV[:, :], a["b_in_2"][0, 3 * D:4 * D], bv_in)
            load_all(BAV[:, :], a["b_in_2"][0, D:2 * D], bv_in)
            for j in range(TT):
                pool.wait_ge(squared, MT + TT + j + 1)
                rstd(RST[:, 6 + j:7 + j], SSQ[:, 6 + j:7 + j], 1, 1.0, RMS_EPS)
            pool.wait_ge(x1_done, TT)
            pool.dma_start(x1_spill.rearrange("(j p) n -> p j n", p=P), RES[:, :, :]).then_inc(x1_spilled, 16)
            for t in (SC[:, :, :], QE[:, :], KE[:, :]):
                pool.memset(t, 0.0).then_inc(zeros_set, 1)
            pool.wait_ge(x1_spilled, 16)
            for i in range(2):
                drained(pool, ("x1T", TT - 1, i))
            pool.dma_start(WSR[:, :, :], a["sg_w_s_2"][0].rearrange("g t s -> t g s")).then_inc(ws_in, 16)
            full(pool, ("lg", TT - 1))
            load_all(SGG[:, :], a["sg_ln_g_2"][0], sg_in)
            load_all(SGB[:, :], a["sg_ln_b_2"][0], sg_in)
            for j in range(TT):
                drained(pool, ("tm", first["a_v"] + 2, j))
            load_all(BS[:, :, :], a["sg_b_s_2"][0], bs_in)
            pool.wait_ge(sg_in, 32)

            def v_gain(j):
                link(pool.tensor_tensor(VH[:, j, :], VH[:, j, :], SGG[:, :], ALU.mult))
                pool.tensor_tensor(VH[:, j, :], VH[:, j, :], SGB[:, :], ALU.add).then_inc(vh_ready, 1)

            for j in range(TT):
                pool.wait_ge(ln_var, j + 1)
                rstd(RST[:, j:j + 1], MV[:, j, 1:2], 1, 1.0, LN_EPS)
                if j:
                    pool.wait_ge(vhat_done, j)
                    v_gain(j - 1)
            pool.wait_ge(vhat_done, TT)
            v_gain(TT - 1)
            for j in range(TT):
                pool.wait_ge(squared, MT + 2 * TT + H * (j + 1))
                rstd(RST[:, 10:14], SSQ[:, 10:14], 4, 1.0, LN_EPS)
            pool.wait_ge(m_ready, KC)
            pool.dma_start(RES[:, :, :], x1_spill.rearrange("(j p) n -> p j n", p=P)).then_inc(x1_back, 16)
            load_all(L1G[:, :], a["ln1_g_2"][0], ln1_in)
            load_all(L1B[:, :], a["ln1_b_2"][0], ln1_in)
            load_all(L2G[:, :], a["ln2_g_2"][0], ln2_in)
            load_all(L2B[:, :], a["ln2_b_2"][0], ln2_in)
            for j in range(2 * TT):
                pool.wait_ge(ln_var, TT + j + 1)
                rstd(RST[:, j % TT:j % TT + 1], MV[:, j % TT, 1:2], 1, 1.0, LN_EPS)

        @block.sync
        def _(sp):
            def load(n, src, more=0):
                if n >= 2:
                    sp.wait_ge(w_lo, more + (n - 1))
                k, c = blocks[n][2].shape[1:]
                sp.dma_start(RAW[n % 2][:, 0:k * c].rearrange("p (k c) -> p k c", c=c), src).then_inc(w_loaded[n % 2], 16)

            sp.dma_start(MEM[:, :, :], a["mem"][0].rearrange("(j p) n -> p j n", p=P)).then_inc(mem_in, 16)
            load(0, blocks[0][2])
            for j in range(TT):
                sp.dma_start(RES[:, j, :], a["x"][0, j * P:j * P + P, :]).then_inc(x_in[j], 16)
            for n in range(1, ff1_0):
                load(n, blocks[n][2])
            up = a["w_ff1_2"][0].rearrange("(k p) (b c) -> b p k c", p=P, c=256)
            with sp.Fori(0, 8) as i:
                for b in range(2):
                    load(ff1_0 + b, up[i * 2 + b], i * 2)
            down = a["w_ff2_2"][0].rearrange("(g k p) (h c) -> h g p k c", p=P, k=4, h=2)
            for half in range(2):
                with sp.Fori(0, 4) as i:
                    for b in range(2):
                        load(ff2_0 + 8 * half + b, down[half, i * 2 + b], i * 2)
            for j in range(TT):
                sp.wait_ge(h2_done, j + 1)
                sp.dma_start(out[0, j * P:j * P + P, :], RES[:, j, :]).then_inc(stored, 16)
            sp.wait_ge(stored, 16 * TT)


def constants():
    s, t = np.arange(P)[:, None], np.arange(P)[None, :]
    masks = np.zeros((P, LEVELS + 1, P), np.float32)
    for l in range(LEVELS):
        half = P >> (l + 1)
        masks[:, l] = (s // (2 * half) == t // (2 * half)) & (s % (2 * half) < half) & (t % (2 * half) >= half)
    masks[:, LEVELS] = s == t
    nsel = np.zeros((H, H, P), np.float32)
    for h in range(H):
        nsel[h, h] = -1
    edge = 1 / np.minimum(np.arange(1, 17)[None, :], np.array(WINDOWS)[:, None]).astype(np.float32)
    return {"c_ident": (s == t).astype(np.float32), "c_triu": (s <= t).astype(np.float32),
            "c_triu16": ((s <= t) / 16).astype(np.float32), "c_masks": masks, "c_nsel": nsel,
            "c_pool_edge": edge.astype(np.float32)}


def kernel(**inputs):
    import concourse.bacc as bacc
    from concourse import mybir
    from concourse.bass_utils import run_bass_kernel_spmd

    nc = bacc.Bacc("TRN2", target_bir_lowering=False, num_devices=1)
    arrays = {f"in_{k}": np.ascontiguousarray(v) for k, v in inputs.items()}
    arrays.update({f"in_{k}": v for k, v in constants().items()})
    a = {k[3:]: nc.dram_tensor(k, v.shape, mybir.dt.from_np(v.dtype), kind="ExternalInput").ap() for k, v in arrays.items()}
    out = nc.dram_tensor("out_0", (1, S, D), mybir.dt.float32, kind="ExternalOutput").ap()
    x1_spill = nc.dram_tensor("x1_spill", (S, D), mybir.dt.float32, kind="Internal").ap()
    two_blocks(nc, a, out, x1_spill)
    r = run_bass_kernel_spmd(nc, [arrays], core_ids=[0])
    return r.results[0]["out_0"]
```

```python
import numpy as np


P = 128
S = 512
D = 1024
TT = S // P
KC = D // P
NMEM = 256
MT = NMEM // P
H = 4
GW = 512
RMS_EPS = 1e-6
LN_EPS = 1e-5
SCALE = float(P) ** -0.5
ALPHA = 2.0 ** 0.25
LEVELS = 7
WINDOWS = (2, 4, 8, 16)
K1 = 1024
DV = 256
PAD = 8
ML_OFF = (0, 512, 896, 1152)


def block_list(a):
    w_in, w_kv, w_out = a["w_in"][0], a["w_mem_kv"][0], a["w_out"][0]
    w_in2, w_out2, w_ff1, w_ff2 = a["w_in_2"][0], a["w_out_2"][0], a["w_ff1_2"][0], a["w_ff2_2"][0]

    def chunks(w):
        return w.rearrange("(k p) n -> p k n", p=P)

    blocks = []

    def fm(name, w, c0, width):
        for c in range(c0, c0 + width, 256):
            blocks.append(("fm", name, chunks(w)[:, :, c:c + 256]))

    def tm(name, w, c0, width, groups):
        for c in range(c0, c0 + width, 512):
            for g in groups:
                blocks.append(("tm", name, chunks(w)[:, 4 * g:4 * g + 4, c:c + 512]))

    fm("km", w_kv, 0, GW)
    tm("vm", w_kv, GW, GW, (0, 1))
    blocks.append(("fm", "gates", chunks(w_in)[:, :, 5 * GW:5 * GW + P]))
    fm("q", w_in, 0, GW)
    fm("k", w_in, GW, GW)
    tm("v", w_in, 2 * GW, GW, (0, 1))
    tm("o", w_in, 3 * GW, GW, (0, 1))
    z_a = 4 * GW
    u = 5 * GW + 2 * H
    fm("z_a", w_in, z_a, GW)
    fm("qc", w_in, u + 2 * GW, GW)
    fm("z_c", w_in, u + 3 * GW, GW)
    fm("u", w_in, u, GW)
    fm("z_b", w_in, u + GW, GW)
    tm("w_out", w_out, 0, D, (0, 2, 1))
    low = 5 * D
    fm("q2", w_in2, 2 * D, 256)
    blocks.append(("fm", "low", chunks(w_in2)[:, :, low:low + P]))
    fm("q2", w_in2, 2 * D + 256, 256)
    fm("k2", w_in2, 2 * D + D // 2, D // 2)
    tm("v2", w_in2, 3 * D, D, (0, 1))
    tm("a_v", w_in2, D, D, (0, 1))
    fm("a_u", w_in2, 0, D)
    fm("g_a", w_in2, low + 16, D)
    fm("r", w_in2, 4 * D, D)
    fm("g_b", w_in2, low + 16 + D, D)
    tm("w_out2", w_out2, 0, D, (0, 1))
    fm("ff1", w_ff1, 0, 4 * D)
    tm("ff2", w_ff2, 0, D, range(8))
    return blocks


def two_blocks(nc, a, out, x1_spill):
    from concourse import mybir
    from contextlib import ExitStack

    f32 = mybir.dt.float32
    f32r = mybir.dt.float32r
    u8 = mybir.dt.uint8
    ALU = mybir.AluOpType
    ACT = mybir.ActivationFunctionType
    AX = mybir.AxisListType

    blocks = block_list(a)
    N = len(blocks)
    steps = {}
    for n, (_, name, _) in enumerate(blocks):
        steps.setdefault(name, []).append(n)
    first = {name: of[0] for name, of in steps.items()}

    def name_of(n):
        return blocks[n][1], steps[blocks[n][1]].index(n)

    base = 16512
    top = [base]

    def at(name, shape, offset, dt=f32):
        return nc.alloc_sbuf_tensor_at(name, shape, dt, offset=offset)

    def place(name, shape, dt=f32, size=4):
        n = int(np.prod(shape[1:])) * size
        t = at(name, shape, top[0], dt)
        top[0] += (n + 31) // 32 * 32
        return t

    RAW = [place(f"w_raw{i}", [P, 2048]) for i in range(2)]
    WH = [place(f"w_hi{i}", [P, 2048], f32r) for i in range(2)]
    WL = [place(f"w_lo{i}", [P, 2048], f32r) for i in range(2)]
    XS = top[0]
    top[0] += 32 * K1
    TH = place("act_t_hi", [P, KC, S], f32r)
    TL = place("act_t_lo", [P, KC, S], f32r)
    A = top[0]
    top[0] += 88 * K1 + 64

    IDENT = place("ident", [P, P])
    TRIU = place("triu", [P, P])
    TRI16 = place("triu_16th", [P, P])
    ONES = place("ones", [P, P])
    MASK = place("level_masks", [P, LEVELS + 1, P], u8, 1)
    VC = place("vector_columns_sb", [P, P + 2])
    PINV = place("pool_edge", [P, 4, 16])
    NHALF = place("minus_half", [P, 16])
    SSQ = place("mean_squares", [P, 16])
    RST = place("rstd", [P, 16])
    RTMP = place("rstd_tmp", [P, 16])
    G8 = place("gates", [P, TT, 2 * H])
    LF = place("log_f", [P, TT, H])
    GT1 = place("gate_tmp", [P, TT, H])
    GG = place("i_minus_F", [P, TT, H])
    FS = place("F", [P, TT, H])
    FLOOR = place("den_floor", [P, TT, H])
    RDEN = place("den", [P, TT])
    SMX = place("neg_max", [P, H])
    SSUM = place("row_sum", [P, H])
    BN = place("bn", [P, TT, 2, 6])
    MV = place("mean_var", [P, TT, 2])
    ETOT = place("exp_total", [P, H * TT])
    assert top[0] <= 229344, top[0]

    XH = [at(f"x_hi{i}", [P, 2048], XS + 8 * K1 * i, f32r) for i in range(2)]
    XL = [at(f"x_lo{i}", [P, 2048], XS + 16 * K1 + 8 * K1 * i, f32r) for i in range(2)]
    XH.append(at("x_hi2", [P, 2048], A + 56 * K1, f32r))
    XL.append(at("x_lo2", [P, 2048], A + 16 * K1, f32r))
    WH.append(at("w_hi2", [P, 2048], A + 40 * K1, f32r))
    WL.append(at("w_lo2", [P, 2048], A + 48 * K1, f32r))
    MEMH = at("mem_t_hi", [P, KC, NMEM], XS, f32r)
    MEML = at("mem_t_lo", [P, KC, NMEM], XS + 8 * K1, f32r)
    MEM = at("mem", [P, MT, D], XS + 16 * K1)
    MASKF = at("level_masks_loaded", [P, LEVELS + 1, P], XS + 26 * K1)
    GATES_T = at("gates_t", [2 * H, S], XS + 20 * K1)
    GROW = at("g_rows", [H, S], XS + 16 * K1)
    MROW = at("m_rows", [H, S], XS + 18 * K1)
    MB = at("minus_m_all", [P, H, S], XS)
    PP = [at(f"mlstm_p{i}", [P, 1280], XS + 8 * K1 + 5 * K1 * i) for i in range(2)]
    HM = [at(f"mlstm_h{i}", [P, TT, P], XS + 18 * K1 + 2 * K1 * i) for i in range(2)]
    SQ = at("mlstm_sq", [P, TT, P], XS + 22 * K1)
    QC = at("q_c", [P, H, S], XS + 24 * K1)
    PT = [at(f"probs_t{i}", [P, 2 * H, P], XS + 8 * K1 + 4 * K1 * i) for i in range(2)]
    LF2 = at("log_f2", [P, TT, S], XS)
    EE = at("decay", [P, H * S], XS)
    KDT = at("k_dec_t", [P, H, TT, P], XS)
    QE = at("q_decayed", [P, H * S], XS + 8 * K1)
    QEC = at("q_decayed_right_halves", [P, H * S // 2], XS + 8 * K1)
    KE = at("k_decayed", [P, H * S], XS + 16 * K1)
    SC = at("gla_scores", [P, H * TT, P], XS + 24 * K1)

    RES = at("residual", [P, TT, D], A)
    XN = at("x_normed", [P, TT, D], A + 16 * K1)
    Y = at("y", [P, 12, S], A + 16 * K1)
    QK = at("qk", [P, 8, S], A + 40 * K1)
    V = at("v_and_ones", [P, TT, H, P + 1], A + 56 * K1)
    O = at("o_gate", [P, TT, GW], A + 64 * K1 + 64)
    KM = at("k_mem", [P, H, NMEM], A + 72 * K1 + 64)
    VM = at("v_mem", [P, MT, GW], A + 76 * K1 + 64)
    FG = at("final_g_all", [P, D], A + 80 * K1 + 64)
    WG2 = at("w_gate2_and_bias", [17, S], A + 84 * K1 + 64)
    NSEL = at("minus_head_rows", [H, H, P], A + 86 * K1 + 64)
    PROB = [at(f"probs{i}", [P, H, NMEM], A + 56 * K1 + 4 * K1 * i) for i in range(2)]
    UP = at("u_padded", [P, 4, PAD + S], A + 40 * K1)
    PW = [at(f"pool_sum{i}", [P, PAD + S], A + 49 * K1 + 2560 * i) for i in range(2)]
    POOLW = at("pool_w_sb", [P, 4, P], A + 64 * K1)
    SINK = at("squares_sink", [P, D], A + 68 * K1)
    U = at("u_gelu", [P, KC, S], A)
    WSR = at("w_s_rows", [P, 8, P], A)
    Q2 = at("q2", [P, H * S], A + 16 * K1)
    K2 = at("k2", [P, H * S], A + 24 * K1)
    CUM = at("cum", [P, H * S], A + 32 * K1)
    V2 = at("v2", [P, TT, D], A + 40 * K1)
    VH = at("v_hat", [P, TT, D], A + 56 * K1)
    R = at("r_silu", [P, KC, S], A + 56 * K1)
    BV = at("b_v_all", [P, D], A + 72 * K1)
    WST = at("w_s_t", [P, 8, P], A + 72 * K1)
    BAV = at("b_av_all", [P, D], A + 76 * K1)
    BS = at("b_s_all", [P, 8, P], A + 76 * K1)
    ALT = at("a_low_t", [32, S], A + 86 * K1 + 64)
    SGG = at("sg_g_all", [P, D], A + 80 * K1)
    SGB = at("sg_b_all", [P, D], A + 84 * K1)
    STATE = at("gla_state", [P, H, 256], A + 80 * K1)
    OJ = at("gla_o", [P, D], A + 84 * K1)
    L1G = at("ln1_g_all", [P, D], A + 72 * K1)
    L1B = at("ln1_b_all", [P, D], A + 76 * K1)
    L2G = at("ln2_g_all", [P, D], A + 80 * K1)
    L2B = at("ln2_b_all", [P, D], A + 84 * K1)
    F1 = at("ff_hidden", [P, 8, 2048], A + 16 * K1)

    C_NORM, C_MEMN, C_CW, C_CB, C_MN, C_PS = 0, 8, 16, 48, 56, 60
    C_B2, C_B2G, C_GN, C_LOW, C_BG = 64, 64 + 40, 64 + 56, P, P + 1

    def col(c):
        return VC[:, c:c + 1]

    ctx = ExitStack()
    with ctx:
        bank = [ctx.enter_context(nc.psum_tensor(f"bank{b}", [P, 512], f32)) for b in range(8)]

        def sem(name):
            return ctx.enter_context(nc.semaphore(name))

        w_loaded = [sem(f"w_loaded{i}") for i in range(2)]
        w_hi, w_lo, w_used = sem("w_hi_done"), sem("w_lo_done"), sem("w_block_used")
        x_hi, x_lo = sem("x_hi_done"), sem("x_lo_done")
        bank_full = [sem(f"bank_full{b}") for b in range(8)]
        bank_free = [sem(f"bank_free{b}") for b in range(8)]
        ident_in, columns_in, tables_in, masks_in, fg_in, wg2_in = (
            sem(s + "_in") for s in ("ident", "columns", "tables", "masks", "fg", "wg2"))
        mem_in = [sem(f"mem_in{j}") for j in range(MT)]
        x_in = [sem(f"x_in{j}") for j in range(TT)]
        poolw_in, bv_in, ws_in, sg_in, bs_in, ln1_in, ln2_in = (sem(s + "_in") for s in
                                                                ("poolw", "bv", "ws", "sg", "bs", "ln1", "ln2"))
        x1_spilled, x1_back, stored = sem("x1_spilled"), sem("x1_back"), sem("stored")
        ones_set, alt_set, zeros_set, masks_set = (sem(s) for s in ("ones_set", "alt_set", "zeros_set", "masks_set"))
        squared, rstd_done = sem("squares_summed"), sem("rstd_done")
        mem_normed, x_normed, t_hi = (sem(s) for s in ("mem_normed", "x_normed", "turned_hi"))
        softplus_done, logf_done, g_done, m_done, floor_done = (sem(s) for s in
                                                                ("softplus_done", "logf_done", "g_done", "m_done", "floor_done"))
        conv_first, qk_done = sem("conv_first_tap"), sem("qk_done")
        ml_arg, ml_exp, ml_ss, ml_h = sem("mlstm_arg"), sem("mlstm_exp"), sem("mlstm_ss"), sem("mlstm_h_done")
        max_done, probs_done = sem("softmax_max"), sem("probs_normed")
        pooled, yb_done, x1_done = sem("pooled"), sem("yb_done"), sem("x1_done")
        lg_min, lg_softplus = sem("logit_min"), sem("logit_softplus")
        lv_arg, lv_exp, lv_qk = sem("level_arg"), sem("level_exp"), sem("level_operands")
        av_gelu, vhat_done, vh_ready, ga_sig, gb_sig = (sem(s) for s in
                                                        ("av_gelu", "vhat_done", "vh_ready", "ga_sigmoid", "gb_sigmoid"))
        qc_exp, qcum_done, kd_arg, kd_exp, kd_done, etot_done = (sem("gla_" + s) for s in
                                                                ("qcum_exp", "qcum", "kdec_arg", "kdec_exp", "kdec", "exp_total"))
        m_ready = sem("m_ready")
        centered = sem("ln_centered")
        ln_var, h1_done, h2_done, f1_done = sem("ln_var"), sem("h1_done"), sem("h2_done"), sem("f1_done")
        pool_chain, dve_chain, act_chain = sem("pool_chain"), sem("dve_chain"), sem("act_chain")

        block = ctx.enter_context(nc.Block())

        turn, uses, block_done = {}, [0] * 8, {}

        def full(eng, key):
            b, u = turn[key]
            eng.wait_ge(bank_full[b], u + 1)
            return bank[b]

        def free(ins, key):
            ins.then_inc(bank_free[turn[key][0]], 1)

        def drained(eng, key):
            b, u = turn[key]
            eng.wait_ge(bank_free[b], u + 1)

        def quarters(t):
            return t.rearrange("p (a b) -> p a b", a=4)

        def slot_of(n):
            return 2 if n - 1 in PAIRED else n % 2

        def weights(n, pair):
            k, c = blocks[n][2].shape[1:]
            return tuple(t[slot_of(n)][:, 0:k * c].rearrange("p (k c) -> p k c", c=c) for t in pair)

        def tile_of(j):
            return slice(j * P, j * P + P)

        ff1_0, ff2_0 = first["ff1"], first["ff2"]
        WO, WO2 = first["w_out"], first["w_out2"]
        WO_GROUPS = (0, 2, 1)
        GATES = first["gates"]
        TURN_X = {2: (0, 1, 2, 3), 3: (4, 5, 6, 7)}
        ML = first["z_a"]
        AT = ML + 4
        LG = first["low"] + 1
        LV = first["v2"]
        GO = LV + 2 * LEVELS + 4
        SG = first["a_u"] + 4
        PAIRED = (WO + 5, WO2 + 3)
        E_WO2 = 6
        E_FF2 = E_WO2 + 4

        def fm_key(name, c):
            return ("fm", steps[name][c // 2], c % 2)

        @block.tensor
        def _(pe):
            n_used = [0]

            def take(b, key):
                turn[key] = (b, uses[b])
                if uses[b]:
                    pe.wait_ge(bank_free[b], uses[b])
                uses[b] += 1
                return bank[b]

            def give(ins, key):
                ins.then_inc(bank_full[turn[key][0]], 1)

            def three(dst, lh, ll, rh, rl, start, stop):
                pe.matmul(dst, lh, rh, start=start, stop=False)
                pe.matmul(dst, lh, rl, start=False, stop=False)
                return pe.matmul(dst, ll, rh, start=False, stop=stop)

            def fm_block(n, xh, xl, tokens=S, chunk_ready=None):
                wh, wlo = weights(n, (WH, WL))
                pe.wait_ge(w_lo, n + 1)
                for t in range(wh.shape[2] // P):
                    key = ("fm", n, t)
                    dst = take(t, key)[:, 0:tokens]
                    for k in range(KC):
                        if chunk_ready and t == 0:
                            chunk_ready(k)
                        last = three(dst, wh[:, k, tile_of(t)], wlo[:, k, tile_of(t)], xh[:, k, :], xl[:, k, :],
                                     k == 0, k == KC - 1)
                    give(last, key)
                b, u = turn[key]
                block_done[n] = (bank_full[b], u + 1)

            def fm_block_by_halves(n, name, done):
                wh, wlo = weights(n, (WH, WL))
                pe.wait_ge(w_lo, n + 1)
                for half in range(2):
                    for j in (2 * half, 2 * half + 1):
                        for i in range(2):
                            drained(pe, (name, j, i))
                    c = slice(half * S // 2, (half + 1) * S // 2)
                    for t in range(2):
                        key = ("fm", n, t)
                        if half == 0:
                            take(t, key)
                        for k in range(KC):
                            last = three(bank[t][:, c], wh[:, k, tile_of(t)], wlo[:, k, tile_of(t)], TH[:, k, c], TL[:, k, c],
                                         k == 0, k == KC - 1)
                        if half == 0:
                            turn_row(name, done, 2 + t)
                        else:
                            give(last, key)
                b, u = turn[key]
                block_done[n] = (bank_full[b], u + 1)

            def tm_block(n, g, groups, lhs, tiles=TT):
                wh, wlo = weights(n, (WH, WL))
                pe.wait_ge(w_lo, n + 1)
                for j in range(tiles):
                    key = ("tm", n - g, j)
                    if g == 0:
                        take(2 + j, key)
                    for kk in range(4):
                        xh, xl = lhs(kk)
                        last = three(bank[2 + j][:, :], xh[:, tile_of(j)], xl[:, tile_of(j)], wh[:, kk, :], wlo[:, kk, :],
                                     g == 0 and kk == 0, g == groups - 1 and kk == 3)
                    if g == groups - 1:
                        give(last, key)
                if g == groups - 1:
                    b, u = turn[key]
                    block_done[n] = (bank_full[b], u + 1)
                else:
                    n_used[0] += 1
                    last.then_inc(w_used, 1)
                    block_done[n] = (w_used, n_used[0])

            def tm_pair(n, groups, e, turn_one):
                w = [weights(n - 1 + b, (WH, WL)) for b in range(2)]
                x = [staged(0), staged(2)]
                n0 = n + 1 - groups
                for b, j in ((0, 0), (0, 1), (1, 0), (0, 2), (1, 1), (0, 3), (1, 2), (1, 3)):
                    g, key = groups - 2 + b, ("tm", n0, j)
                    if j == 0:
                        pe.wait_ge(w_lo, n + b)
                        pe.wait_ge(x_lo, e + b + 1)
                    if g == 0:
                        take(2 + j, key)
                    for kk in range(4):
                        xh, xl = x[b](kk)
                        last = three(bank[2 + j][:, :], xh[:, tile_of(j)], xl[:, tile_of(j)], w[b][0][:, kk, :], w[b][1][:, kk, :],
                                     g == 0 and kk == 0, b == 1 and kk == 3)
                    if b:
                        give(last, key)
                    elif j == TT - 1:
                        n_used[0] += 1
                        last.then_inc(w_used, 1)
                        block_done[n - 1] = (w_used, n_used[0])
                    if (b, j) in ((0, 3), (1, 2)) and turn_one:
                        turn_one(j - 3 if b == 0 else 1)
                b, u = turn["tm", n0, TT - 1]
                block_done[n] = (bank_full[b], u + 1)

            def staged(slot):
                h, l = quarters(XH[slot][:, :]), quarters(XL[slot][:, :])
                return lambda kk: (h[:, kk, :], l[:, kk, :])

            def resident(h, l, g):
                return lambda kk: (h[:, 4 * g + kk, :], l[:, 4 * g + kk, :])

            def turn_four(src, b, key):
                dst = take(b, key)
                for i in range(4):
                    last = pe.transpose(dst[:, tile_of(i)], src(i), IDENT[:, :])
                give(last, key)

            def turn_mem():
                pe.wait_ge(ident_in, 16)
                pe.wait_ge(mem_normed, MT)
                for c in range(KC):
                    b, key = 4 + c // 2, ("memT", c // 2)
                    if c % 2 == 0:
                        take(b, key)
                    for j in range(MT):
                        q = (c % 2) * NMEM + j * P
                        last = pe.transpose(bank[b][:, q:q + P], MEM[:, j, tile_of(c)], IDENT[:, :])
                    if c % 2:
                        give(last, key)

            def turn_x(chunks):
                for c in chunks:
                    pe.wait_ge(x_normed, TT)
                    turn_four(lambda j: XN[:, j, tile_of(c)], 4 + c % 4, ("xT", c))

            def gates():
                drained(pe, ("fm", GATES, 0))
                dst = take(6, "gates")
                for j in range(TT):
                    last = pe.transpose(dst[:, 2 * H * j:2 * H * (j + 1)], GATES_T[:, tile_of(j)], IDENT[0:2 * H, 0:2 * H])
                give(last, "gates")

            def sum_f():
                pe.wait_ge(logf_done, 1)
                pe.wait_ge(ones_set, 1)
                pe.wait_ge(tables_in, 16 * 4)
                dst = take(6, "F")
                for j in range(TT):
                    for i in range(j + 1):
                        last = pe.matmul(dst[:, H * j:H * j + H], (TRIU if i == j else ONES)[:, :], LF[:, i, :],
                                         start=i == 0, stop=i == j)
                give(last, "F")

            def g_rows():
                pe.wait_ge(g_done, 1)
                dst = take(7, "g_rows")
                for j in range(TT):
                    last = pe.transpose(dst[0:H, tile_of(j)], GG[:, j, :], IDENT[:, :])
                give(last, "g_rows")

            def m_all(h, b):
                pe.wait_ge(m_done, 1)
                dst = take(b, ("m_all", h))
                give(pe.matmul(dst[:, :], NSEL[:, h, :], MROW[:, :], start=True, stop=True), ("m_all", h))

            def m_columns():
                dst = take(7, "m_columns")
                for j in range(TT):
                    last = pe.transpose(dst[:, H * j:H * j + H], MROW[:, tile_of(j)], IDENT[0:H, 0:H])
                give(last, "m_columns")

            def mlstm_scores(h):
                pe.wait_ge(qk_done, 8)
                for i, b, c0 in ((0, 2, 0), (1, 3, 0), (3, 3, 384), (2, 4, 0)):
                    key = ("ms", h, b)
                    if i != 3:
                        take(b, key)
                    last = pe.matmul(bank[b][:, c0:c0 + S - i * P], QK[:, 4 + h, tile_of(i)], QK[:, h, i * P:S],
                                     start=True, stop=True)
                    if i != 1:
                        give(last, key)

            def mlstm_sums(h):
                for b in (2, 3, 4):
                    drained(pe, ("ms", h, b))
                if h == 0:
                    for j in range(TT):
                        drained(pe, ("tm", first["v"], j))
                pe.wait_ge(ones_set, 2)
                for j in range(TT):
                    key, c = ("num", h, j // 2), j % 2 * (P + 1)
                    if j % 2 == 0:
                        dst = take(5 + j // 2, key)
                    for i in range(j + 1):
                        w = ML_OFF[i] + (j - i) * P
                        last = pe.matmul(dst[:, c:c + P + 1], PP[h % 2][:, w:w + P], V[:, i, h, :], start=i == 0, stop=i == j)
                    if j % 2:
                        give(last, key)

            def mlstm_turn(h):
                pe.wait_ge(ml_h, h + 1)
                turn_four(lambda j: HM[h % 2][:, j, :], 7, ("hT", h))

            def mem_scores(j):
                if j == 0:
                    for c in range(H):
                        drained(pe, fm_key("qc", c))
                        drained(pe, fm_key("km", c))
                for i in range(2):
                    dst = take(2 + i, ("cs", j, i))
                    for h in (2 * i, 2 * i + 1):
                        q = (h % 2) * NMEM
                        last = pe.matmul(dst[:, q:q + NMEM], QC[:, h, tile_of(j)], KM[:, h, :], start=True, stop=True)
                    give(last, ("cs", j, i))

            def probs_turn(j):
                pe.wait_ge(probs_done, j + 1)
                for i in range(2):
                    turn_four(lambda q: PROB[j % 2][:, 2 * i + q // 2, tile_of(q % 2)], 4 + i, ("pT", j, i))

            def mem_values(j):
                for i in range(2):
                    drained(pe, ("pT", j, i))
                    drained(pe, ("tm", first["vm"], i))
                dst = take(6, ("yc", j))
                for h in range(H):
                    for m in range(MT):
                        last = pe.matmul(dst[:, tile_of(h)], VM[:, m, tile_of(h)], PT[j % 2][:, 2 * h + m, :],
                                         start=m == 0, stop=m == MT - 1)
                give(last, ("yc", j))

            def pool_mix():
                pe.wait_ge(poolw_in, 16)
                for g in range(4):
                    pe.wait_ge(pooled, g + 1)
                    dst = take(2 + g, ("pool", g))
                    give(pe.matmul(dst[:, :], POOLW[:, g, :], UP[:, g, PAD:PAD + S], start=True, stop=True), ("pool", g))

            def gate_logits():
                drained(pe, ("fm", first["low"], 0))
                pe.wait_ge(wg2_in, 32)
                for j in range(TT):
                    dst = take(2 + j, ("lg", j))
                    give(pe.matmul(dst[:, :], ALT[0:17, tile_of(j)], WG2[:, :], start=True, stop=True), ("lg", j))

            def cum_sums():
                for j in range(TT):
                    drained(pe, ("lg", j))
                for h in range(H):
                    dst = take(2 + h, ("cum", h))
                    for j in range(TT):
                        last = pe.matmul(dst[:, tile_of(j)], LF2[:, j, tile_of(h)], TRI16[:, :], start=True, stop=True)
                    give(last, ("cum", h))

            def gla_pairs(level, half):
                if level >= 0:
                    pe.wait_ge(lv_qk, 2 * (level + 1))
                elif half == 0:
                    for c in range(H):
                        drained(pe, fm_key("q2", c))
                        drained(pe, fm_key("k2", c))
                if level < 0:
                    for h in (2 * half, 2 * half + 1):
                        dst = take(6 + h % 2, ("lv", level, h))
                        for j in range(TT):
                            c = slice(h * S + j * P, h * S + j * P + P)
                            last = pe.matmul(dst[:, tile_of(j)], K2[:, c], Q2[:, c], start=True, stop=True)
                        give(last, ("lv", level, h))
                    return
                dst = take(6 + half, ("lv", level, half))
                for i in range(2 * TT):
                    c = half * 2 * TT + i
                    last = pe.matmul(dst[:, i * P // 2:(i + 1) * P // 2], KE[:, c * P:c * P + P], QEC[:, c * P // 2:(c + 1) * P // 2],
                                     start=True, stop=True)
                give(last, ("lv", level, half))

            def kdec_turn():
                pe.wait_ge(kd_done, 1)
                for h in range(H):
                    turn_four(lambda j: KE[:, h * S + j * P:h * S + j * P + P], 2 + h, ("kdT", h))

            def gla_out(j):
                if j == 0:
                    for h in range(H):
                        drained(pe, ("lv", LEVELS - 1, h // 2))
                        drained(pe, ("kdT", h))
                        for half in range(2):
                            drained(pe, ("tm", first["v2"] + 2 * half, h))
                    pe.wait_ge(qcum_done, 1)
                else:
                    drained(pe, ("kv", j - 1, 0))
                    drained(pe, ("kv", j - 1, 1))
                for i in range(2):
                    dst = take(2 + i, ("o2", j, i))
                    for h in (2 * i, 2 * i + 1):
                        c, v = slice((h % 2) * DV, (h % 2 + 1) * DV), slice(h * DV, h * DV + DV)
                        last = pe.matmul(dst[:, c], SC[:, h * TT + j, :], V2[:, j, v], start=True, stop=j == 0)
                        if j:
                            last = pe.matmul(dst[:, c], QE[:, h * S + j * P:h * S + j * P + P], STATE[:, h, :],
                                             start=False, stop=True)
                    give(last, ("o2", j, i))
                if j < TT - 1:
                    for i in range(2):
                        dst = take(4 + i, ("kv", j, i))
                        for h in (2 * i, 2 * i + 1):
                            c, v = slice((h % 2) * DV, (h % 2 + 1) * DV), slice(h * DV, h * DV + DV)
                            last = pe.matmul(dst[:, c], KDT[:, h, j, :], V2[:, j, v], start=True, stop=True)
                        give(last, ("kv", j, i))

            def gla_turn(j):
                for i in range(2):
                    drained(pe, ("o2", j, i))
                for i in range(2):
                    turn_four(lambda c: OJ[:, tile_of(4 * i + c)], 6 + i, ("oT", j, i))

            def ws_turn():
                pe.wait_ge(ws_in, 16)
                for i in range(2):
                    turn_four(lambda g: WSR[:, 4 * i + g, :], i, ("wsT", i))

            def sg_mix(i):
                if i == 0:
                    pe.wait_ge(vh_ready, TT)
                    drained(pe, ("wsT", 0))
                    drained(pe, ("wsT", 1))
                for g in (2 * i, 2 * i + 1):
                    dst = take(2 + g % 2, ("sg", g))
                    for j in range(TT):
                        last = pe.matmul(dst[:, tile_of(j)], VH[:, j, tile_of(g)], WST[:, g, :], start=True, stop=True)
                    give(last, ("sg", g))

            def turn_row(name, done, j):
                pe.wait_ge(done, j + 1)
                for i in range(2):
                    turn_four(lambda c: RES[:, j, tile_of(4 * i + c)], 6 + i, (name, j, i))

            def side(n):
                turn_x(TURN_X.get(n, ()))
                if n == GATES + 1: gates()
                if n == GATES + 2: sum_f()
                if n == GATES + 3: g_rows()
                if n == GATES + 4: m_all(0, 6); m_columns()
                if n == GATES + 5: m_all(1, 6); m_all(2, 7)
                if n == GATES + 6: m_all(3, 6)
                if 0 <= n - ML < H: mlstm_scores(n - ML)
                if 0 <= n - ML - 1 < H: mlstm_sums(n - ML - 1)
                if 0 <= n - ML - 2 < H: mlstm_turn(n - ML - 2)
                if 0 <= n - AT - 2 < TT: mem_values(n - AT - 2)
                if 0 <= n - AT - 1 < TT: probs_turn(n - AT - 1)
                if 0 <= n - AT < TT: mem_scores(n - AT)
                if n == WO - 1: pool_mix()
                if n == LG: gate_logits()
                if n == LG + 2: cum_sums()
                if n == LV + 4: ws_turn()
                if 0 <= n - LV < 2 * (LEVELS + 1): gla_pairs((n - LV) // 2 - 1, (n - LV) % 2)
                if 0 <= n - SG < 4: sg_mix(n - SG)
                if n == GO - 1: kdec_turn()
                if 0 <= n - GO - 1 < TT: gla_turn(n - GO - 1)
                if 0 <= n - GO < TT: gla_out(n - GO)

            turn_mem()
            for n in range(ff1_0):
                name, i = name_of(n)
                side(n)
                if n + 1 in PAIRED:
                    pass
                elif n == WO + 5:
                    tm_pair(n, 3, 4, lambda j: turn_row("x1T", x1_done, j))
                elif n == WO2 + 3:
                    tm_pair(n, 2, E_WO2 + 2, lambda j: turn_row("h1T", h1_done, j))
                elif n == WO + 6:
                    fm_block_by_halves(n, "x1T", x1_done)
                elif name == "km":
                    fm_block(n, MEMH, MEML, NMEM, (lambda k: drained(pe, ("memT", k // 2))) if i == 0 else None)
                elif name == "vm":
                    tm_block(n, i, 2, resident(MEMH, MEML, i), MT)
                elif name in ("w_out", "w_out2"):
                    g = len(WO_GROUPS) if name == "w_out" else 2
                    pe.wait_ge(x_lo, i + 1 + (0 if name == "w_out" else E_WO2))
                    tm_block(n, i % g, g, staged(i % 2))
                elif blocks[n][0] == "tm":
                    tm_block(n, i % 2, 2, resident(TH, TL, i % 2))
                else:
                    fm_block(n, TH, TL, S, (lambda k: drained(pe, ("xT", k))) if n == GATES else None)

            fm_block_by_halves(ff1_0, "h1T", h1_done)
            fm_block(ff1_0 + 1, TH, TL)
            u0 = list(uses)
            with pe.Fori(0, 7) as i:
                for b in range(2):
                    n = ff1_0 + 2 + b
                    wh, wlo = weights(n, (WH, WL))
                    pe.wait_ge(w_lo, i * 2 + (n + 1))
                    for t in range(2):
                        pe.wait_ge(bank_free[t], i * 2 + (u0[t] + b))
                        for k in range(KC):
                            last = three(bank[t][:, :], wh[:, k, tile_of(t)], wlo[:, k, tile_of(t)], TH[:, k, :], TL[:, k, :],
                                         k == 0, k == KC - 1)
                        last.then_inc(bank_full[t], 1)
            for n in range(14):
                for t in range(2):
                    turn["fm", ff1_0 + 2 + n, t] = (t, u0[t] + n)
                block_done[ff1_0 + 2 + n] = (bank_full[1], u0[1] + n + 1)
            uses[0] += 14
            uses[1] += 14

            for half in range(2):
                n0, e0, used0 = ff2_0 + 8 * half, E_FF2 + 8 * half, n_used[0]

                def group(g, more=0):
                    wh, wlo = weights(n0 + g, (WH, WL))
                    lhs = staged(g % 2)
                    pe.wait_ge(w_lo, more + (n0 + g + 1))
                    pe.wait_ge(x_lo, more + (e0 + g + 1))
                    for j in range(TT):
                        key = ("tm", n0, j)
                        if g == 0:
                            take(2 + j, key)
                        for kk in range(4):
                            h, l = lhs(kk)
                            last = three(bank[2 + j][:, :], h[:, tile_of(j)], l[:, tile_of(j)], wh[:, kk, :], wlo[:, kk, :],
                                         g == 0 and kk == 0, g == 7 and kk == 3)
                        if g == 7:
                            give(last, key)
                    if g < 7:
                        last.then_inc(w_used, 1)

                group(0)
                group(1)
                with pe.Fori(0, 2) as i:
                    group(2, i * 2)
                    group(3, i * 2)
                for g in range(7):
                    block_done[n0 + g] = (w_used, used0 + g + 1)
                if half == 0:
                    group(6)
                    group(7)
                    n_used[0] += 7
                    block_done[n0 + 7] = (bank_full[5], turn["tm", n0, 3][1] + 1)
                else:
                    n_used[0] += 6
                    tm_pair(n0 + 7, 8, e0 + 6, None)

        f0 = [turn["fm", ff1_0, t][1] for t in range(2)]

        @block.scalar
        def _(act):
            links = [0]

            def link(ins):
                links[0] += 1
                ins.then_inc(act_chain, 1)
                act.wait_ge(act_chain, links[0])

            def split(n, loads=0, more=0):
                w = blocks[n][2].shape[1] * blocks[n][2].shape[2]
                act.wait_ge(w_loaded[n % 2], loads + 16 * (n // 2 + 1))
                if n >= 2 and slot_of(n) != 2:
                    s, v = block_done[n - 2]
                    act.wait_ge(s, more + v)
                act.activation(WH[slot_of(n)][:, 0:w], RAW[n % 2][:, 0:w], ACT.Copy).then_inc(w_hi, 1)

            def split_x(slot, src):
                act.activation(XH[slot][:, :], src, ACT.Copy).then_inc(x_hi, 1)

            def load_constants():
                act.dma_start(IDENT[:, :], a["c_ident"]).then_inc(ident_in, 16)
                act.dma_start(VC[:, :], a["vector_columns"]).then_inc(columns_in, 16)

            def mean_squares(dst, src, c, before=0):
                if before:
                    act.wait_ge(squared, before)
                act.activation(dst, src, ACT.Square, scale=1 / 32, accum_out=SSQ[:, c:c + 1]).then_inc(squared, 1)

            def gates_softplus():
                drained(act, "gates")
                link(act.activation(GT1[:, :, :], G8[:, :, H:2 * H], ACT.Abs))
                link(act.activation(GT1[:, :, :], GT1[:, :, :], ACT.Exp, scale=-1.0))
                act.activation(GT1[:, :, :], GT1[:, :, :], ACT.Ln, bias=1.0).then_inc(softplus_done, 1)

            def copy_m(h):
                b = full(act, ("m_all", h))
                free(act.activation(MB[:, h, :], b[:, :], ACT.Copy), ("m_all", h))

            def den_floor():
                drained(act, "m_columns")
                act.activation(FLOOR[:, :, :], FLOOR[:, :, :], ACT.Exp, scale=-1.0).then_inc(floor_done, 1)

            def mlstm_exp(h):
                act.wait_ge(ml_arg, h + 1)
                act.activation(PP[h % 2][:, :], PP[h % 2][:, :], ACT.Exp).then_inc(ml_exp, 1)

            def softmax_exp(j):
                act.wait_ge(max_done, j + 1)
                for h in range(H):
                    b = full(act, ("cs", j, h // 2))
                    ins = act.activation(PROB[j % 2][:, h, :], b[:, (h % 2) * NMEM:(h % 2 + 1) * NMEM], ACT.Exp,
                                         bias=SMX[:, h:h + 1], scale=SCALE, accum_out=SSUM[:, h:h + 1])
                    if h % 2:
                        free(ins, ("cs", j, h // 2))

            def probs_copy(j):
                for i in range(2):
                    b = full(act, ("pT", j, i))
                    free(act.activation(PT[j % 2][:, 4 * i:4 * i + 4, :], quarters(b[:, :]), ACT.Copy), ("pT", j, i))

            def logits_softplus():
                for f, kw in ((ACT.Abs, {}), (ACT.Exp, {"scale": -1.0}), (ACT.Ln, {"bias": 1.0})):
                    for j in range(TT):
                        b = full(act, ("lg", j))
                        if f == ACT.Abs:
                            act.wait_ge(lg_min, j + 1)
                        ins = act.activation(b[:, :], b[:, :], f, **kw)
                        if f == ACT.Ln:
                            ins.then_inc(lg_softplus, 1)
                    if f != ACT.Ln:
                        link(ins)

            def copy_cum():
                for h in range(H):
                    b = full(act, ("cum", h))
                    free(act.activation(CUM[:, h * S:h * S + S], b[:, :], ACT.Copy), ("cum", h))

            def level_exp(l):
                act.wait_ge(lv_arg, 2 * (l + 1))
                act.activation(EE[:, :], EE[:, :], ACT.Exp).then_inc(lv_exp, 1)

            def squares_o(j):
                if j:
                    full(act, ("oT", j - 1, 1))
                for h in range(H):
                    b = full(act, ("o2", j, h // 2))
                    act.activation(OJ[:, h * DV:h * DV + DV], b[:, (h % 2) * DV:(h % 2 + 1) * DV], ACT.Square,
                                   scale=1 / 16, accum_out=SSQ[:, 10 + h:11 + h]).then_inc(squared, 1)

            def rows_hi(name, j):
                for i in range(2):
                    b = full(act, (name, j, i))
                    act.activation(TH[:, 4 * i:4 * i + 4, tile_of(j)], quarters(b[:, :]), ACT.Copy).then_inc(t_hi, 1)

            def side(n):
                if n == 0:
                    for j in range(TT):
                        act.wait_ge(x_in[j], 16)
                        mean_squares(XN[:, j, :], RES[:, j, :], MT + j)
                for c in TURN_X.get(n, ()):
                    b = full(act, ("xT", c))
                    act.activation(TH[:, c, :], b[:, :], ACT.Copy, scale=col(C_NORM + c)).then_inc(t_hi, 1)
                if n == GATES + 1: gates_softplus()
                if n == GATES + 4: copy_m(0)
                if n == GATES + 5: copy_m(1); copy_m(2); den_floor()
                if n == GATES + 6: copy_m(3)
                if 0 <= n - ML < H: mlstm_exp(n - ML)
                if 0 <= n - AT - 1 < TT: probs_copy(n - AT - 1)
                if 0 <= n - AT < TT: softmax_exp(n - AT)
                if n == LG: logits_softplus()
                if n == LG + 2: copy_cum()
                if 0 <= n - LV < 2 * LEVELS and (n - LV) % 2 == 0: level_exp((n - LV) // 2)
                if n == GO - 3:
                    act.wait_ge(lv_qk, 2 * LEVELS)
                    act.activation(ETOT[:, :], CUM[:, :].rearrange("p (c t) -> p c t", t=P)[:, :, P - 1], ACT.Exp).then_inc(etot_done, 1)
                    act.activation(EE[:, :], CUM[:, :], ACT.Exp).then_inc(qc_exp, 1)
                if n == GO - 2:
                    act.wait_ge(kd_arg, 1)
                    act.activation(EE[:, :], EE[:, :], ACT.Exp).then_inc(kd_exp, 1)
                if n == GO - 1:
                    act.wait_ge(kd_done, 1)
                    for h in range(H):
                        b = full(act, ("kdT", h))
                        free(act.activation(KDT[:, h, :, :], quarters(b[:, :]), ACT.Copy), ("kdT", h))
                if 0 <= n - GO < TT: squares_o(n - GO)

            def drain(n):
                name, i = name_of(n)
                fm = [(("fm", n, t), 2 * i + t) for t in range(2)]
                if name == "km":
                    for key, c in fm:
                        b = full(act, key)
                        free(act.activation(KM[:, c, :], b[:, 0:NMEM], ACT.Copy), key)
                if name in ("vm", "v", "o") and i == 1:
                    dst, f = {"vm": (VM, ACT.Copy), "v": (V, ACT.Copy), "o": (O, ACT.Sigmoid)}[name]
                    for j in range(MT if name == "vm" else TT):
                        b = full(act, ("tm", n - 1, j))
                        to, src = (dst[:, j, :, 0:P], quarters(b[:, :])) if name == "v" else (dst[:, j, :], b[:, :])
                        free(act.activation(to, src, f), ("tm", n - 1, j))
                if name in ("q", "k"):
                    c0 = 4 if name == "k" else 0
                    for key, c in fm:
                        b = full(act, key)
                        act.activation(QK[:, c0 + c, :], b[:, :], ACT.Identity, bias=col(C_CB + c0 + c),
                                       scale=col(C_CW + 24 + c0 + c)).then_inc(conv_first, 1)
                    for key, c in fm:
                        drained(act, key)
                        act.activation(QK[:, c0 + c, :], QK[:, c0 + c, :], ACT.Silu).then_inc(qk_done, 1)
                to = {"qc": lambda c: QC[:, c, :], "u": lambda c: UP[:, c, PAD:PAD + S], "z_a": lambda c: Y[:, c, :],
                      "z_b": lambda c: Y[:, 4 + c, :], "z_c": lambda c: Y[:, 8 + c, :]}.get(name)
                if to:
                    for key, c in fm:
                        b = full(act, key)
                        free(act.activation(to(c), b[:, :], ACT.Silu if name[0] == "z" else ACT.Copy), key)
                if name == "w_out" and i == 5:
                    def squares(j):
                        drained(act, ("tm", n - 2, j))
                        mean_squares(SINK[:, :], RES[:, j, :], 6 + j, MT + TT + j)

                    squares(0)
                    squares(1)
                    rows_hi("x1T", 0)
                    squares(2)
                    rows_hi("x1T", 1)
                    squares(3)
                    rows_hi("x1T", 2)
                    rows_hi("x1T", 3)
                if name == "a_v" and i % 2:
                    h = slice(i // 2 * 512, i // 2 * 512 + 512)
                    for j in range(TT):
                        drained(act, ("tm", n - 1, j))
                        act.activation(VH[:, j, h], VH[:, j, h], ACT.Gelu_apprx_tanh).then_inc(av_gelu, 1)
                if name in ("a_u", "g_a", "r", "g_b"):
                    for key, c in fm:
                        b = full(act, key)
                        if name == "a_u":
                            free(act.activation(U[:, c, :], b[:, :], ACT.Gelu_apprx_tanh, bias=col(C_B2 + c)), key)
                        if name == "g_a":
                            act.activation(b[:, :], b[:, :], ACT.Sigmoid, bias=col(C_B2G + c)).then_inc(ga_sig, 1)
                        if name == "r":
                            if c == 0:
                                full(act, ("sg", 7))
                            free(act.activation(R[:, c, :], b[:, :], ACT.Silu, bias=col(C_B2 + 32 + c)), key)
                        if name == "g_b":
                            act.activation(b[:, :], b[:, :], ACT.Sigmoid, bias=col(C_B2G + 8 + c)).then_inc(gb_sig, 1)
                if name == "w_out2" and i == 3:
                    for j in range(TT):
                        rows_hi("h1T", j)

            def stage(n):
                if n + 1 >= ff1_0:
                    return
                name, i = name_of(n + 1)
                if name == "w_out":
                    if i == 0: drained(act, ("hT", H - 1))
                    if i == 1: drained(act, ("yc", TT - 1))
                    if i == 2: act.wait_ge(yb_done, 4)
                    g, src = WO_GROUPS[i % 3], Y
                elif name == "w_out2":
                    act.wait_ge(m_ready, 4 if i == 0 else 8)
                    g, src = i % 2, R
                else:
                    return
                slot = 2 if n + 1 in PAIRED else i % 2
                if i >= 2 and slot != 2:
                    act.wait_ge(*block_done[n - 1])
                if slot == 2:
                    act.wait_ge(x_lo, i + (0 if name == "w_out" else E_WO2))
                split_x(slot, src[:, 4 * g:4 * g + 4, :].rearrange("p a b -> p (a b)"))

            load_constants()
            act.wait_ge(ones_set, 1)
            act.activation(SSUM[:, 0:1], ONES[:, 0:1], ACT.Square)
            for j in range(MT):
                act.wait_ge(mem_in[j], 16)
                mean_squares(SINK[:, :], MEM[:, j, :], j, j)
            split(0)
            act.wait_ge(columns_in, 16)
            for c in range(KC):
                full(act, ("memT", c // 2))
                q = (c % 2) * NMEM
                act.activation(MEMH[:, c, :], bank[4 + c // 2][:, q:q + NMEM], ACT.Copy, scale=col(C_MEMN + c)).then_inc(t_hi, 1)
            for n in range(ff1_0):
                if n + 1 in PAIRED:
                    stage(n)
                split(n + 1)
                side(n)
                if n + 1 not in PAIRED:
                    stage(n)
                drain(n)

            def relus(m, group, more=0):
                for t in range(2):
                    act.wait_ge(bank_full[t], more + (f0[t] + m + 1))
                    q = (2 * m + t) % 4 * S
                    act.activation(F1[:, group, q:q + S], bank[t][:, :], ACT.Relu).then_inc(bank_free[t], 1)

            split(ff1_0 + 1)
            relus(0, 0)
            with act.Fori(0, 7) as i:
                split(ff1_0 + 2, i * 16, i * 2)
                relus(1, i, i * 2)
                split(ff1_0 + 3, i * 16, i * 2)
                relus(2, i + 1, i * 2)
            split(ff2_0)
            act.wait_ge(f1_done, 4)
            act.wait_ge(*block_done[WO2 + 2])
            split_x(0, F1[:, 0, :])
            relus(15, 7)

            act.wait_ge(f1_done, 32)
            for half in range(2):
                n0 = ff2_0 + 8 * half
                for g in (1, 2):
                    split(n0 + g)
                    if n0 + g == ff2_0 + 1:
                        act.wait_ge(*block_done[WO2 + 3])
                    split_x(g % 2, F1[:, g, :])
                with act.Fori(0, 2) as i:
                    for g in (3, 4):
                        split(n0 + g, i * 16, i * 2)
                        split_x(g % 2, F1[:, i * 2 + g, :])
                if half == 0:
                    split(n0 + 7)
                    split_x(1, F1[:, 7, :])
                    split(n0 + 8)
                    split_x(0, F1[:, 0, :])
                else:
                    act.wait_ge(x_lo, E_FF2 + 15)
                    split_x(2, F1[:, 7, :])
                    split(n0 + 7)

        @block.vector
        def _(dve):
            links = [0]

            def link(ins):
                links[0] += 1
                ins.then_inc(dve_chain, 1)
                dve.wait_ge(dve_chain, links[0])

            def lower(dst, src, hi):
                return dve.tensor_tensor(dst, src, hi.bitcast(f32), ALU.subtract)

            def split(n, more=0):
                w = blocks[n][2].shape[1] * blocks[n][2].shape[2]
                dve.wait_ge(w_hi, more + (n + 1))
                lower(WL[slot_of(n)][:, 0:w], RAW[n % 2][:, 0:w], WH[slot_of(n)][:, 0:w]).then_inc(w_lo, 1)

            def split_x(slot, e, src, more=0):
                dve.wait_ge(x_hi, more + (e + 1))
                lower(XL[slot][:, :], src, XH[slot][:, :]).then_inc(x_lo, 1)

            def gates_logf():
                b = full(dve, "gates")
                free(dve.tensor_copy(G8[:, :, :], b[:, 0:TT * 2 * H].rearrange("p (a b) -> p a b", a=TT)), "gates")
                drained(dve, "gates")
                link(dve.tensor_scalar(LF[:, :, :], G8[:, :, H:2 * H], 0.0, None, ALU.min))
                dve.wait_ge(softplus_done, 1)
                dve.tensor_tensor(LF[:, :, :], LF[:, :, :], GT1[:, :, :], ALU.subtract).then_inc(logf_done, 1)

            def gates_g():
                b = full(dve, "F")
                free(dve.tensor_copy(FS[:, :, :], b[:, 0:TT * H].rearrange("p (a b) -> p a b", a=TT)), "F")
                drained(dve, "F")
                dve.tensor_tensor(GG[:, :, :], G8[:, :, 0:H], FS[:, :, :], ALU.subtract).then_inc(g_done, 1)

            def running_max():
                b = full(dve, "g_rows")
                free(dve.tensor_copy(GROW[:, :], b[0:H, :]), "g_rows")
                drained(dve, "g_rows")
                dve.tensor_tensor_scan(MROW[:, :], GROW[:, :], GROW[:, :], 0.0, ALU.max, ALU.max).then_inc(m_done, 1)

            def m_sum():
                b = full(dve, "m_columns")
                free(dve.tensor_tensor(FLOOR[:, :, :], FS[:, :, :], b[:, 0:TT * H].rearrange("p (a b) -> p a b", a=TT),
                                       ALU.add), "m_columns")

            def conv_taps(c, key):
                dve.wait_ge(conv_first, c + 1)
                b = full(dve, key)
                for back in (1, 2, 3):
                    ins = dve.scalar_tensor_tensor(QK[:, c, back:S], b[:, 0:S - back], col(C_CW + 8 * (3 - back) + c),
                                                   QK[:, c, back:S], ALU.mult, ALU.add)
                    if back < 3:
                        link(ins)
                free(ins, key)

            def mlstm_weights(h):
                p = PP[h % 2]
                drained(dve, ("m_all", h))
                for i in range(TT):
                    w = S - i * P
                    ins = dve.tensor_scalar(p[:, ML_OFF[i]:ML_OFF[i] + w], MB[:, h, i * P:S], GG[:, i, h:h + 1], 0.0,
                                            ALU.add, ALU.min)
                ins.then_inc(ml_arg, 1)
                dve.wait_ge(ml_exp, h + 1)
                for i in range(TT):
                    c = slice(ML_OFF[i], ML_OFF[i] + P)
                    ins = dve.tensor_tensor(p[:, c], p[:, c], TRIU[:, :], ALU.mult)
                link(ins)
                for i, b, c0 in ((0, 2, 0), (1, 3, 0), (3, 3, 384), (2, 4, 0)):
                    full(dve, ("ms", h, b))
                    w = S - i * P
                    c = slice(ML_OFF[i], ML_OFF[i] + w)
                    ins = dve.scalar_tensor_tensor(p[:, c], bank[b][:, c0:c0 + w], SCALE, p[:, c], ALU.mult, ALU.mult)
                    if i != 1:
                        free(ins, ("ms", h, b))

            def mlstm_out(h):
                hm = HM[h % 2]
                if h == 0:
                    dve.wait_ge(floor_done, 1)
                    for j in range(TT):
                        drained(dve, ("tm", first["o"], j))
                sums = [full(dve, ("num", h, i))[:, 0:2 * (P + 1)].rearrange("p (a b) -> p a b", a=2) for i in range(2)]
                for i in range(2):
                    ins = dve.tensor_scalar(RDEN[:, 2 * i:2 * i + 2], sums[i][:, :, P], -1.0, None, ALU.mult)
                link(ins)
                for i in range(2):
                    ins = dve.tensor_tensor(RDEN[:, 2 * i:2 * i + 2], sums[i][:, :, P], RDEN[:, 2 * i:2 * i + 2], ALU.max)
                link(ins)
                link(dve.tensor_tensor(RDEN[:, :], RDEN[:, :], FLOOR[:, :, h], ALU.max))
                link(dve.reciprocal(RDEN[:, :], RDEN[:, :]))
                for i in range(2):
                    free(dve.tensor_tensor(hm[:, 2 * i:2 * i + 2, :], sums[i][:, :, 0:P],
                                           RDEN[:, 2 * i:2 * i + 2].unsqueeze(2).to_broadcast([P, 2, P]), ALU.mult), ("num", h, i))
                drained(dve, ("num", h, 0))
                drained(dve, ("num", h, 1))
                link(dve.tensor_tensor(hm[:, :, :], hm[:, :, :], O[:, :, tile_of(h)], ALU.mult))
                link(dve.tensor_tensor(SQ[:, :, :], hm[:, :, :], hm[:, :, :], ALU.mult))
                dve.tensor_reduce(SSQ[:, 10:14], SQ[:, :, :], AX.X, ALU.add).then_inc(ml_ss, 1)
                dve.wait_ge(rstd_done, MT + TT + h + 1)
                dve.tensor_tensor(hm[:, :, :], hm[:, :, :], RST[:, 10:14].unsqueeze(2).to_broadcast([P, TT, P]),
                                  ALU.mult).then_inc(ml_h, 1)

            def mlstm_y(h):
                b = full(dve, ("hT", h))
                drained(dve, fm_key("z_a", h))
                free(dve.scalar_tensor_tensor(Y[:, h, :], b[:, :], col(C_MN + h), Y[:, h, :], ALU.mult, ALU.mult), ("hT", h))

            def softmax(j):
                for i in range(2):
                    b = full(dve, ("cs", j, i))
                    ins = dve.tensor_reduce(SMX[:, 2 * i:2 * i + 2], b[:, :].rearrange("p (a b) -> p a b", a=2), AX.X,
                                            ALU.max, negate=True)
                link(ins)
                dve.tensor_scalar(SMX[:, :], SMX[:, :], SCALE, None, ALU.mult).then_inc(max_done, 1)
                drained(dve, ("cs", j, 0))
                drained(dve, ("cs", j, 1))
                link(dve.reciprocal(SSUM[:, :], SSUM[:, :]))
                dve.tensor_tensor(PROB[j % 2][:, :, :], PROB[j % 2][:, :, :],
                                  SSUM[:, :].unsqueeze(2).to_broadcast([P, H, NMEM]), ALU.mult).then_inc(probs_done, 1)

            def mem_y(j):
                if j == 0:
                    for c in range(H):
                        drained(dve, fm_key("z_c", c))
                b = full(dve, ("yc", j))
                y = Y[:, 8:12, tile_of(j)]
                free(dve.tensor_tensor(y, quarters(b[:, :]), y, ALU.mult), ("yc", j))

            def pool_window(g):
                drained(dve, fm_key("u", g))
                if g:
                    dve.wait_ge(pooled, g)
                src, w = UP[:, g, :], 1
                while w < WINDOWS[g]:
                    dst = PW[w.bit_length() % 2][:, :]
                    link(dve.tensor_tensor(dst[:, PAD:], src[:, PAD:], src[:, PAD - w:PAD + S - w], ALU.add))
                    src, w = dst, 2 * w
                edge, rest = slice(PAD, PAD + 16), slice(PAD + 16, PAD + S)
                link(dve.tensor_tensor(src[:, edge], src[:, edge], PINV[:, g, :], ALU.mult))
                link(dve.tensor_tensor(UP[:, g, edge], src[:, edge], UP[:, g, edge], ALU.subtract))
                dve.scalar_tensor_tensor(UP[:, g, rest], src[:, rest], 1 / w, UP[:, g, rest], ALU.mult,
                                         ALU.subtract).then_inc(pooled, 1)

            def pool_scaled():
                for g in range(4):
                    b = full(dve, ("pool", g))
                    free(dve.tensor_scalar(UP[:, g, PAD:PAD + S], b[:, :], col(C_PS + g), None, ALU.mult), ("pool", g))

            def pool_y():
                for g in range(4):
                    drained(dve, ("pool", g))
                    drained(dve, fm_key("z_b", g))
                    dve.tensor_tensor(Y[:, 4 + g, :], Y[:, 4 + g, :], UP[:, g, PAD:PAD + S], ALU.mult).then_inc(yb_done, 1)

            def logits_logf():
                for j in range(TT):
                    b = full(dve, ("lg", j))
                    dve.tensor_scalar(LF2[:, j, :], b[:, :], 0.0, None, ALU.min).then_inc(lg_min, 1)
                for j in range(TT):
                    dve.wait_ge(lg_softplus, j + 1)
                    free(dve.tensor_tensor(LF2[:, j, :], LF2[:, j, :], bank[turn["lg", j][0]][:, :], ALU.subtract), ("lg", j))

            def level_views(l):
                half = P >> (l + 1)
                return half, slice(0, half), slice(half, 2 * half), lambda t: t[:, :].rearrange("p (b t) -> p b t", t=2 * half)

            def level_args(l):
                half, left, right, view = level_views(l)
                cum, ee = view(CUM), view(EE)
                mid = cum[:, :, half - 1:half].to_broadcast([P, H * S // (2 * half), half])
                if l == 0:
                    for h in range(H):
                        drained(dve, ("cum", h))
                else:
                    dve.wait_ge(lv_qk, 2 * l)
                dve.tensor_tensor(ee[:, :, right], cum[:, :, right], mid, ALU.subtract).then_inc(lv_arg, 1)
                dve.tensor_tensor(ee[:, :, left], mid, cum[:, :, left], ALU.subtract).then_inc(lv_arg, 1)

            def level_operands(l):
                half, left, right, view = level_views(l)
                if l == 0:
                    dve.wait_ge(zeros_set, 2)
                dve.wait_ge(lv_exp, l + 1)
                dve.tensor_tensor(QEC[:, :].rearrange("p (b t) -> p b t", t=half), view(Q2)[:, :, right], view(EE)[:, :, right],
                                  ALU.mult).then_inc(lv_qk, 1)
                dve.tensor_tensor(view(KE)[:, :, left], view(K2)[:, :, left], view(EE)[:, :, left], ALU.mult).then_inc(lv_qk, 1)

            def level_merge(l, pair):
                if l < 0:
                    dve.wait_ge(masks_set, 1)
                    dve.wait_ge(zeros_set, 2)
                    mask = MASK[:, LEVELS, :].unsqueeze(1).to_broadcast([P, TT, P])
                    for h in (2 * pair, 2 * pair + 1):
                        b = full(dve, ("lv", l, h))
                        free(dve.copy_predicated(SC[:, h * TT:h * TT + TT, :], mask, quarters(b[:, :])), ("lv", l, h))
                    return
                half, left, right, view = level_views(l)
                nb = P // (2 * half)
                b = full(dve, ("lv", l, pair))
                to = SC[:, 2 * TT * pair:2 * TT * (pair + 1), :].rearrange("p c (b t) -> p c b t", t=2 * half)[:, :, :, right]
                mask = MASK[:, l, :].rearrange("p (b t) -> p b t", t=2 * half)[:, :, right]
                free(dve.copy_predicated(to, mask.unsqueeze(1).to_broadcast([P, 2 * TT, nb, half]),
                                         b[:, :].rearrange("p (c b t) -> p c b t", c=2 * TT, t=half)), ("lv", l, pair))

            def q_cum():
                dve.wait_ge(qc_exp, 1)
                dve.tensor_tensor(QE[:, :], Q2[:, :], EE[:, :], ALU.mult).then_inc(qcum_done, 1)

            def k_dec():
                dve.wait_ge(qcum_done, 1)
                cum = CUM[:, :].rearrange("p (c t) -> p c t", t=P)
                dve.tensor_tensor(EE[:, :].rearrange("p (c t) -> p c t", t=P), cum[:, :, P - 1:P].to_broadcast([P, H * TT, P]),
                                  cum, ALU.subtract).then_inc(kd_arg, 1)
                dve.wait_ge(kd_exp, 1)
                dve.tensor_tensor(KE[:, :], K2[:, :], EE[:, :], ALU.mult).then_inc(kd_done, 1)

            def gla_norm(j):
                dve.wait_ge(rstd_done, MT + TT + H + TT + TT + j + 1)
                for i in range(2):
                    b = full(dve, ("o2", j, i))
                    free(dve.tensor_tensor(OJ[:, 512 * i:512 * i + 512].rearrange("p (a b) -> p a b", a=2),
                                           b[:, :].rearrange("p (a b) -> p a b", a=2),
                                           RST[:, 10 + 2 * i:12 + 2 * i].unsqueeze(2).to_broadcast([P, 2, DV]),
                                           ALU.mult), ("o2", j, i))
                if j < TT - 1:
                    dve.wait_ge(etot_done, 1)
                    for h in range(H):
                        b = full(dve, ("kv", j, h // 2))
                        src = b[:, (h % 2) * DV:(h % 2 + 1) * DV]
                        if j == 0:
                            ins = dve.tensor_copy(STATE[:, h, :], src)
                        else:
                            ins = dve.scalar_tensor_tensor(STATE[:, h, :], STATE[:, h, :], ETOT[:, h * TT + j:h * TT + j + 1],
                                                           src, ALU.mult, ALU.add)
                        if h % 2:
                            free(ins, ("kv", j, h // 2))

            def gla_y(j, i):
                b = full(dve, ("oT", j, i))
                if GO + 1 + j > first["g_b"]:
                    drained(dve, ("fm", GO + j, 1))
                for cc in range(4):
                    c = 4 * i + cc
                    if j == 0:
                        drained(dve, fm_key("r", c))
                    r = R[:, c, tile_of(j)]
                    ins = dve.scalar_tensor_tensor(r, b[:, tile_of(cc)], col(C_GN + c), r, ALU.mult, ALU.mult)
                free(ins, ("oT", j, i))

            def add_branches(c0, c1):
                drained(dve, ("oT", TT - 1, 0))
                drained(dve, ("oT", TT - 1, 1))
                for c in range(c0, c1):
                    drained(dve, fm_key("g_b", c))
                    dve.tensor_tensor(R[:, c, :], R[:, c, :], U[:, c, :], ALU.add).then_inc(m_ready, 1)

            def half_stats(src, j, i):
                return dve.bn_stats(BN[:, j, i, :], src[:, j, 512 * i:512 * i + 512])

            def mean_var(j):
                return dve.bn_aggr(MV[:, j, :], BN[:, j, :, :].rearrange("p a b -> p (a b)"))

            def layer_scale(dst, j, r):
                dve.wait_ge(rstd_done, r)
                return dve.tensor_scalar(dst[:, j, :], dst[:, j, :], MV[:, j, 0:1], RST[:, j:j + 1], ALU.subtract, ALU.mult)

            def v_norm(j):
                dve.wait_ge(av_gelu, TT + j + 1)
                half_stats(VH, j, 0)
                link(half_stats(VH, j, 1))
                mean_var(j).then_inc(ln_var, 1)
                layer_scale(VH, j, MT + TT + H + TT + j + 1).then_inc(vhat_done, 1)

            def w_s_lower():
                for j in range(TT):
                    drained(dve, ("tm", first["v2"] + 2, j))
                for i in range(2):
                    b = full(dve, ("wsT", i))
                    free(dve.tensor_tensor(WST[:, 4 * i:4 * i + 4, :], quarters(b[:, :]),
                                           TRIU[:, :].unsqueeze(1).to_broadcast([P, 4, P]), ALU.mult), ("wsT", i))

            def sg_gate(i):
                if i == 0:
                    dve.wait_ge(bs_in, 16)
                for g in (2 * i, 2 * i + 1):
                    drained(dve, fm_key("a_u", g))
                    b = full(dve, ("sg", g))
                    link(dve.tensor_tensor(quarters(b[:, :]), quarters(b[:, :]),
                                           BS[:, g, :].unsqueeze(1).to_broadcast([P, TT, P]), ALU.add))
                    free(dve.tensor_tensor(U[:, g, :], U[:, g, :], b[:, :], ALU.mult), ("sg", g))

            def side(n):
                if n == 0:
                    for j in range(TT):
                        dve.wait_ge(rstd_done, MT + j + 1)
                        dve.tensor_scalar(XN[:, j, :], RES[:, j, :], RST[:, MT + j:MT + j + 1], None, ALU.mult).then_inc(x_normed, 1)
                for c in TURN_X.get(n, ()):
                    dve.wait_ge(t_hi, KC + c + 1)
                    free(dve.scalar_tensor_tensor(TL[:, c, :], bank[4 + c % 4][:, :], col(C_NORM + c),
                                                  TH[:, c, :].bitcast(f32), ALU.mult, ALU.subtract), ("xT", c))
                if n == GATES + 1:
                    gates_logf()
                    dve.wait_ge(tables_in, 16 * 4)
                    dve.wait_ge(masks_in, 16)
                    dve.tensor_copy(MASK[:, :, :], MASKF[:, :, :]).then_inc(masks_set, 1)
                if n == GATES + 2: gates_g()
                if n == GATES + 3: running_max()
                if n == GATES + 4: m_sum()
                if 0 <= n - ML < H: mlstm_weights(n - ML)
                if 0 <= n - ML - 1 < H: mlstm_out(n - ML - 1)
                if 0 <= n - ML - 2 < H: mlstm_y(n - ML - 2)
                if n == AT:
                    dve.memset(UP[:, :, 0:PAD], 0.0)
                    for i in range(2):
                        dve.memset(PW[i][:, 0:PAD], 0.0)
                if 0 <= n - AT - 2 < TT: mem_y(n - AT - 2)
                if 0 <= n - AT < TT: softmax(n - AT)
                if n == first["u"] + 1: pool_window(0); pool_window(1)
                if n == first["u"] + 2: pool_window(2); pool_window(3)
                if n == WO - 1: pool_scaled()
                if n == LG: logits_logf()
                if n == LV + 4: w_s_lower()
                if 0 <= n - LV < 2 * (LEVELS + 1): level_merge((n - LV) // 2 - 1, (n - LV) % 2)
                if 0 <= n - LV < 2 * LEVELS: (level_operands if (n - LV) % 2 else level_args)((n - LV) // 2)
                if n in (first["a_u"], first["a_u"] + 1):
                    v_norm(2 * (n - first["a_u"]))
                    v_norm(2 * (n - first["a_u"]) + 1)
                if 0 <= n - SG < 4: sg_gate(n - SG)
                if n == GO - 3: q_cum()
                if n == GO - 2: k_dec()
                if 0 <= n - GO < TT: gla_norm(n - GO)
                if 0 <= n - GO - 1 < TT:
                    gla_y(n - GO - 1, 0)
                    if n > GO + 1:
                        gla_y(n - GO - 1, 1)
                if n == WO2 - 1: add_branches(4, 6)

            def add_half(n0, half, scale, j):
                key = ("tm", n0, j)
                b = full(dve, key)
                r = RES[:, j, 512 * half:512 * half + 512]
                free(dve.scalar_tensor_tensor(r, r, scale, b[:, :], ALU.mult, ALU.add), key)
                drained(dve, key)

            def rows_lo(name, j, t0):
                for i in range(2):
                    dve.wait_ge(t_hi, t0 + 2 * j + i + 1)
                    free(lower(TL[:, 4 * i:4 * i + 4, tile_of(j)], quarters(bank[6 + i][:, :]),
                               TH[:, 4 * i:4 * i + 4, tile_of(j)]), (name, j, i))

            def center_rows(n0, j, g, v):
                add_half(n0, 1, ALPHA, j)
                link(half_stats(RES, j, 1))
                mean_var(j).then_inc(ln_var, 1)
                dve.wait_ge(ln_var, v + j + 1)
                dve.scalar_tensor_tensor(RES[:, j, :], RES[:, j, :], MV[:, j, 0:1], g[:, :], ALU.subtract,
                                         ALU.mult).then_inc(centered, 1)

            def scale_rows(j, r, b, c, done):
                dve.wait_ge(centered, c + j + 1)
                dve.wait_ge(rstd_done, r + j + 1)
                dve.scalar_tensor_tensor(RES[:, j, :], RES[:, j, :], RST[:, j:j + 1], b[:, :], ALU.mult, ALU.add).then_inc(done, 1)

            def drain(n):
                name, i = name_of(n)
                fm = [(("fm", n, t), 2 * i + t) for t in range(2)]
                if name == "gates":
                    key = ("fm", n, 0)
                    b = full(dve, key)
                    free(dve.tensor_scalar(GATES_T[:, :], b[0:2 * H, :], VC[0:2 * H, C_BG:C_BG + 1], None, ALU.add), key)
                if name in ("q", "k"):
                    for key, c in fm:
                        conv_taps(c + (4 if name == "k" else 0), key)
                if name == "z_b" and i == 1:
                    pool_y()
                if name == "w_out" and i == 2:
                    for j in range(TT):
                        add_half(n - 2, 0, 1.0, j)
                if name == "w_out" and i == 5:
                    dve.wait_ge(fg_in, 16)

                    def scale(j):
                        dve.wait_ge(rstd_done, MT + TT + H + j + 1)
                        r = RES[:, j, :]
                        dve.scalar_tensor_tensor(r, r, RST[:, 6 + j:7 + j], FG[:, :], ALU.mult, ALU.mult).then_inc(x1_done, 1)

                    for j in range(2):
                        add_half(n - 2, 1, 1.0, j)
                        scale(j)
                    rows_lo("x1T", 0, 2 * KC)
                    add_half(n - 2, 1, 1.0, 2)
                    rows_lo("x1T", 1, 2 * KC)
                    add_half(n - 2, 1, 1.0, 3)
                    scale(2)
                    scale(3)
                    rows_lo("x1T", 2, 2 * KC)
                    rows_lo("x1T", 3, 2 * KC)
                if name == "low":
                    key = ("fm", n, 0)
                    dve.wait_ge(alt_set, 1)
                    b = full(dve, key)
                    free(dve.tensor_scalar(ALT[0:16, :], b[0:16, :], VC[0:16, C_LOW:C_LOW + 1], None, ALU.add), key)
                if name in ("q2", "k2"):
                    for key, c in fm:
                        b = full(dve, key)
                        if name == "q2":
                            ins = dve.tensor_scalar(Q2[:, c * S:c * S + S], b[:, :], col(C_B2 + 16 + c), SCALE, ALU.add, ALU.mult)
                        else:
                            ins = dve.tensor_scalar(K2[:, c * S:c * S + S], b[:, :], col(C_B2 + 20 + c), None, ALU.add)
                        free(ins, key)
                if name in ("v2", "a_v") and i % 2:
                    dst, bias = (V2, BV) if name == "v2" else (VH, BAV)
                    h = slice(i // 2 * 512, i // 2 * 512 + 512)
                    dve.wait_ge(bv_in, 32)
                    for j in range(TT):
                        key = ("tm", n - 1, j)
                        b = full(dve, key)
                        free(dve.tensor_tensor(dst[:, j, h], b[:, :], bias[:, h], ALU.add), key)
                if name == "g_a":
                    for key, c in fm:
                        dve.wait_ge(ga_sig, c + 1)
                        drained(dve, ("sg", c))
                        b = full(dve, key)
                        free(dve.tensor_tensor(U[:, c, :], U[:, c, :], b[:, :], ALU.mult), key)
                if n == GO + 1:
                    gla_y(0, 1)
                if name == "g_b":
                    for half in range(2):
                        drained(dve, ("oT", min(n - GO - 1, TT - 1), half))
                    for key, c in fm:
                        dve.wait_ge(gb_sig, c + 1)
                        b = full(dve, key)
                        free(dve.tensor_tensor(R[:, c, :], R[:, c, :], b[:, :], ALU.mult), key)
                    if i == 2:
                        add_branches(0, 4)
                    if i == 3:
                        add_branches(6, 8)
                if name == "w_out2" and i == 1:
                    dve.wait_ge(x1_back, 16)
                    for j in range(TT):
                        add_half(n - 1, 0, ALPHA, j)
                        half_stats(RES, j, 0)
                if name == "w_out2" and i == 3:
                    dve.wait_ge(ln1_in, 32)
                    r0, t0 = MT + TT + H + 3 * TT, 2 * KC + 2 * TT
                    for j in range(2):
                        center_rows(n - 1, j, L1G, TT)
                        scale_rows(j, r0, L1B, 0, h1_done)
                    rows_lo("h1T", 0, t0)
                    center_rows(n - 1, 2, L1G, TT)
                    rows_lo("h1T", 1, t0)
                    scale_rows(2, r0, L1B, 0, h1_done)
                    center_rows(n - 1, 3, L1G, TT)
                    scale_rows(3, r0, L1B, 0, h1_done)
                    rows_lo("h1T", 2, t0)
                    rows_lo("h1T", 3, t0)

            def stage(n):
                if n + 1 >= ff1_0:
                    return
                name, i = name_of(n + 1)
                slot = 2 if n + 1 in PAIRED else i % 2
                if name == "w_out":
                    g = WO_GROUPS[i % 3]
                    split_x(slot, i, Y[:, 4 * g:4 * g + 4, :].rearrange("p a b -> p (a b)"))
                if name == "w_out2":
                    g = i % 2
                    split_x(slot, E_WO2 + i, R[:, 4 * g:4 * g + 4, :].rearrange("p a b -> p (a b)"))

            dve.wait_ge(columns_in, 16)
            for j in range(MT):
                dve.wait_ge(rstd_done, j + 1)
                dve.tensor_scalar(MEM[:, j, :], MEM[:, j, :], RST[:, j:j + 1], None, ALU.mult).then_inc(mem_normed, 1)
            split(0)
            for c in range(KC):
                dve.wait_ge(t_hi, (c | 1) + 1)
                q = (c % 2) * NMEM
                ins = dve.scalar_tensor_tensor(MEML[:, c, :], bank[4 + c // 2][:, q:q + NMEM], col(C_MEMN + c),
                                               MEMH[:, c, :].bitcast(f32), ALU.mult, ALU.subtract)
                if c % 2:
                    free(ins, ("memT", c // 2))
            for n in range(ff1_0):
                if n + 1 in PAIRED:
                    stage(n)
                split(n + 1)
                side(n)
                if n + 1 not in PAIRED:
                    stage(n)
                drain(n)

            def squares(m, group, more=0):
                for t in range(2):
                    dve.wait_ge(bank_free[t], more + (f0[t] + m + 1))
                    q = (2 * m + t) % 4 * S
                    f = F1[:, group, q:q + S]
                    dve.tensor_tensor(f, f, f, ALU.mult).then_inc(f1_done, 1)

            split(ff1_0 + 1)
            squares(0, 0)
            with dve.Fori(0, 7) as i:
                split(ff1_0 + 2, i * 2)
                squares(1, i, i * 2)
                split(ff1_0 + 3, i * 2)
                squares(2, i + 1, i * 2)
            split(ff2_0)
            split_x(0, E_FF2, F1[:, 0, :])
            squares(15, 7)

            for half in range(2):
                n0, e0 = ff2_0 + 8 * half, E_FF2 + 8 * half
                for g in (1, 2):
                    split(n0 + g)
                    split_x(g % 2, e0 + g, F1[:, g, :])
                with dve.Fori(0, 2) as i:
                    for g in (3, 4):
                        split(n0 + g, i * 2)
                        split_x(g % 2, e0 + g, F1[:, i * 2 + g, :], i * 2)
                if half == 1:
                    split_x(2, e0 + 7, F1[:, 7, :])
                    split(n0 + 7)
                else:
                    split(n0 + 7)
                    split_x(1, e0 + 7, F1[:, 7, :])
                    split(n0 + 8)
                    split_x(0, e0 + 8, F1[:, 0, :])
                    for j in range(TT):
                        add_half(n0, 0, ALPHA, j)
                        half_stats(RES, j, 0)
            dve.wait_ge(ln2_in, 32)
            for j in range(TT):
                center_rows(ff2_0 + 8, j, L2G, 2 * TT)
                scale_rows(j, MT + TT + H + 4 * TT, L2B, TT, h2_done)

        @block.gpsimd
        def _(pool):
            links, roots = [0], [0]

            def link(ins):
                links[0] += 1
                ins.then_inc(pool_chain, 1)
                pool.wait_ge(pool_chain, links[0])

            def rstd(dst, src, w, mean, eps):
                if roots[0]:
                    pool.wait_ge(rstd_done, roots[0])
                roots[0] += 1
                link(pool.tensor_scalar(RTMP[:, 0:w], src, mean, eps, ALU.mult, ALU.add))
                pool.tensor_tensor(dst, RTMP[:, 0:w], NHALF[:, 0:w], ALU.pow).then_inc(rstd_done, 1)

            def load_all(dst, src, s):
                pool.dma_start(dst, src.partition_broadcast(P)).then_inc(s, 16)

            pool.memset(ONES[:, :], 1.0).then_inc(ones_set, 1)
            pool.memset(V[:, :, :, P:P + 1], 1.0).then_inc(ones_set, 1)
            link(pool.memset(NHALF[:, :], -0.5))
            for c in range(MT + TT):
                pool.wait_ge(squared, c + 1)
                rstd(RST[:, c:c + 1], SSQ[:, c:c + 1], 1, 1.0, RMS_EPS)
            full(pool, ("m_all", H - 1))
            pool.memset(ALT[:, :], 1.0).then_inc(alt_set, 1)
            for h in range(H):
                pool.wait_ge(ml_ss, h + 1)
                rstd(RST[:, 10:14], SSQ[:, 10:14], 4, 1 / P, RMS_EPS)
            pool.wait_ge(ml_h, H)
            pool.dma_start(POOLW[:, :, :], a["pool_w"][0].rearrange("g c d -> c g d")).then_inc(poolw_in, 16)
            full(pool, ("yc", TT - 1))
            load_all(BV[:, :], a["b_in_2"][0, 3 * D:4 * D], bv_in)
            load_all(BAV[:, :], a["b_in_2"][0, D:2 * D], bv_in)
            for j in range(TT):
                pool.wait_ge(squared, MT + TT + j + 1)
                rstd(RST[:, 6 + j:7 + j], SSQ[:, 6 + j:7 + j], 1, 1.0, RMS_EPS)
            pool.wait_ge(x1_done, TT)
            pool.dma_start(x1_spill.rearrange("(j p) n -> p j n", p=P), RES[:, :, :]).then_inc(x1_spilled, 16)
            for t in (SC[:, :, :], KE[:, :]):
                pool.memset(t, 0.0).then_inc(zeros_set, 1)
            pool.wait_ge(x1_spilled, 16)
            for i in range(2):
                drained(pool, ("x1T", TT - 1, i))
            pool.dma_start(WSR[:, :, :], a["sg_w_s_2"][0].rearrange("g t s -> t g s")).then_inc(ws_in, 16)
            full(pool, ("lg", TT - 1))
            load_all(SGG[:, :], a["sg_ln_g_2"][0], sg_in)
            load_all(SGB[:, :], a["sg_ln_b_2"][0], sg_in)
            for j in range(TT):
                drained(pool, ("tm", first["a_v"] + 2, j))
            load_all(BS[:, :, :], a["sg_b_s_2"][0], bs_in)
            pool.wait_ge(sg_in, 32)

            def v_gain(j):
                link(pool.tensor_tensor(VH[:, j, :], VH[:, j, :], SGG[:, :], ALU.mult))
                pool.tensor_tensor(VH[:, j, :], VH[:, j, :], SGB[:, :], ALU.add).then_inc(vh_ready, 1)

            for j in range(TT):
                pool.wait_ge(ln_var, j + 1)
                rstd(RST[:, j:j + 1], MV[:, j, 1:2], 1, 1.0, LN_EPS)
                if j:
                    pool.wait_ge(vhat_done, j)
                    v_gain(j - 1)
            pool.wait_ge(vhat_done, TT)
            v_gain(TT - 1)
            for j in range(TT):
                pool.wait_ge(squared, MT + 2 * TT + H * (j + 1))
                rstd(RST[:, 10:14], SSQ[:, 10:14], 4, 1.0, LN_EPS)
            pool.wait_ge(m_ready, KC)
            pool.dma_start(RES[:, :, :], x1_spill.rearrange("(j p) n -> p j n", p=P)).then_inc(x1_back, 16)
            load_all(L1G[:, :], a["ln1_g_2"][0], ln1_in)
            load_all(L1B[:, :], a["ln1_b_2"][0], ln1_in)
            load_all(L2G[:, :], a["ln2_g_2"][0], ln2_in)
            load_all(L2B[:, :], a["ln2_b_2"][0], ln2_in)
            for j in range(2 * TT):
                pool.wait_ge(ln_var, TT + j + 1)
                rstd(RST[:, j % TT:j % TT + 1], MV[:, j % TT, 1:2], 1, 1.0, LN_EPS)

        @block.sync
        def _(sp):
            def load(n, src, more=0):
                if n >= 2:
                    sp.wait_ge(w_lo, more + (n - 1))
                k, c = blocks[n][2].shape[1:]
                sp.dma_start(RAW[n % 2][:, 0:k * c].rearrange("p (k c) -> p k c", c=c), src).then_inc(w_loaded[n % 2], 16)

            for j in range(MT):
                sp.dma_start(MEM[:, j, :], a["mem"][0, j * P:j * P + P, :]).then_inc(mem_in[j], 16)
            load(0, blocks[0][2])
            load(1, blocks[1][2])
            for j in range(TT):
                sp.dma_start(RES[:, j, :], a["x"][0, j * P:j * P + P, :]).then_inc(x_in[j], 16)
            load(2, blocks[2][2])
            load(3, blocks[3][2])
            sp.dma_start(TRIU[:, :], a["c_triu"]).then_inc(tables_in, 16)
            sp.dma_start(TRI16[:, :], a["c_triu16"]).then_inc(tables_in, 16)
            sp.dma_start(NSEL[:, :, :], a["c_nsel"]).then_inc(tables_in, 16)
            sp.dma_start(PINV[:, :, :], a["c_pool_edge"].partition_broadcast(P)).then_inc(tables_in, 16)
            sp.dma_start(MASKF[:, :, :], a["c_masks"]).then_inc(masks_in, 16)
            sp.dma_start(FG[:, :], a["final_norm_g"].partition_broadcast(P)).then_inc(fg_in, 16)
            sp.dma_start(WG2[0:16, :], a["gla_w_gate2_2"][0]).then_inc(wg2_in, 16)
            sp.dma_start(WG2[16:17, :], a["gla_b_gate_2"]).then_inc(wg2_in, 16)
            for n in range(4, ff1_0):
                load(n, blocks[n][2])
            up = a["w_ff1_2"][0].rearrange("(k p) (b c) -> b p k c", p=P, c=256)
            with sp.Fori(0, 8) as i:
                for b in range(2):
                    load(ff1_0 + b, up[i * 2 + b], i * 2)
            down = a["w_ff2_2"][0].rearrange("(g k p) (h c) -> h g p k c", p=P, k=4, h=2)
            for half in range(2):
                with sp.Fori(0, 4) as i:
                    for b in range(2):
                        load(ff2_0 + 8 * half + b, down[half, i * 2 + b], i * 2)
            for j in range(TT):
                sp.wait_ge(h2_done, j + 1)
                sp.dma_start(out[0, j * P:j * P + P, :], RES[:, j, :]).then_inc(stored, 16)
            sp.wait_ge(stored, 16 * TT)


def constants():
    s, t = np.arange(P)[:, None], np.arange(P)[None, :]
    masks = np.zeros((P, LEVELS + 1, P), np.float32)
    for l in range(LEVELS):
        half = P >> (l + 1)
        masks[:, l] = (s // (2 * half) == t // (2 * half)) & (s % (2 * half) < half) & (t % (2 * half) >= half)
    masks[:, LEVELS] = s == t
    nsel = np.zeros((H, H, P), np.float32)
    for h in range(H):
        nsel[h, h] = -1
    edge = 1 / np.minimum(np.arange(1, 17)[None, :], np.array(WINDOWS)[:, None]).astype(np.float32)
    return {"c_ident": (s == t).astype(np.float32), "c_triu": (s <= t).astype(np.float32),
            "c_triu16": ((s <= t) / 16).astype(np.float32), "c_masks": masks, "c_nsel": nsel,
            "c_pool_edge": edge.astype(np.float32)}


def vector_columns(i):
    b_in = i["b_in_2"][0]
    low = 5 * D
    rows = [i["norm_g"][0], i["mem_norm_g"][0], i["conv_w"][0].reshape(-1), i["conv_b"][0], i["mlstm_norm_g"][0],
            i["pool_scale"][0], b_in[:low], b_in[low + 16:], i["gla_norm_g_2"][0], b_in[low:low + 16], np.zeros(P - 16, np.float32),
            i["b_gates"][0], np.zeros(P - 2 * H, np.float32)]
    rows = np.concatenate([np.asarray(r) for r in rows])
    return rows.reshape(-1, P).T


def kernel(**inputs):
    import concourse.bacc as bacc
    from concourse import mybir
    from concourse.bass_utils import run_bass_kernel_spmd

    nc = bacc.Bacc("TRN2", target_bir_lowering=False, num_devices=1)
    arrays = {f"in_{k}": np.ascontiguousarray(v) for k, v in inputs.items()}
    arrays["in_vector_columns"] = np.ascontiguousarray(vector_columns(inputs))
    arrays.update({f"in_{k}": v for k, v in constants().items()})
    a = {k[3:]: nc.dram_tensor(k, v.shape, mybir.dt.from_np(v.dtype), kind="ExternalInput").ap() for k, v in arrays.items()}
    out = nc.dram_tensor("out_0", (1, S, D), mybir.dt.float32, kind="ExternalOutput").ap()
    x1_spill = nc.dram_tensor("x1_spill", (S, D), mybir.dt.float32, kind="Internal").ap()
    two_blocks(nc, a, out, x1_spill)
    r = run_bass_kernel_spmd(nc, [arrays], core_ids=[0])
    return r.results[0]["out_0"]
```

```python
import numpy as np


P = 128
S = 512
D = 1024
TT = S // P
KC = D // P
NMEM = 256
MT = NMEM // P
H = 4
GW = 512
RMS_EPS = 1e-6
LN_EPS = 1e-5
SCALE = float(P) ** -0.5
ALPHA = 2.0 ** 0.25
TEMP = 16
THIN = 16
STACK = 6 * THIN
LEVELS = 7
WINDOWS = (2, 4, 8, 16)
K1 = 1024
DV = 256
WARM_UP = 12
PAD = 8
ML_OFF = (0, 512, 896, 1152)


def block_list(a):
    w_in, w_kv, w_out = a["w_in"][0], a["w_mem_kv"][0], a["w_out"][0]
    w_in2, w_out2, w_ff1, w_ff2 = a["w_in_2"][0], a["w_out_2"][0], a["w_ff1_2"][0], a["w_ff2_2"][0]

    def chunks(w):
        return w.rearrange("(k p) n -> p k n", p=P)

    blocks = []

    def fm(name, w, c0, width):
        for c in range(c0, c0 + width, 256):
            blocks.append(("fm", name, chunks(w)[:, :, c:c + 256]))

    def tm(name, w, c0, width, groups):
        for c in range(c0, c0 + width, 512):
            for g in groups:
                blocks.append(("tm", name, chunks(w)[:, 4 * g:4 * g + 4, c:c + 512]))

    fm("km", w_kv, 0, GW)
    tm("vm", w_kv, GW, GW, (0, 1))
    fm("q", w_in, 0, GW)
    fm("k", w_in, GW, GW)
    tm("v", w_in, 2 * GW, GW, (0, 1))
    tm("o", w_in, 3 * GW, GW, (0, 1))
    z_a = 4 * GW
    u = 5 * GW + 2 * H
    fm("z_a", w_in, z_a, GW)
    fm("qc", w_in, u + 2 * GW, GW)
    fm("z_c", w_in, u + 3 * GW, GW)
    fm("u", w_in, u, GW)
    fm("z_b", w_in, u + GW, GW)
    tm("w_out", w_out, 0, D, (0, 2, 1))
    low = 5 * D
    fm("q2", w_in2, 2 * D, D // 2)
    fm("k2", w_in2, 2 * D + D // 2, D // 2)
    tm("v2", w_in2, 3 * D, D, (0, 1))
    tm("a_v", w_in2, D, D, (0, 1))
    fm("a_u", w_in2, 0, D)
    fm("g_a", w_in2, low + 16, D)
    fm("r", w_in2, 4 * D, D)
    fm("g_b", w_in2, low + 16 + D, D)
    tm("w_out2", w_out2, 0, D, (0, 1))
    fm("ff1", w_ff1, 0, 4 * D)
    tm("ff2", w_ff2, 0, D, range(8))
    return blocks


def two_blocks(nc, a, out, x1_spill, m_spill):
    from concourse import mybir
    from contextlib import ExitStack

    f32 = mybir.dt.float32
    f32r = mybir.dt.float32r
    u8 = mybir.dt.uint8
    ALU = mybir.AluOpType
    ACT = mybir.ActivationFunctionType
    AX = mybir.AxisListType

    blocks = block_list(a)
    N = len(blocks)
    steps = {}
    for n, (_, name, _) in enumerate(blocks):
        steps.setdefault(name, []).append(n)
    first = {name: of[0] for name, of in steps.items()}

    def name_of(n):
        return blocks[n][1], steps[blocks[n][1]].index(n)

    base = 16512
    top = [base]

    def at(name, shape, offset, dt=f32):
        return nc.alloc_sbuf_tensor_at(name, shape, dt, offset=offset)

    def place(name, shape, dt=f32, size=4):
        n = int(np.prod(shape[1:])) * size
        t = at(name, shape, top[0], dt)
        top[0] += (n + 31) // 32 * 32
        return t

    RAW = [place(f"w_raw{i}", [P, 2048]) for i in range(2)]
    WH = [place(f"w_hi{i}", [P, 2048], f32r) for i in range(2)]
    WL = [place(f"w_lo{i}", [P, 2048], f32r) for i in range(2)]
    XS = top[0]
    top[0] += 32 * K1
    TH = place("act_t_hi", [P, KC, S], f32r)
    TL = place("act_t_lo", [P, KC, S], f32r)
    A = top[0]
    top[0] += 88 * K1 + 64

    IDENT = place("ident", [P, P])
    TRIU = place("triu", [P, P])
    ONES = place("ones", [P, P])
    MASK = place("level_masks", [P, LEVELS + 1, P], u8, 1)
    VC = place("vector_columns_sb", [P, P + 2 + H])
    THIN_RAW = place("thin_w_raw", [P, KC, THIN])
    THIN_PLACE = top[0]
    THIN_W = [at(f"thin_w_hi_lo{i}", [P, KC, copies, 2 * THIN], THIN_PLACE, f32r) for i, copies in ((0, 1), (1, 3))]
    top[0] += 3 * K1
    PINV = place("pool_edge", [P, 4, 16])
    NHALF = place("minus_half", [P, H])
    SSQ = place("mean_squares", [P, 16])
    RST = place("rstd", [P, 16])
    RTMP = place("rstd_tmp", [P, H])
    G8 = place("gates", [P, TT, 2 * H])
    LF = place("log_f", [P, TT, H])
    GT1 = place("gate_tmp", [P, TT, H])
    GG = place("i_minus_F", [P, TT, H])
    FS = place("F", [P, TT, H])
    FLOOR = place("den_floor", [P, TT, H])
    RDEN = place("den", [P, TT])
    SMX = place("neg_max", [P, H])
    SSUM = place("row_sum", [P, H])
    BN = place("bn", [P, TT, 2, 6])
    MV = place("mean_var", [P, TT, 2])
    ETOT = place("exp_total", [P, H * TT])
    assert top[0] <= 229344, top[0]

    XH = [at(f"x_hi{i}", [P, 2048], XS + 8 * K1 * i, f32r) for i in range(2)]
    XL = [at(f"x_lo{i}", [P, 2048], XS + 16 * K1 + 8 * K1 * i, f32r) for i in range(2)]
    XH += [at(f"x_hi{i}", [P, 2048], A + k * K1, f32r) for i, k in ((2, 56), (3, 24))]
    XL += [at(f"x_lo{i}", [P, 2048], A + 16 * K1, f32r) for i in (2, 3)]
    WH.append(at("w_hi2", [P, 2048], A + 40 * K1, f32r))
    WL.append(at("w_lo2", [P, 2048], A + 48 * K1, f32r))
    MEMH = at("mem_t_hi", [P, KC, NMEM], XS, f32r)
    MEML = at("mem_t_lo", [P, KC, NMEM], XS + 8 * K1, f32r)
    MEM = at("mem", [P, MT, D], XS + 16 * K1)
    MASKF = at("level_masks_loaded", [P, LEVELS + 1, P], XS + 26 * K1)
    GATES_T = at("gates_t", [2 * THIN, S], XS + 20 * K1)
    GROW = at("g_rows", [H, S], XS + 16 * K1)
    MROW = at("m_rows", [H, S], XS + 18 * K1)
    MB = at("m_all", [P, H, S], XS)
    PP = [at(f"mlstm_p{i}", [P, 1280], XS + 8 * K1 + 5 * K1 * i) for i in range(2)]
    HM = [at(f"mlstm_h{i}", [P, TT, P], XS + 18 * K1 + 2 * K1 * i) for i in range(2)]
    SQ = at("mlstm_sq", [P, TT, P], XS + 22 * K1)
    QC = at("q_c", [P, H, S], XS + 24 * K1)
    PT = [at(f"probs_t{i}", [P, 2 * H, P], XS + 8 * K1 + 4 * K1 * i) for i in range(2)]
    LF2 = at("log_f2", [P, TT, S], XS)
    EE = at("decay", [P, H * S], XS)
    KDTH = at("k_dec_t_hi", [P, H, TT, P], XS, f32r)
    KDTL = at("k_dec_t_lo", [P, H, TT, P], XS + 16 * K1, f32r)
    QE = at("q_decayed", [P, H * S], XS + 8 * K1)
    QEC = at("q_decayed_right_halves", [P, H * S // 2], XS + 8 * K1)
    KE = at("k_decayed", [P, H * S], XS + 16 * K1)
    SC = at("gla_scores", [P, H * TT, P], XS + 24 * K1)
    SCL = at("gla_scores_lo", [P, H, TT, P], XS + 24 * K1, f32r)

    RES = at("residual", [P, TT, D], A)
    XN = at("x_normed", [P, TT, D], A + 16 * K1)
    Y = at("y", [P, 12, S], A + 16 * K1)
    QK = at("qk", [P, 8, S], A + 40 * K1)
    V = at("v_and_ones", [P, TT, H, P + 1], A + 56 * K1)
    O = at("o_gate", [P, TT, GW], A + 64 * K1 + 64)
    KM = at("k_mem", [P, H, NMEM], A + 72 * K1 + 64)
    VM = at("v_mem", [P, MT, GW], A + 76 * K1 + 64)
    FG = at("final_g_all", [P, D], A + 80 * K1 + 64)
    WG2 = at("w_gate2_repeated", [STACK, S], A + 84 * K1 + 64)
    PROB = [at(f"probs{i}", [P, H, NMEM], A + 56 * K1 + 4 * K1 * i) for i in range(2)]
    UP = at("u_padded", [P, 4, PAD + S], A + 40 * K1)
    PW = [at(f"pool_sum{i}", [P, PAD + S], A + 49 * K1 + 2560 * i) for i in range(2)]
    POOLW = at("pool_w_sb", [P, 4, P], A + 64 * K1)
    SINK = at("squares_sink", [P, D], A + 68 * K1)
    U = at("u_gelu", [P, KC, S], A)
    WSR = at("w_s_rows", [P, 8, P], A)
    Q2 = at("q2", [P, H * S], A + 16 * K1)
    K2 = at("k2", [P, H * S], A + 24 * K1)
    CUM = at("cum", [P, H * S], A + 32 * K1)
    V2 = at("v2", [P, TT, D], A + 40 * K1)
    V2H = at("v2_hi", [P, TT, D], A + 16 * K1, f32r)
    V2L = at("v2_lo", [P, TT, D], A + 40 * K1, f32r)
    SCH = at("gla_scores_hi", [P, H, TT, P], A + 32 * K1, f32r)
    VH = at("v_hat", [P, TT, D], A + 56 * K1)
    R = at("r_silu", [P, KC, S], A + 56 * K1)
    BV = at("b_v_all", [P, D], A + 72 * K1)
    WST = at("w_s_t", [P, 8, P], A + 72 * K1)
    BAV = at("b_av_all", [P, D], A + 76 * K1)
    BS = at("b_s_all", [P, 8, P], A + 76 * K1)
    ALT = at("a_low_t_hi_lo_hi", [STACK, S], A + 86 * K1 + 64, f32r)
    WG2S = at("w_gate2_hi_hi_lo", [STACK, S], A + 32 * K1, f32r)
    SGG = at("sg_g_all", [P, D], A + 80 * K1)
    SGB = at("sg_b_all", [P, D], A + 84 * K1)
    STATE = at("gla_state", [P, H, 256], A + 80 * K1)
    OJ = at("gla_o", [P, D], A + 84 * K1)
    L1G = at("ln1_g_all", [P, D], A + 72 * K1)
    L1B = at("ln1_b_all", [P, D], A + 76 * K1)
    L2G = at("ln2_g_all", [P, D], A + 80 * K1)
    L2B = at("ln2_b_all", [P, D], A + 84 * K1)
    F1 = at("ff_hidden", [P, 8, 2048], A + 16 * K1)

    C_NORM, C_MEMN, C_CW, C_CB, C_MN, C_PS = 0, 8, 16, 48, 56, 60
    C_B2, C_B2G, C_GN, C_LOW, C_BG, C_GATE2 = 64, 64 + 40, 64 + 56, P, P + 1, P + 2

    def col(c):
        return VC[:, c:c + 1]

    ctx = ExitStack()
    with ctx:
        bank = [ctx.enter_context(nc.psum_tensor(f"bank{b}", [P, 512], f32)) for b in range(8)]

        def sem(name):
            return ctx.enter_context(nc.semaphore(name))

        w_loaded = [sem(f"w_loaded{i}") for i in range(2)]
        w_hi, w_lo, w_used = sem("w_hi_done"), sem("w_lo_done"), sem("w_block_used")
        w0_loaded, w_half_hi = sem("w_block0_first_half_loaded"), sem("w_block1_2_first_half_hi")
        w0_hi, w0_lo = sem("w_block0_second_half_hi"), sem("w_block0_second_half_lo")
        own_lo = sem("w_lo_done_by_gpsimd")
        x_hi, x_lo = sem("x_hi_done"), sem("x_lo_done")
        bank_full = [sem(f"bank_full{b}") for b in range(8)]
        bank_free = [sem(f"bank_free{b}") for b in range(8)]
        ident_in, columns_in, tables_in, masks_in, thin_in, fg_in, wg2_in = (
            sem(s + "_in") for s in ("ident", "columns", "tables", "masks", "thin", "fg", "wg2"))
        thin_hi, thin_lo = sem("thin_hi"), sem("thin_lo")
        gate2_hi, gate2_lo, low_hi = sem("w_gate2_hi"), sem("w_gate2_lo"), sem("a_low_hi")
        mem_in, mb_in = [sem(f"mem_in{j}") for j in range(MT)], sem("m_all_in")
        x_in = [sem(f"x_in{j}") for j in range(TT)]
        poolw_in, bv_in, ws_in, sg_in, bs_in, ln1_in, ln2_in = (sem(s + "_in") for s in
                                                                ("poolw", "bv", "ws", "sg", "bs", "ln1", "ln2"))
        m_spilled, x1_spilled, x1_back, stored = (sem(s) for s in ("m_spilled", "x1_spilled", "x1_back", "stored"))
        ones_set, zeros_set, masks_set = (sem(s) for s in ("ones_set", "zeros_set", "masks_set"))
        squared, rstd_done = sem("squares_summed"), sem("rstd_done")
        mem_normed, x_normed, t_hi = (sem(s) for s in ("mem_normed", "x_normed", "turned_hi"))
        softplus_done, logf_done, g_done, m_done, floor_done = (sem(s) for s in
                                                                ("softplus_done", "logf_done", "g_done", "m_done", "floor_done"))
        conv_first, qk_done = sem("conv_first_tap"), sem("qk_done")
        ml_arg, ml_exp, ml_ss, ml_h = sem("mlstm_arg"), sem("mlstm_exp"), sem("mlstm_ss"), sem("mlstm_h_done")
        max_done, probs_done = sem("softmax_max"), sem("probs_normed")
        pooled, yb_done, x1_done = sem("pooled"), sem("yb_done"), sem("x1_done")
        lg_min, lg_softplus = sem("logit_min"), sem("logit_softplus")
        lv_arg, lv_exp, lv_qk = sem("level_arg"), sem("level_exp"), sem("level_operands")
        av_gelu, vhat_done, vh_ready, ga_sig, gb_sig = (sem(s) for s in
                                                        ("av_gelu", "vhat_done", "vh_ready", "ga_sigmoid", "gb_sigmoid"))
        qc_exp, qcum_done, kd_arg, kd_exp, kd_done, etot_done = (sem("gla_" + s) for s in
                                                                ("qcum_exp", "qcum", "kdec_arg", "kdec_exp", "kdec", "exp_total"))
        kdt_hi, chunk_hi, chunk_lo = sem("gla_kdec_t_hi"), sem("gla_chunk_hi"), sem("gla_chunk_lo")
        m_ready = sem("m_ready")
        centered = sem("ln_centered")
        ln_var, h1_done, h2_done, f1_done = sem("ln_var"), sem("h1_done"), sem("h2_done"), sem("f1_done")
        pool_chain, dve_chain, act_chain = sem("pool_chain"), sem("dve_chain"), sem("act_chain")

        block = ctx.enter_context(nc.Block())

        turn, uses, block_done = {}, [0] * 8, {}

        def full(eng, key):
            b, u = turn[key]
            eng.wait_ge(bank_full[b], u + 1)
            return bank[b]

        def free(ins, key):
            ins.then_inc(bank_free[turn[key][0]], 1)

        def drained(eng, key):
            b, u = turn[key]
            eng.wait_ge(bank_free[b], u + 1)

        def quarters(t):
            return t.rearrange("p (a b) -> p a b", a=4)

        def slot_of(n):
            return 2 if n - 1 in PAIRED else n % 2

        def weights(n, pair):
            k, c = blocks[n][2].shape[1:]
            return tuple(t[slot_of(n)][:, 0:k * c].rearrange("p (k c) -> p k c", c=c) for t in pair)

        def tile_of(j):
            return slice(j * P, j * P + P)

        ff1_0, ff2_0 = first["ff1"], first["ff2"]
        WO, WO2 = first["w_out"], first["w_out2"]
        WO_GROUPS = (0, 2, 1)
        GATES = first["q"]
        TURN_X = {2: (0, 1, 2, 3), 3: (4, 5, 6, 7)}
        ML = first["z_a"]
        AT = ML + 4
        LOW = WO + 7
        LG = LOW + 1
        LV = first["v2"]
        GO = LV + 2 * LEVELS + 4
        SG = first["a_u"] + 4
        OWN = {WO + 5: 2, WO2 + 3: 3}
        PAIRED = tuple(OWN)
        MID = (GATES + 5, LV, GO - 1, GO + 2)
        E_WO2 = 6
        E_FF2 = E_WO2 + 4

        def fm_key(name, c):
            return ("fm", steps[name][c // 2], c % 2)

        @block.tensor
        def _(pe):
            n_used = [0]

            def take(b, key):
                turn[key] = (b, uses[b])
                if uses[b]:
                    pe.wait_ge(bank_free[b], uses[b])
                uses[b] += 1
                return bank[b]

            def give(ins, key):
                ins.then_inc(bank_full[turn[key][0]], 1)

            def three(dst, lh, ll, rh, rl, start, stop):
                pe.matmul(dst, lh, rh, start=start, stop=False)
                pe.matmul(dst, lh, rl, start=False, stop=False)
                return pe.matmul(dst, ll, rh, start=False, stop=stop)

            def fm_block(n, xh, xl, tokens=S, between=None):
                wh, wlo = weights(n, (WH, WL))
                pe.wait_ge(w_lo, n + 1)
                for t in range(wh.shape[2] // P):
                    key = ("fm", n, t)
                    dst = take(t + 2 * (n == 1), key)[:, 0:tokens]
                    for k in range(KC):
                        last = three(dst, wh[:, k, tile_of(t)], wlo[:, k, tile_of(t)], xh[:, k, :], xl[:, k, :],
                                     k == 0, k == KC - 1)
                    give(last, key)
                    if between and t == 0:
                        between()
                b, u = turn[key]
                block_done[n] = (bank_full[b], u + 1)

            def fm_block_by_halves(n, name, done, turns):
                wh, wlo = weights(n, (WH, WL))
                pe.wait_ge(own_lo, 1 + PAIRED.index(n - 1))
                for half in range(2):
                    c = slice(half * S // 2, (half + 1) * S // 2)
                    for t in range(2):
                        key = ("fm", n, t)
                        if half == 0:
                            take(t, key)
                        for k in range(KC):
                            if t == 0 and k % 4 == 0:
                                for j in (2 * half, 2 * half + 1):
                                    drained(pe, (name, j, k // 4))
                            last = three(bank[t][:, c], wh[:, k, tile_of(t)], wlo[:, k, tile_of(t)], TH[:, k, c], TL[:, k, c],
                                         k == 0, k == KC - 1)
                            if half == 0 and (t, k) in turns:
                                turn_row(name, done, turns[t, k])
                        if half:
                            give(last, key)
                b, u = turn[key]
                block_done[n] = (bank_full[b], u + 1)

            def tm_block(n, g, groups, lhs, tiles=TT, between=None):
                wh, wlo = weights(n, (WH, WL))
                pe.wait_ge(w_lo, n + 1)
                for j in range(tiles):
                    key = ("tm", n - g, j)
                    if g == 0:
                        take(2 + j, key)
                    for kk in range(4):
                        xh, xl = lhs(kk)
                        last = three(bank[2 + j][:, :], xh[:, tile_of(j)], xl[:, tile_of(j)], wh[:, kk, :], wlo[:, kk, :],
                                     g == 0 and kk == 0, g == groups - 1 and kk == 3)
                    if g == groups - 1:
                        give(last, key)
                    if between and j == 1:
                        between()
                if g == groups - 1:
                    b, u = turn[key]
                    block_done[n] = (bank_full[b], u + 1)
                else:
                    n_used[0] += 1
                    last.then_inc(w_used, 1)
                    block_done[n] = (w_used, n_used[0])

            def tm_pair(n, groups, e, own, turn_one=None, turns=None):
                w = [weights(n - 1 + b, (WH, WL)) for b in range(2)]
                x = [staged(0), staged(own)]
                n0 = n + 1 - groups
                for b, j in ((0, 0), (0, 1), (1, 0), (1, 1), (0, 2), (1, 2), (0, 3), (1, 3)):
                    g, key = groups - 2 + b, ("tm", n0, j)
                    if j == 0:
                        pe.wait_ge(w_lo, n + b)
                        pe.wait_ge(x_lo, e + b + 1)
                    if g == 0:
                        take(2 + j, key)
                    for kk in range(4):
                        xh, xl = x[b](kk)
                        last = three(bank[2 + j][:, :], xh[:, tile_of(j)], xl[:, tile_of(j)], w[b][0][:, kk, :], w[b][1][:, kk, :],
                                     g == 0 and kk == 0, b == 1 and kk == 3)
                    if b:
                        give(last, key)
                    elif j == TT - 1:
                        n_used[0] += 1
                        last.then_inc(w_used, 1)
                        block_done[n - 1] = (w_used, n_used[0])
                    if turn_one and (b, j) in turns:
                        turn_one(turns[b, j])
                b, u = turn["tm", n0, TT - 1]
                block_done[n] = (bank_full[b], u + 1)

            def staged(slot):
                h, l = quarters(XH[slot][:, :]), quarters(XL[slot][:, :])
                return lambda kk: (h[:, kk, :], l[:, kk, :])

            def resident(h, l, g):
                return lambda kk: (h[:, 4 * g + kk, :], l[:, 4 * g + kk, :])

            def turn_four(src, b, key):
                dst = take(b, key)
                for i in range(4):
                    last = pe.transpose(dst[:, tile_of(i)], src(i), IDENT[:, :])
                give(last, key)

            def warm_up():
                pe.wait_ge(ones_set, 1)
                for _ in range(WARM_UP):
                    pe.matmul(bank[7][:, 0:P], ONES[:, :], ONES[:, :], start=True, stop=True)

            def turn_mem():
                pe.wait_ge(ident_in, 16)
                for i in range(KC // 2):
                    take(4 + i, ("memT", i))
                for j in range(MT):
                    pe.wait_ge(mem_normed, j + 1)
                    for c in range(KC):
                        q = (c % 2) * NMEM + j * P
                        last = pe.transpose(bank[4 + c // 2][:, q:q + P], MEM[:, j, tile_of(c)], IDENT[:, :])
                        if j == MT - 1 and c % 2:
                            give(last, ("memT", c // 2))

            def first_block():
                wh, wlo = weights(0, (WH, WL))
                for half, ready in enumerate((w_lo, w0_lo)):
                    pe.wait_ge(ready, 1)
                    for t in range(2):
                        key = ("fm", 0, t)
                        if half == 0:
                            take(t, key)
                        for k in range(KC // 2 * half, KC // 2 * (half + 1)):
                            drained(pe, ("memT", k // 2))
                            last = three(bank[t][:, 0:NMEM], wh[:, k, tile_of(t)], wlo[:, k, tile_of(t)], MEMH[:, k, :], MEML[:, k, :],
                                         k == 0, k == KC - 1)
                        if half:
                            give(last, key)
                b, u = turn["fm", 0, 1]
                block_done[0] = (bank_full[b], u + 1)

            def turn_x(chunks):
                for c in chunks:
                    pe.wait_ge(x_normed, TT)
                    turn_four(lambda j: XN[:, j, tile_of(c)], 4 + c % 4, ("xT", c))

            def thin(i, key, chunk_ready=None):
                pe.wait_ge(thin_lo, i + 1)
                w = THIN_W[i][:, :, :, :].rearrange("p k i c -> p k (i c)")
                dst = take(7, key)[0:w.shape[2], :]
                for k in range(KC):
                    if chunk_ready:
                        chunk_ready(k)
                    pe.matmul(dst, w[:, k, :], TH[:, k, :], start=k == 0, stop=False)
                    last = pe.matmul(dst, w[:, k, :], TL[:, k, :], start=False, stop=k == KC - 1)
                give(last, key)

            def gates():
                drained(pe, "thin_gates")
                dst = take(6, "gates")
                for j in range(TT):
                    last = pe.transpose(dst[:, 2 * THIN * j:2 * THIN * (j + 1)], GATES_T[:, tile_of(j)],
                                        IDENT[0:2 * THIN, 0:2 * THIN])
                give(last, "gates")

            def sum_f():
                pe.wait_ge(logf_done, 1)
                pe.wait_ge(ones_set, 1)
                pe.wait_ge(tables_in, 16 * 2)
                dst = take(6, "F")
                pe.matmul(dst[:, 0:TT * H], TRIU[:, :], LF[:, :, :].rearrange("p a b -> p (a b)"), start=True, stop=False)
                for back in range(1, TT):
                    last = pe.matmul(dst[:, back * H:TT * H], ONES[:, :], LF[:, 0:TT - back, :].rearrange("p a b -> p (a b)"),
                                     start=False, stop=back == TT - 1)
                give(last, "F")

            def g_rows():
                pe.wait_ge(g_done, 1)
                dst = take(7, "g_rows")
                for j in range(TT):
                    last = pe.transpose(dst[0:H, tile_of(j)], GG[:, j, :], IDENT[:, :])
                give(last, "g_rows")

            def m_columns():
                pe.wait_ge(m_done, 1)
                dst = take(7, "m_columns")
                for j in range(TT):
                    last = pe.transpose(dst[:, H * j:H * j + H], MROW[:, tile_of(j)], IDENT[0:H, 0:H])
                give(last, "m_columns")

            def mlstm_scores(h):
                pe.wait_ge(qk_done, 8)
                for i, b, c0 in ((0, 2, 0), (1, 3, 0), (3, 3, 384), (2, 4, 0)):
                    key = ("ms", h, b)
                    if i != 3:
                        take(b, key)
                    last = pe.matmul(bank[b][:, c0:c0 + S - i * P], QK[:, 4 + h, tile_of(i)], QK[:, h, i * P:S],
                                     start=True, stop=True)
                    if i != 1:
                        give(last, key)

            def mlstm_sums(h):
                for b in (2, 3, 4):
                    drained(pe, ("ms", h, b))
                if h == 0:
                    for j in range(TT):
                        drained(pe, ("tm", first["v"], j))
                pe.wait_ge(ones_set, 2)
                for j in range(TT):
                    key, c = ("num", h, j // 2), j % 2 * (P + 1)
                    if j % 2 == 0:
                        dst = take(5 + j // 2, key)
                    for i in range(j + 1):
                        w = ML_OFF[i] + (j - i) * P
                        last = pe.matmul(dst[:, c:c + P + 1], PP[h % 2][:, w:w + P], V[:, i, h, :], start=i == 0, stop=i == j)
                    if j % 2:
                        give(last, key)

            def mlstm_turn(h):
                pe.wait_ge(ml_h, h + 1)
                turn_four(lambda j: HM[h % 2][:, j, :], 7, ("hT", h))

            def mem_scores(j):
                if j == 0:
                    for c in range(H):
                        drained(pe, fm_key("qc", c))
                        drained(pe, fm_key("km", c))
                for i in range(2):
                    dst = take(2 + i, ("cs", j, i))
                    for h in (2 * i, 2 * i + 1):
                        q = (h % 2) * NMEM
                        last = pe.matmul(dst[:, q:q + NMEM], QC[:, h, tile_of(j)], KM[:, h, :], start=True, stop=True)
                    give(last, ("cs", j, i))

            def probs_turn(j):
                pe.wait_ge(probs_done, j + 1)
                for i in range(2):
                    turn_four(lambda q: PROB[j % 2][:, 2 * i + q // 2, tile_of(q % 2)], 4 + i, ("pT", j, i))

            def mem_values(j):
                for i in range(2):
                    drained(pe, ("pT", j, i))
                    drained(pe, ("tm", first["vm"], i))
                dst = take(6, ("yc", j))
                for h in range(H):
                    for m in range(MT):
                        last = pe.matmul(dst[:, tile_of(h)], VM[:, m, tile_of(h)], PT[j % 2][:, 2 * h + m, :],
                                         start=m == 0, stop=m == MT - 1)
                give(last, ("yc", j))

            def pool_mix():
                pe.wait_ge(poolw_in, 16)
                for g in range(4):
                    pe.wait_ge(pooled, g + 1)
                    dst = take(2 + g, ("pool", g))
                    give(pe.matmul(dst[:, :], POOLW[:, g, :], UP[:, g, PAD:PAD + S], start=True, stop=True), ("pool", g))

            def gate_logits():
                drained(pe, "thin_low")
                pe.wait_ge(gate2_lo, 1)
                for h in range(H):
                    dst = take(2 + h, ("lg", h))
                    give(pe.matmul(dst[:, :], WG2S[:, tile_of(h)], ALT[:, :], start=True, stop=True), ("lg", h))

            def gla_pairs(level, half):
                if level >= 0:
                    pe.wait_ge(lv_qk, 2 * (level + 1))
                elif half == 0:
                    for c in range(H):
                        drained(pe, fm_key("q2", c))
                        drained(pe, fm_key("k2", c))
                if level < 0:
                    for h in (2 * half, 2 * half + 1):
                        dst = take(6 + h % 2, ("lv", level, h))
                        for j in range(TT):
                            c = slice(h * S + j * P, h * S + j * P + P)
                            last = pe.matmul(dst[:, tile_of(j)], K2[:, c], Q2[:, c], start=True, stop=True)
                        give(last, ("lv", level, h))
                    return
                dst = take(6 + half, ("lv", level, half))
                for i in range(2 * TT):
                    c = half * 2 * TT + i
                    keys = P if level else P // 2
                    last = pe.matmul(dst[0:keys, i * P // 2:(i + 1) * P // 2], KE[:, c * P:c * P + keys], QEC[:, c * P // 2:(c + 1) * P // 2],
                                     start=True, stop=True)
                give(last, ("lv", level, half))

            def kdec_turn():
                pe.wait_ge(kd_done, 1)
                for h in range(H):
                    turn_four(lambda j: KE[:, h * S + j * P:h * S + j * P + P], 2 + h, ("kdT", h))

            def gla_out(j):
                if j == 0:
                    for h in range(H):
                        drained(pe, ("kdT", h))
                    pe.wait_ge(qcum_done, 1)
                else:
                    drained(pe, ("kv", j - 1, 0))
                    drained(pe, ("kv", j - 1, 1))
                pe.wait_ge(chunk_lo, 2 * (j + 1))
                for i in range(2):
                    dst = take(2 + i, ("o2", j, i))
                    for h in (2 * i, 2 * i + 1):
                        c, v = slice((h % 2) * DV, (h % 2 + 1) * DV), slice(h * DV, h * DV + DV)
                        last = three(dst[:, c], SCH[:, h, j, :], SCL[:, h, j, :], V2H[:, j, v], V2L[:, j, v], True, j == 0)
                        if j:
                            last = pe.matmul(dst[:, c], QE[:, h * S + j * P:h * S + j * P + P], STATE[:, h, :],
                                             start=False, stop=True)
                    give(last, ("o2", j, i))
                if j < TT - 1:
                    for i in range(2):
                        dst = take(4 + i, ("kv", j, i))
                        for h in (2 * i, 2 * i + 1):
                            c, v = slice((h % 2) * DV, (h % 2 + 1) * DV), slice(h * DV, h * DV + DV)
                            last = three(dst[:, c], KDTH[:, h, j, :], KDTL[:, h, j, :], V2H[:, j, v], V2L[:, j, v], True, True)
                        give(last, ("kv", j, i))

            def gla_turn(j):
                for i in range(2):
                    drained(pe, ("o2", j, i))
                for i in range(2):
                    turn_four(lambda c: OJ[:, tile_of(4 * i + c)], 6 + i, ("oT", j, i))

            def ws_turn():
                pe.wait_ge(ws_in, 16)
                for i in range(2):
                    turn_four(lambda g: WSR[:, 4 * i + g, :], i, ("wsT", i))

            def sg_mix(i):
                if i == 0:
                    pe.wait_ge(vh_ready, TT)
                    drained(pe, ("wsT", 0))
                    drained(pe, ("wsT", 1))
                for g in (2 * i, 2 * i + 1):
                    dst = take(2 + g % 2, ("sg", g))
                    for j in range(TT):
                        last = pe.matmul(dst[:, tile_of(j)], VH[:, j, tile_of(g)], WST[:, g, :], start=True, stop=True)
                    give(last, ("sg", g))

            def turn_row(name, done, j):
                pe.wait_ge(done, j + 1)
                for i in range(2):
                    turn_four(lambda c: RES[:, j, tile_of(4 * i + c)], 6 + i, (name, j, i))

            def side(n):
                turn_x(TURN_X.get(n, ()))
                if n == GATES: thin(0, "thin_gates", lambda k: drained(pe, ("xT", k)))
                if n == LOW: thin(1, "thin_low")
                if n == GATES + 1: gates()
                if n == GATES + 5: sum_f()
                if n == GATES + 6: g_rows()
                if n == GATES + 7: m_columns()
                if 0 <= n - ML < H: mlstm_scores(n - ML)
                if 0 <= n - ML - 1 < H: mlstm_sums(n - ML - 1)
                if 0 <= n - ML - 2 < H: mlstm_turn(n - ML - 2)
                if 0 <= n - AT - 2 < TT: mem_values(n - AT - 2)
                if 0 <= n - AT < TT: mem_scores(n - AT)
                if 0 <= n - AT - 1 < TT: probs_turn(n - AT - 1)
                if n == WO - 1: pool_mix()
                if n == LG: gate_logits()
                if n == LV + 4: ws_turn()
                if 0 <= n - LV < 2 * (LEVELS + 1): gla_pairs((n - LV) // 2 - 1, (n - LV) % 2)
                if 0 <= n - SG < 4: sg_mix(n - SG)
                if n == GO - 1: kdec_turn()
                if 0 <= n - GO - 1 < TT: gla_turn(n - GO - 1)
                if 0 <= n - GO < TT: gla_out(n - GO)

            warm_up()
            turn_mem()
            for n in range(ff1_0):
                name, i = name_of(n)
                if n not in MID:
                    side(n)
                if n + 1 in PAIRED:
                    pass
                elif n == WO + 5:
                    tm_pair(n, 3, 4, 2, lambda j: turn_row("x1T", x1_done, j), {(0, 2): 0, (1, 2): 1})
                elif n == WO2 + 3:
                    tm_pair(n, 2, E_WO2 + 2, 3, lambda j: turn_row("h1T", h1_done, j), {(0, 2): 0, (0, 3): 1})
                elif n == WO + 6:
                    fm_block_by_halves(n, "x1T", x1_done, {(0, 0): 2, (1, 3): 3})
                elif n == 0:
                    first_block()
                elif name == "km":
                    fm_block(n, MEMH, MEML, NMEM)
                elif name == "vm":
                    tm_block(n, i, 2, resident(MEMH, MEML, i), MT)
                elif name in ("w_out", "w_out2"):
                    g = len(WO_GROUPS) if name == "w_out" else 2
                    pe.wait_ge(x_lo, i + 1 + (0 if name == "w_out" else E_WO2))
                    tm_block(n, i % g, g, staged(i % 2))
                elif blocks[n][0] == "tm":
                    tm_block(n, i % 2, 2, resident(TH, TL, i % 2), between=(lambda: side(n)) if n in MID else None)
                else:
                    fm_block(n, TH, TL, between=(lambda: side(n)) if n in MID else None)

            fm_block_by_halves(ff1_0, "h1T", h1_done, {(0, 7): 2, (1, 5): 3})
            fm_block(ff1_0 + 1, TH, TL)
            u0 = list(uses)
            with pe.Fori(0, 7) as i:
                for b in range(2):
                    n = ff1_0 + 2 + b
                    wh, wlo = weights(n, (WH, WL))
                    pe.wait_ge(w_lo, i * 2 + (n + 1))
                    for t in range(2):
                        pe.wait_ge(bank_free[t], i * 2 + (u0[t] + b))
                        for k in range(KC):
                            last = three(bank[t][:, :], wh[:, k, tile_of(t)], wlo[:, k, tile_of(t)], TH[:, k, :], TL[:, k, :],
                                         k == 0, k == KC - 1)
                        last.then_inc(bank_full[t], 1)
            for n in range(14):
                for t in range(2):
                    turn["fm", ff1_0 + 2 + n, t] = (t, u0[t] + n)
                block_done[ff1_0 + 2 + n] = (bank_full[1], u0[1] + n + 1)
            uses[0] += 14
            uses[1] += 14

            for half in range(2):
                n0, e0, used0 = ff2_0 + 8 * half, E_FF2 + 8 * half, n_used[0]

                def group(g, more=0):
                    wh, wlo = weights(n0 + g, (WH, WL))
                    lhs = staged(g % 2)
                    pe.wait_ge(w_lo, more + (n0 + g + 1))
                    pe.wait_ge(x_lo, more + (e0 + g + 1))
                    for j in range(TT):
                        key = ("tm", n0, j)
                        if g == 0:
                            take(2 + j, key)
                        for kk in range(4):
                            h, l = lhs(kk)
                            last = three(bank[2 + j][:, :], h[:, tile_of(j)], l[:, tile_of(j)], wh[:, kk, :], wlo[:, kk, :],
                                         g == 0 and kk == 0, g == 7 and kk == 3)
                        if g == 7:
                            give(last, key)
                    if g < 7:
                        last.then_inc(w_used, 1)

                group(0)
                group(1)
                with pe.Fori(0, 2) as i:
                    group(2, i * 2)
                    group(3, i * 2)
                for g in range(7):
                    block_done[n0 + g] = (w_used, used0 + g + 1)
                if half == 0:
                    group(6)
                    group(7)
                    n_used[0] += 7
                    block_done[n0 + 7] = (bank_full[5], turn["tm", n0, 3][1] + 1)
                else:
                    n_used[0] += 6
                    tm_pair(n0 + 7, 8, e0 + 6, 3)

        f0 = [turn["fm", ff1_0, t][1] for t in range(2)]

        @block.scalar
        def _(act):
            links = [0]

            def link(ins):
                links[0] += 1
                ins.then_inc(act_chain, 1)
                act.wait_ge(act_chain, links[0])

            def split(n, loads=0, more=0):
                w = blocks[n][2].shape[1] * blocks[n][2].shape[2]
                act.wait_ge(w_loaded[n % 2], loads + 16 * (n // 2 + 1))
                if n >= 2 and slot_of(n) != 2:
                    s, v = block_done[n - 2]
                    act.wait_ge(s, more + v)
                c0 = w // 2 if n in (1, 2) else 0
                if c0:
                    act.activation(WH[n % 2][:, 0:c0], RAW[n % 2][:, 0:c0], ACT.Copy).then_inc(w_half_hi, 1)
                act.activation(WH[slot_of(n)][:, c0:w], RAW[n % 2][:, c0:w], ACT.Copy).then_inc(w_hi, 1)

            def split_x(slot, src):
                act.activation(XH[slot][:, :], src, ACT.Copy).then_inc(x_hi, 1)

            def load_constants():
                act.dma_start(IDENT[:, :], a["c_ident"]).then_inc(ident_in, 16)
                act.dma_start(VC[:, :], a["vector_columns"]).then_inc(columns_in, 16)

            def mean_squares(dst, src, c, before=0):
                if before:
                    act.wait_ge(squared, before)
                act.activation(dst, src, ACT.Square, scale=1 / 32, accum_out=SSQ[:, c:c + 1]).then_inc(squared, 1)

            def gates_softplus():
                drained(act, "gates")
                link(act.activation(GT1[:, :, :], G8[:, :, H:2 * H], ACT.Abs))
                link(act.activation(GT1[:, :, :], GT1[:, :, :], ACT.Exp, scale=-1.0))
                act.activation(GT1[:, :, :], GT1[:, :, :], ACT.Ln, bias=1.0).then_inc(softplus_done, 1)

            def den_floor():
                drained(act, "m_columns")
                act.activation(FLOOR[:, :, :], FLOOR[:, :, :], ACT.Exp, scale=-1.0).then_inc(floor_done, 1)

            def mlstm_exp(h):
                act.wait_ge(ml_arg, h + 1)
                act.activation(PP[h % 2][:, :], PP[h % 2][:, :], ACT.Exp, scale=-1.0).then_inc(ml_exp, 1)

            def softmax_exp(j):
                act.wait_ge(max_done, j + 1)
                for h in range(H):
                    b = full(act, ("cs", j, h // 2))
                    ins = act.activation(PROB[j % 2][:, h, :], b[:, (h % 2) * NMEM:(h % 2 + 1) * NMEM], ACT.Exp,
                                         bias=SMX[:, h:h + 1], scale=SCALE, accum_out=SSUM[:, h:h + 1])
                    if h % 2:
                        free(ins, ("cs", j, h // 2))

            def probs_copy(j):
                for i in range(2):
                    b = full(act, ("pT", j, i))
                    free(act.activation(PT[j % 2][:, 4 * i:4 * i + 4, :], quarters(b[:, :]), ACT.Copy), ("pT", j, i))

            def logits_softplus():
                for f, kw in ((ACT.Abs, None), (ACT.Exp, {"scale": -1.0}), (ACT.Ln, {"bias": 1.0})):
                    for h in range(H):
                        b = full(act, ("lg", h))
                        if f == ACT.Abs:
                            act.wait_ge(lg_min, h + 1)
                        ins = act.activation(b[:, :], b[:, :], f, **(kw or {"bias": col(C_GATE2 + h)}))
                        if f == ACT.Ln:
                            ins.then_inc(lg_softplus, 1)
                    if f != ACT.Ln:
                        link(ins)

            def level_exp(l):
                act.wait_ge(lv_arg, 2 * (l + 1))
                act.activation(EE[:, :], EE[:, :], ACT.Exp, scale=1 / TEMP).then_inc(lv_exp, 1)

            def chunk_split(j):
                act.activation(V2H[:, j, :], V2[:, j, :], ACT.Copy).then_inc(chunk_hi, 1)
                act.activation(SCH[:, :, j, :], SC[:, j::TT, :], ACT.Copy).then_inc(chunk_hi, 1)

            def squares_o(j):
                if j:
                    full(act, ("oT", j - 1, 1))
                for h in range(H):
                    b = full(act, ("o2", j, h // 2))
                    act.activation(OJ[:, h * DV:h * DV + DV], b[:, (h % 2) * DV:(h % 2 + 1) * DV], ACT.Square,
                                   scale=1 / 16, accum_out=SSQ[:, 10 + h:11 + h]).then_inc(squared, 1)

            def rows_hi(name, j):
                for i in range(2):
                    b = full(act, (name, j, i))
                    act.activation(TH[:, 4 * i:4 * i + 4, tile_of(j)], quarters(b[:, :]), ACT.Copy).then_inc(t_hi, 1)

            def side(n):
                if n == 0:
                    for j in range(TT):
                        act.wait_ge(x_in[j], 16)
                        mean_squares(XN[:, j, :], RES[:, j, :], MT + j)
                if n in (2, first["u"]):
                    i = 0 if n == 2 else 1
                    act.wait_ge(thin_in, 16 * (i + 1))
                    w = THIN_W[i][:, :, :, 0:THIN]
                    act.activation(w, THIN_RAW[:, :, :].unsqueeze(2).to_broadcast(w.shape), ACT.Copy).then_inc(thin_hi, 1)
                for c in TURN_X.get(n, ()):
                    b = full(act, ("xT", c))
                    act.activation(TH[:, c, :], b[:, :], ACT.Copy, scale=col(C_NORM + c)).then_inc(t_hi, 1)
                if n == LOW:
                    act.wait_ge(wg2_in, 16 * STACK // THIN)
                    act.activation(WG2S[:, :], WG2[:, :], ACT.Copy).then_inc(gate2_hi, 1)
                    b = full(act, "thin_low")
                    act.activation(ALT[:, :], b[0:STACK, :], ACT.Identity, bias=VC[0:STACK, C_LOW:C_LOW + 1]).then_inc(low_hi, 1)
                if n == GATES + 4: gates_softplus()
                if n == GATES + 8: den_floor()
                if 0 <= n - ML < H: mlstm_exp(n - ML)
                if 0 <= n - AT - 1 < TT: probs_copy(n - AT - 1)
                if 0 <= n - AT < TT: softmax_exp(n - AT)
                if n == LG: logits_softplus()
                if 0 <= n - LV < 2 * LEVELS and (n - LV) % 2 == 0: level_exp((n - LV) // 2)
                if n == GO - 3:
                    act.wait_ge(lv_qk, 2 * LEVELS)
                    act.activation(ETOT[:, :], CUM[:, :].rearrange("p (c t) -> p c t", t=P)[:, :, P - 1], ACT.Exp,
                                   scale=1 / TEMP).then_inc(etot_done, 1)
                    act.activation(EE[:, :], CUM[:, :], ACT.Exp, scale=1 / TEMP).then_inc(qc_exp, 1)
                if n == GO - 2:
                    act.wait_ge(kd_arg, 1)
                    act.activation(EE[:, :], EE[:, :], ACT.Exp, scale=1 / TEMP).then_inc(kd_exp, 1)
                if n == GO - 1:
                    act.wait_ge(kd_done, 1)
                    chunk_split(0)
                    chunk_split(1)
                    for h in range(H):
                        b = full(act, ("kdT", h))
                        act.activation(KDTH[:, h, :, :], quarters(b[:, :]), ACT.Copy).then_inc(kdt_hi, 1)
                if 0 <= n - GO < TT:
                    squares_o(n - GO)
                    if n - GO + 2 < TT:
                        chunk_split(n - GO + 2)

            def drain(n):
                name, i = name_of(n)
                fm = [(("fm", n, t), 2 * i + t) for t in range(2)]
                if name == "km":
                    for key, c in fm:
                        b = full(act, key)
                        free(act.activation(KM[:, c, :], b[:, 0:NMEM], ACT.Copy), key)
                if name in ("vm", "v", "o") and i == 1:
                    dst, f = {"vm": (VM, ACT.Copy), "v": (V, ACT.Copy), "o": (O, ACT.Sigmoid)}[name]
                    for j in range(MT if name == "vm" else TT):
                        b = full(act, ("tm", n - 1, j))
                        to, src = (dst[:, j, :, 0:P], quarters(b[:, :])) if name == "v" else (dst[:, j, :], b[:, :])
                        free(act.activation(to, src, f), ("tm", n - 1, j))
                if name in ("q", "k"):
                    c0 = 4 if name == "k" else 0
                    for key, c in fm:
                        b = full(act, key)
                        act.activation(QK[:, c0 + c, :], b[:, :], ACT.Identity, bias=col(C_CB + c0 + c),
                                       scale=col(C_CW + 24 + c0 + c)).then_inc(conv_first, 1)
                    for key, c in fm:
                        drained(act, key)
                        act.activation(QK[:, c0 + c, :], QK[:, c0 + c, :], ACT.Silu).then_inc(qk_done, 1)
                to = {"qc": lambda c: QC[:, c, :], "u": lambda c: UP[:, c, PAD:PAD + S], "z_a": lambda c: Y[:, c, :],
                      "z_b": lambda c: Y[:, 4 + c, :], "z_c": lambda c: Y[:, 8 + c, :]}.get(name)
                if to:
                    for key, c in fm:
                        b = full(act, key)
                        free(act.activation(to(c), b[:, :], ACT.Silu if name[0] == "z" else ACT.Copy), key)
                if name == "w_out" and i == 5:
                    def squares(j):
                        drained(act, ("tm", n - 2, j))
                        mean_squares(SINK[:, :], RES[:, j, :], 6 + j, MT + TT + j)

                    squares(0)
                    squares(1)
                    rows_hi("x1T", 0)
                    squares(2)
                    rows_hi("x1T", 1)
                    squares(3)
                    rows_hi("x1T", 2)
                    rows_hi("x1T", 3)
                if name == "a_v" and i % 2:
                    h = slice(i // 2 * 512, i // 2 * 512 + 512)
                    for j in range(TT):
                        drained(act, ("tm", n - 1, j))
                        act.activation(VH[:, j, h], VH[:, j, h], ACT.Gelu_apprx_tanh).then_inc(av_gelu, 1)
                if name in ("a_u", "g_a", "r", "g_b"):
                    for key, c in fm:
                        b = full(act, key)
                        if name == "a_u":
                            free(act.activation(U[:, c, :], b[:, :], ACT.Gelu_apprx_tanh, bias=col(C_B2 + c)), key)
                        if name == "g_a":
                            act.activation(b[:, :], b[:, :], ACT.Sigmoid, bias=col(C_B2G + c)).then_inc(ga_sig, 1)
                        if name == "r":
                            if c == 0:
                                full(act, ("sg", 7))
                            free(act.activation(R[:, c, :], b[:, :], ACT.Silu, bias=col(C_B2 + 32 + c)), key)
                        if name == "g_b":
                            act.activation(b[:, :], b[:, :], ACT.Sigmoid, bias=col(C_B2G + 8 + c)).then_inc(gb_sig, 1)
                if name == "w_out2" and i == 3:
                    for j in range(TT):
                        rows_hi("h1T", j)

            def stage(n):
                if n + 1 >= ff1_0:
                    return
                name, i = name_of(n + 1)
                if name == "w_out":
                    if i == 0: drained(act, ("hT", H - 1))
                    if i == 1: drained(act, ("yc", TT - 1))
                    if i == 2: act.wait_ge(yb_done, 4)
                    g, src = WO_GROUPS[i % 3], Y
                elif name == "w_out2":
                    act.wait_ge(m_ready, 4 if i == 0 else 8)
                    g, src = i % 2, R
                else:
                    return
                slot = OWN.get(n + 1, i % 2)
                if i >= 2 and slot < 2:
                    act.wait_ge(*block_done[n - 1])
                split_x(slot, src[:, 4 * g:4 * g + 4, :].rearrange("p a b -> p (a b)"))

            load_constants()
            act.wait_ge(ones_set, 1)
            act.activation(SSUM[:, 0:1], ONES[:, 0:1], ACT.Square)
            for j in range(MT):
                act.wait_ge(mem_in[j], 16)
                mean_squares(SINK[:, :], MEM[:, j, :], j, j)
            act.wait_ge(w0_loaded, 16)
            act.activation(WH[0][:, 0:1024], RAW[0][:, 0:1024], ACT.Copy).then_inc(w_hi, 1)
            act.wait_ge(columns_in, 16)
            for c in range(KC):
                if c == KC // 2:
                    act.wait_ge(w_loaded[0], 16)
                    act.activation(WH[0][:, 1024:], RAW[0][:, 1024:], ACT.Copy).then_inc(w0_hi, 1)
                full(act, ("memT", c // 2))
                q = (c % 2) * NMEM
                act.activation(MEMH[:, c, :], bank[4 + c // 2][:, q:q + NMEM], ACT.Copy, scale=col(C_MEMN + c)).then_inc(t_hi, 1)
            for n in range(ff1_0):
                split(n + 1)
                side(n)
                if n + 1 not in PAIRED:
                    stage(n)
                if n + 2 in PAIRED:
                    stage(n + 1)
                drain(n)

            def relus(m, group, more=0):
                for t in range(2):
                    act.wait_ge(bank_full[t], more + (f0[t] + m + 1))
                    q = (2 * m + t) % 4 * S
                    act.activation(F1[:, group, q:q + S], bank[t][:, :], ACT.Relu).then_inc(bank_free[t], 1)

            split(ff1_0 + 1)
            relus(0, 0)
            with act.Fori(0, 7) as i:
                split(ff1_0 + 2, i * 16, i * 2)
                relus(1, i, i * 2)
                split(ff1_0 + 3, i * 16, i * 2)
                relus(2, i + 1, i * 2)
            split(ff2_0)
            act.wait_ge(f1_done, 4)
            act.wait_ge(*block_done[WO2 + 2])
            split_x(0, F1[:, 0, :])
            relus(15, 7)

            act.wait_ge(f1_done, 32)
            for half in range(2):
                n0 = ff2_0 + 8 * half
                for g in (1, 2):
                    split(n0 + g)
                    if n0 + g == ff2_0 + 1:
                        act.wait_ge(*block_done[WO2 + 3])
                    split_x(g % 2, F1[:, g, :])
                with act.Fori(0, 2) as i:
                    for g in (3, 4):
                        split(n0 + g, i * 16, i * 2)
                        split_x(g % 2, F1[:, i * 2 + g, :])
                if half == 0:
                    split(n0 + 7)
                    split_x(1, F1[:, 7, :])
                    split(n0 + 8)
                    split_x(0, F1[:, 0, :])
                else:
                    act.wait_ge(x_lo, E_FF2 + 10)
                    split_x(3, F1[:, 7, :])
                    split(n0 + 7)

        @block.vector
        def _(dve):
            links = [0]

            def link(ins):
                links[0] += 1
                ins.then_inc(dve_chain, 1)
                dve.wait_ge(dve_chain, links[0])

            def lower(dst, src, hi):
                return dve.tensor_tensor(dst, src, hi.bitcast(f32), ALU.subtract)

            def split(n, more=0):
                if n - 1 in PAIRED:
                    return
                w = blocks[n][2].shape[1] * blocks[n][2].shape[2]
                c0 = w // 2 if n in (1, 2) else 0
                if c0:
                    dve.wait_ge(w_half_hi, n)
                    lower(WL[n % 2][:, 0:c0], RAW[n % 2][:, 0:c0], WH[n % 2][:, 0:c0])
                dve.wait_ge(w_hi, more + (n + 1))
                if n - 2 in PAIRED:
                    dve.wait_ge(own_lo, 1 + PAIRED.index(n - 2))
                    lower(WL[slot_of(n)][:, 0:w], RAW[n % 2][:, 0:w], WH[slot_of(n)][:, 0:w]).then_inc(w_lo, 2)
                    return
                lower(WL[slot_of(n)][:, c0:w], RAW[n % 2][:, c0:w], WH[slot_of(n)][:, c0:w]).then_inc(w_lo, 1)

            def split_x(slot, e, src, more=0):
                dve.wait_ge(x_hi, more + (e + 1))
                lower(XL[slot][:, :], src, XH[slot][:, :]).then_inc(x_lo, 1)

            def gates_logf():
                parts = full(dve, "gates")[:, 0:TT * 2 * THIN].rearrange("p (a b) -> p a b", a=TT)
                link(dve.tensor_copy(G8[:, :, :], parts[:, :, 0:2 * H]))
                free(dve.tensor_tensor(G8[:, :, :], G8[:, :, :], parts[:, :, THIN:THIN + 2 * H], ALU.add), "gates")
                drained(dve, "gates")
                link(dve.tensor_scalar(LF[:, :, :], G8[:, :, H:2 * H], 0.0, None, ALU.min))
                dve.wait_ge(softplus_done, 1)
                dve.tensor_tensor(LF[:, :, :], LF[:, :, :], GT1[:, :, :], ALU.subtract).then_inc(logf_done, 1)

            def gates_g():
                b = full(dve, "F")
                free(dve.tensor_copy(FS[:, :, :], b[:, 0:TT * H].rearrange("p (a b) -> p a b", a=TT)), "F")
                drained(dve, "F")
                dve.tensor_tensor(GG[:, :, :], G8[:, :, 0:H], FS[:, :, :], ALU.subtract).then_inc(g_done, 1)

            def running_max():
                b = full(dve, "g_rows")
                free(dve.tensor_copy(GROW[:, :], b[0:H, :]), "g_rows")
                drained(dve, "g_rows")
                dve.tensor_tensor_scan(MROW[:, :], GROW[:, :], GROW[:, :], 0.0, ALU.max, ALU.max).then_inc(m_done, 1)

            def m_sum():
                b = full(dve, "m_columns")
                free(dve.tensor_tensor(FLOOR[:, :, :], FS[:, :, :], b[:, 0:TT * H].rearrange("p (a b) -> p a b", a=TT),
                                       ALU.add), "m_columns")

            def conv_taps(c, key):
                dve.wait_ge(conv_first, c + 1)
                b = full(dve, key)
                for back in (1, 2, 3):
                    ins = dve.scalar_tensor_tensor(QK[:, c, back:S], b[:, 0:S - back], col(C_CW + 8 * (3 - back) + c),
                                                   QK[:, c, back:S], ALU.mult, ALU.add)
                    if back < 3:
                        link(ins)
                free(ins, key)

            def mlstm_weights(h):
                p = PP[h % 2]
                dve.wait_ge(mb_in, 16)
                for i in range(TT):
                    w = S - i * P
                    ins = dve.tensor_scalar(p[:, ML_OFF[i]:ML_OFF[i] + w], MB[:, h, i * P:S], GG[:, i, h:h + 1], 0.0,
                                            ALU.subtract, ALU.max)
                ins.then_inc(ml_arg, 1)
                dve.wait_ge(ml_exp, h + 1)
                for i in range(TT):
                    c = slice(ML_OFF[i], ML_OFF[i] + P)
                    ins = dve.tensor_tensor(p[:, c], p[:, c], TRIU[:, :], ALU.mult)
                link(ins)
                for i, b, c0 in ((0, 2, 0), (1, 3, 0), (3, 3, 384), (2, 4, 0)):
                    full(dve, ("ms", h, b))
                    w = S - i * P
                    c = slice(ML_OFF[i], ML_OFF[i] + w)
                    ins = dve.scalar_tensor_tensor(p[:, c], bank[b][:, c0:c0 + w], SCALE, p[:, c], ALU.mult, ALU.mult)
                    if i != 1:
                        free(ins, ("ms", h, b))

            def mlstm_out(h):
                hm = HM[h % 2]
                if h == 0:
                    dve.wait_ge(floor_done, 1)
                    for j in range(TT):
                        drained(dve, ("tm", first["o"], j))
                sums = [full(dve, ("num", h, i))[:, 0:2 * (P + 1)].rearrange("p (a b) -> p a b", a=2) for i in range(2)]
                for i in range(2):
                    ins = dve.tensor_scalar(RDEN[:, 2 * i:2 * i + 2], sums[i][:, :, P], -1.0, None, ALU.mult)
                link(ins)
                for i in range(2):
                    ins = dve.tensor_tensor(RDEN[:, 2 * i:2 * i + 2], sums[i][:, :, P], RDEN[:, 2 * i:2 * i + 2], ALU.max)
                link(ins)
                link(dve.tensor_tensor(RDEN[:, :], RDEN[:, :], FLOOR[:, :, h], ALU.max))
                link(dve.reciprocal(RDEN[:, :], RDEN[:, :]))
                for i in range(2):
                    free(dve.tensor_tensor(hm[:, 2 * i:2 * i + 2, :], sums[i][:, :, 0:P],
                                           RDEN[:, 2 * i:2 * i + 2].unsqueeze(2).to_broadcast([P, 2, P]), ALU.mult), ("num", h, i))
                drained(dve, ("num", h, 0))
                drained(dve, ("num", h, 1))
                link(dve.tensor_tensor(hm[:, :, :], hm[:, :, :], O[:, :, tile_of(h)], ALU.mult))
                link(dve.tensor_tensor(SQ[:, :, :], hm[:, :, :], hm[:, :, :], ALU.mult))
                dve.tensor_reduce(SSQ[:, 10:14], SQ[:, :, :], AX.X, ALU.add).then_inc(ml_ss, 1)
                dve.wait_ge(rstd_done, MT + TT + h + 1)
                dve.tensor_tensor(hm[:, :, :], hm[:, :, :], RST[:, 10:14].unsqueeze(2).to_broadcast([P, TT, P]),
                                  ALU.mult).then_inc(ml_h, 1)

            def mlstm_y(h):
                b = full(dve, ("hT", h))
                drained(dve, fm_key("z_a", h))
                free(dve.scalar_tensor_tensor(Y[:, h, :], b[:, :], col(C_MN + h), Y[:, h, :], ALU.mult, ALU.mult), ("hT", h))

            def softmax(j):
                for i in range(2):
                    b = full(dve, ("cs", j, i))
                    ins = dve.tensor_reduce(SMX[:, 2 * i:2 * i + 2], b[:, :].rearrange("p (a b) -> p a b", a=2), AX.X,
                                            ALU.max, negate=True)
                link(ins)
                dve.tensor_scalar(SMX[:, :], SMX[:, :], SCALE, None, ALU.mult).then_inc(max_done, 1)
                drained(dve, ("cs", j, 0))
                drained(dve, ("cs", j, 1))
                link(dve.reciprocal(SSUM[:, :], SSUM[:, :]))
                dve.tensor_tensor(PROB[j % 2][:, :, :], PROB[j % 2][:, :, :],
                                  SSUM[:, :].unsqueeze(2).to_broadcast([P, H, NMEM]), ALU.mult).then_inc(probs_done, 1)

            def mem_y(j):
                if j == 0:
                    for c in range(H):
                        drained(dve, fm_key("z_c", c))
                b = full(dve, ("yc", j))
                y = Y[:, 8:12, tile_of(j)]
                free(dve.tensor_tensor(y, quarters(b[:, :]), y, ALU.mult), ("yc", j))

            def pool_window(g):
                drained(dve, fm_key("u", g))
                if g:
                    dve.wait_ge(pooled, g)
                src, w = UP[:, g, :], 1
                while w < WINDOWS[g]:
                    dst = PW[w.bit_length() % 2][:, :]
                    link(dve.tensor_tensor(dst[:, PAD:], src[:, PAD:], src[:, PAD - w:PAD + S - w], ALU.add))
                    src, w = dst, 2 * w
                edge, rest = slice(PAD, PAD + 16), slice(PAD + 16, PAD + S)
                link(dve.tensor_tensor(src[:, edge], src[:, edge], PINV[:, g, :], ALU.mult))
                link(dve.tensor_tensor(UP[:, g, edge], src[:, edge], UP[:, g, edge], ALU.subtract))
                dve.scalar_tensor_tensor(UP[:, g, rest], src[:, rest], 1 / w, UP[:, g, rest], ALU.mult,
                                         ALU.subtract).then_inc(pooled, 1)

            def pool_scaled():
                for g in range(4):
                    b = full(dve, ("pool", g))
                    free(dve.tensor_scalar(UP[:, g, PAD:PAD + S], b[:, :], col(C_PS + g), None, ALU.mult), ("pool", g))

            def pool_y():
                for g in range(4):
                    drained(dve, ("pool", g))
                    drained(dve, fm_key("z_b", g))
                    dve.tensor_tensor(Y[:, 4 + g, :], Y[:, 4 + g, :], UP[:, g, PAD:PAD + S], ALU.mult).then_inc(yb_done, 1)

            def logits_min():
                for h in range(H):
                    b = full(dve, ("lg", h))
                    dve.tensor_scalar(LF2[:, h, :], b[:, :], col(C_GATE2 + h), 0.0, ALU.add, ALU.min).then_inc(lg_min, 1)

            def logits_cum():
                for h in range(H):
                    dve.wait_ge(lg_softplus, h + 1)
                    for j in range(TT):
                        ins = dve.tensor_tensor_scan(CUM[:, h * S + j * P:h * S + j * P + P], LF2[:, h, tile_of(j)],
                                                     bank[turn["lg", h][0]][:, tile_of(j)], 0.0, ALU.add, ALU.subtract)
                    free(ins, ("lg", h))

            def level_views(l):
                half = P >> (l + 1)
                return half, slice(0, half), slice(half, 2 * half), lambda t: t[:, :].rearrange("p (b t) -> p b t", t=2 * half)

            def level_args(l):
                half, left, right, view = level_views(l)
                cum, ee = view(CUM), view(EE)
                mid = cum[:, :, half - 1:half].to_broadcast([P, H * S // (2 * half), half])
                if l == 0:
                    for h in range(H):
                        drained(dve, ("lg", h))
                else:
                    dve.wait_ge(lv_qk, 2 * l)
                dve.tensor_tensor(ee[:, :, right], cum[:, :, right], mid, ALU.subtract).then_inc(lv_arg, 1)
                dve.tensor_tensor(ee[:, :, left], mid, cum[:, :, left], ALU.subtract).then_inc(lv_arg, 1)

            def level_operands(l):
                half, left, right, view = level_views(l)
                if l == 0:
                    dve.wait_ge(zeros_set, 2)
                dve.wait_ge(lv_exp, l + 1)
                dve.tensor_tensor(QEC[:, :].rearrange("p (b t) -> p b t", t=half), view(Q2)[:, :, right], view(EE)[:, :, right],
                                  ALU.mult).then_inc(lv_qk, 1)
                dve.tensor_tensor(view(KE)[:, :, left], view(K2)[:, :, left], view(EE)[:, :, left], ALU.mult).then_inc(lv_qk, 1)

            def level_merge(l, pair):
                if l < 0:
                    dve.wait_ge(masks_set, 1)
                    dve.wait_ge(zeros_set, 2)
                    mask = MASK[:, LEVELS, :].unsqueeze(1).to_broadcast([P, TT, P])
                    for h in (2 * pair, 2 * pair + 1):
                        b = full(dve, ("lv", l, h))
                        free(dve.copy_predicated(SC[:, h * TT:h * TT + TT, :], mask, quarters(b[:, :])), ("lv", l, h))
                    return
                half, left, right, view = level_views(l)
                nb = P // (2 * half)
                b = full(dve, ("lv", l, pair))
                if l == 0:
                    free(dve.tensor_copy(SC[0:half, 2 * TT * pair:2 * TT * (pair + 1), right],
                                         b[0:half, :].rearrange("p (c t) -> p c t", t=half)), ("lv", l, pair))
                    return
                to = SC[:, 2 * TT * pair:2 * TT * (pair + 1), :].rearrange("p c (b t) -> p c b t", t=2 * half)[:, :, :, right]
                mask = MASK[:, l, :].rearrange("p (b t) -> p b t", t=2 * half)[:, :, right]
                free(dve.copy_predicated(to, mask.unsqueeze(1).to_broadcast([P, 2 * TT, nb, half]),
                                         b[:, :].rearrange("p (c b t) -> p c b t", c=2 * TT, t=half)), ("lv", l, pair))

            def q_cum():
                dve.wait_ge(qc_exp, 1)
                dve.tensor_tensor(QE[:, :], Q2[:, :], EE[:, :], ALU.mult).then_inc(qcum_done, 1)

            def k_dec():
                dve.wait_ge(qcum_done, 1)
                cum = CUM[:, :].rearrange("p (c t) -> p c t", t=P)
                dve.tensor_tensor(EE[:, :].rearrange("p (c t) -> p c t", t=P), cum[:, :, P - 1:P].to_broadcast([P, H * TT, P]),
                                  cum, ALU.subtract).then_inc(kd_arg, 1)
                dve.wait_ge(kd_exp, 1)
                dve.tensor_tensor(KE[:, :], K2[:, :], EE[:, :], ALU.mult).then_inc(kd_done, 1)

            def chunk_split(j):
                dve.wait_ge(chunk_hi, 2 * j + 1)
                lower(V2L[:, j, :], V2[:, j, :], V2H[:, j, :]).then_inc(chunk_lo, 1)
                dve.wait_ge(chunk_hi, 2 * j + 2)
                lower(SCL[:, :, j, :], SC[:, j::TT, :], SCH[:, :, j, :]).then_inc(chunk_lo, 1)

            def k_dec_lower():
                full(dve, ("kdT", H - 1))
                for h in range(H):
                    dve.wait_ge(kdt_hi, h + 1)
                    b = full(dve, ("kdT", h))
                    free(lower(KDTL[:, h, :, :], quarters(b[:, :]), KDTH[:, h, :, :]), ("kdT", h))

            def gla_norm(j):
                dve.wait_ge(rstd_done, MT + TT + H + TT + TT + j + 1)
                for i in range(2):
                    b = full(dve, ("o2", j, i))
                    free(dve.tensor_tensor(OJ[:, 512 * i:512 * i + 512].rearrange("p (a b) -> p a b", a=2),
                                           b[:, :].rearrange("p (a b) -> p a b", a=2),
                                           RST[:, 10 + 2 * i:12 + 2 * i].unsqueeze(2).to_broadcast([P, 2, DV]),
                                           ALU.mult), ("o2", j, i))
                if j < TT - 1:
                    dve.wait_ge(etot_done, 1)
                    for h in range(H):
                        b = full(dve, ("kv", j, h // 2))
                        src = b[:, (h % 2) * DV:(h % 2 + 1) * DV]
                        if j == 0:
                            ins = dve.tensor_copy(STATE[:, h, :], src)
                        else:
                            ins = dve.scalar_tensor_tensor(STATE[:, h, :], STATE[:, h, :], ETOT[:, h * TT + j:h * TT + j + 1],
                                                           src, ALU.mult, ALU.add)
                        if h % 2:
                            free(ins, ("kv", j, h // 2))

            def gla_y(j, i):
                b = full(dve, ("oT", j, i))
                if GO + 1 + j > first["g_b"]:
                    drained(dve, ("fm", GO + j, 1))
                for cc in range(4):
                    c = 4 * i + cc
                    if j == 0:
                        drained(dve, fm_key("r", c))
                    r = R[:, c, tile_of(j)]
                    ins = dve.scalar_tensor_tensor(r, b[:, tile_of(cc)], col(C_GN + c), r, ALU.mult, ALU.mult)
                free(ins, ("oT", j, i))

            def add_branches(c0, c1):
                drained(dve, ("oT", TT - 1, 0))
                drained(dve, ("oT", TT - 1, 1))
                for c in range(c0, c1):
                    drained(dve, fm_key("g_b", c))
                    dve.tensor_tensor(R[:, c, :], R[:, c, :], U[:, c, :], ALU.add).then_inc(m_ready, 1)

            def half_stats(src, j, i):
                return dve.bn_stats(BN[:, j, i, :], src[:, j, 512 * i:512 * i + 512])

            def mean_var(j):
                return dve.bn_aggr(MV[:, j, :], BN[:, j, :, :].rearrange("p a b -> p (a b)"))

            def layer_scale(dst, j, r):
                dve.wait_ge(rstd_done, r)
                return dve.tensor_scalar(dst[:, j, :], dst[:, j, :], MV[:, j, 0:1], RST[:, j:j + 1], ALU.subtract, ALU.mult)

            def v_norm(j):
                dve.wait_ge(av_gelu, TT + j + 1)
                half_stats(VH, j, 0)
                link(half_stats(VH, j, 1))
                mean_var(j).then_inc(ln_var, 1)
                layer_scale(VH, j, MT + TT + H + TT + j + 1).then_inc(vhat_done, 1)

            def w_s_lower():
                for j in range(TT):
                    drained(dve, ("tm", first["v2"] + 2, j))
                for i in range(2):
                    b = full(dve, ("wsT", i))
                    free(dve.tensor_tensor(WST[:, 4 * i:4 * i + 4, :], quarters(b[:, :]),
                                           TRIU[:, :].unsqueeze(1).to_broadcast([P, 4, P]), ALU.mult), ("wsT", i))

            def sg_gate(i):
                if i == 0:
                    dve.wait_ge(bs_in, 16)
                for g in (2 * i, 2 * i + 1):
                    drained(dve, fm_key("a_u", g))
                    b = full(dve, ("sg", g))
                    link(dve.tensor_tensor(quarters(b[:, :]), quarters(b[:, :]),
                                           BS[:, g, :].unsqueeze(1).to_broadcast([P, TT, P]), ALU.add))
                    free(dve.tensor_tensor(U[:, g, :], U[:, g, :], b[:, :], ALU.mult), ("sg", g))

            def side(n):
                if n == 0:
                    for j in range(TT):
                        dve.wait_ge(rstd_done, MT + j + 1)
                        dve.tensor_scalar(XN[:, j, :], RES[:, j, :], RST[:, MT + j:MT + j + 1], None, ALU.mult).then_inc(x_normed, 1)
                if n in (2, first["u"]):
                    i = 0 if n == 2 else 1
                    dve.wait_ge(thin_hi, i + 1)
                    w = THIN_W[i][:, :, :, THIN:]
                    lower(w, THIN_RAW[:, :, :].unsqueeze(2).to_broadcast(w.shape), THIN_W[i][:, :, :, 0:THIN]).then_inc(thin_lo, 1)
                for c in TURN_X.get(n, ()):
                    dve.wait_ge(t_hi, KC + c + 1)
                    free(dve.scalar_tensor_tensor(TL[:, c, :], bank[4 + c % 4][:, :], col(C_NORM + c),
                                                  TH[:, c, :].bitcast(f32), ALU.mult, ALU.subtract), ("xT", c))
                if n == GATES:
                    b, r = full(dve, "thin_gates"), slice(0, 2 * THIN)
                    free(dve.tensor_scalar(GATES_T[:, :], b[r, :], VC[r, C_BG:C_BG + 1], None, ALU.add), "thin_gates")
                if n == LOW:
                    r = slice(4 * THIN, 6 * THIN)
                    dve.wait_ge(gate2_hi, 1)
                    lower(WG2S[r, :], WG2[r, :], WG2S[r, :]).then_inc(gate2_lo, 1)
                    b, r = full(dve, "thin_low"), slice(2 * THIN, 4 * THIN)
                    dve.wait_ge(low_hi, 1)
                    free(dve.scalar_tensor_tensor(ALT[r, :], b[r, :], VC[r, C_LOW:C_LOW + 1], ALT[r, :].bitcast(f32),
                                                  ALU.add, ALU.subtract), "thin_low")
                if n == GATES + 4:
                    gates_logf()
                    dve.wait_ge(tables_in, 16 * 2)
                    dve.wait_ge(masks_in, 16)
                    dve.tensor_copy(MASK[:, :, :], MASKF[:, :, :]).then_inc(masks_set, 1)
                if n == GATES + 5: gates_g()
                if n == GATES + 6: running_max()
                if n == GATES + 7: m_sum()
                if 0 <= n - ML < H: mlstm_weights(n - ML)
                if 0 <= n - ML - 1 < H: mlstm_out(n - ML - 1)
                if 0 <= n - ML - 2 < H: mlstm_y(n - ML - 2)
                if n == AT:
                    dve.memset(UP[:, :, 0:PAD], 0.0)
                    for i in range(2):
                        dve.memset(PW[i][:, 0:PAD], 0.0)
                if 0 <= n - AT - 2 < TT: mem_y(n - AT - 2)
                if 0 <= n - AT < TT: softmax(n - AT)
                if n == first["u"] + 1: pool_window(0); pool_window(1)
                if n == first["u"] + 2: pool_window(2); pool_window(3)
                if n == WO - 1: pool_scaled()
                if n == LG: logits_min()
                if n == LG + 1: logits_cum()
                if n == LV + 4: w_s_lower()
                if 0 <= n - LV < 2 * (LEVELS + 1): level_merge((n - LV) // 2 - 1, (n - LV) % 2)
                if 0 <= n - LV < 2 * LEVELS: (level_operands if (n - LV) % 2 else level_args)((n - LV) // 2)
                if n in (first["a_u"], first["a_u"] + 1):
                    v_norm(2 * (n - first["a_u"]))
                    v_norm(2 * (n - first["a_u"]) + 1)
                if 0 <= n - SG < 4: sg_gate(n - SG)
                if n == GO - 3: q_cum()
                if n == GO - 2: k_dec()
                if n == GO - 1:
                    chunk_split(0)
                    chunk_split(1)
                    k_dec_lower()
                if 0 <= n - GO < TT: gla_norm(n - GO)
                if 0 <= n - GO - 1 < TT:
                    gla_y(n - GO - 1, 0)
                    if n > GO + 1:
                        gla_y(n - GO - 1, 1)
                if 2 <= n - GO + 2 < TT: chunk_split(n - GO + 2)
                if n == WO2 - 1: add_branches(4, 6)

            def add_half(n0, half, scale, j):
                key = ("tm", n0, j)
                b = full(dve, key)
                r = RES[:, j, 512 * half:512 * half + 512]
                free(dve.scalar_tensor_tensor(r, r, scale, b[:, :], ALU.mult, ALU.add), key)
                drained(dve, key)

            def rows_lo(name, j, t0):
                for i in range(2):
                    dve.wait_ge(t_hi, t0 + 2 * j + i + 1)
                    free(lower(TL[:, 4 * i:4 * i + 4, tile_of(j)], quarters(bank[6 + i][:, :]),
                               TH[:, 4 * i:4 * i + 4, tile_of(j)]), (name, j, i))

            def center_rows(n0, j, g, v):
                add_half(n0, 1, ALPHA, j)
                link(half_stats(RES, j, 1))
                mean_var(j).then_inc(ln_var, 1)
                dve.wait_ge(ln_var, v + j + 1)
                dve.scalar_tensor_tensor(RES[:, j, :], RES[:, j, :], MV[:, j, 0:1], g[:, :], ALU.subtract,
                                         ALU.mult).then_inc(centered, 1)

            def scale_rows(j, r, b, c, done, parts=1):
                dve.wait_ge(centered, c + j + 1)
                dve.wait_ge(rstd_done, r + j + 1)
                for i in range(parts):
                    h = slice(i * D // parts, (i + 1) * D // parts)
                    dve.scalar_tensor_tensor(RES[:, j, h], RES[:, j, h], RST[:, j:j + 1], b[:, h], ALU.mult, ALU.add).then_inc(done, 1)

            def drain(n):
                name, i = name_of(n)
                fm = [(("fm", n, t), 2 * i + t) for t in range(2)]
                if name in ("q", "k"):
                    for key, c in fm:
                        conv_taps(c + (4 if name == "k" else 0), key)
                if name == "z_b" and i == 1:
                    pool_y()
                if name == "w_out" and i == 2:
                    for j in range(TT):
                        add_half(n - 2, 0, 1.0, j)
                if name == "w_out" and i == 5:
                    dve.wait_ge(fg_in, 16)

                    def scale(j):
                        dve.wait_ge(rstd_done, MT + TT + H + j + 1)
                        r = RES[:, j, :]
                        dve.scalar_tensor_tensor(r, r, RST[:, 6 + j:7 + j], FG[:, :], ALU.mult, ALU.mult).then_inc(x1_done, 1)

                    for j in range(2):
                        add_half(n - 2, 1, 1.0, j)
                        scale(j)
                    rows_lo("x1T", 0, 2 * KC)
                    add_half(n - 2, 1, 1.0, 2)
                    rows_lo("x1T", 1, 2 * KC)
                    scale(2)
                    add_half(n - 2, 1, 1.0, 3)
                    rows_lo("x1T", 2, 2 * KC)
                    scale(3)
                    rows_lo("x1T", 3, 2 * KC)
                if name in ("q2", "k2"):
                    for key, c in fm:
                        b = full(dve, key)
                        if name == "q2":
                            ins = dve.tensor_scalar(Q2[:, c * S:c * S + S], b[:, :], col(C_B2 + 16 + c), SCALE, ALU.add, ALU.mult)
                        else:
                            ins = dve.tensor_scalar(K2[:, c * S:c * S + S], b[:, :], col(C_B2 + 20 + c), None, ALU.add)
                        free(ins, key)
                if name in ("v2", "a_v") and i % 2:
                    dst, bias = (V2, BV) if name == "v2" else (VH, BAV)
                    h = slice(i // 2 * 512, i // 2 * 512 + 512)
                    dve.wait_ge(bv_in, 32)
                    for j in range(TT):
                        key = ("tm", n - 1, j)
                        b = full(dve, key)
                        free(dve.tensor_tensor(dst[:, j, h], b[:, :], bias[:, h], ALU.add), key)
                if name == "g_a":
                    for key, c in fm:
                        dve.wait_ge(ga_sig, c + 1)
                        drained(dve, ("sg", c))
                        b = full(dve, key)
                        free(dve.tensor_tensor(U[:, c, :], U[:, c, :], b[:, :], ALU.mult), key)
                if n == GO + 1:
                    gla_y(0, 1)
                if name == "g_b":
                    for half in range(2):
                        drained(dve, ("oT", min(n - GO - 1, TT - 1), half))
                    for key, c in fm:
                        dve.wait_ge(gb_sig, c + 1)
                        b = full(dve, key)
                        free(dve.tensor_tensor(R[:, c, :], R[:, c, :], b[:, :], ALU.mult), key)
                    if i == 2:
                        add_branches(0, 4)
                    if i == 3:
                        add_branches(6, 8)
                if name == "w_out2" and i == 1:
                    dve.wait_ge(x1_back, 16)
                    for j in range(TT):
                        add_half(n - 1, 0, ALPHA, j)
                if name == "w_out2" and i == 2:
                    for j in range(TT):
                        half_stats(RES, j, 0)
                if name == "w_out2" and i == 3:
                    dve.wait_ge(ln1_in, 32)
                    r0, t0 = MT + TT + H + 3 * TT, 2 * KC + 2 * TT
                    for j in range(2):
                        center_rows(n - 1, j, L1G, TT)
                        scale_rows(j, r0, L1B, 0, h1_done)
                    rows_lo("h1T", 0, t0)
                    center_rows(n - 1, 2, L1G, TT)
                    rows_lo("h1T", 1, t0)
                    scale_rows(2, r0, L1B, 0, h1_done)
                    center_rows(n - 1, 3, L1G, TT)
                    scale_rows(3, r0, L1B, 0, h1_done)
                    rows_lo("h1T", 2, t0)
                    rows_lo("h1T", 3, t0)

            def stage(n):
                if n + 1 >= ff1_0:
                    return
                name, i = name_of(n + 1)
                slot = OWN.get(n + 1, i % 2)
                if name == "w_out":
                    g = WO_GROUPS[i % 3]
                    split_x(slot, i, Y[:, 4 * g:4 * g + 4, :].rearrange("p a b -> p (a b)"))
                if name == "w_out2":
                    g = i % 2
                    split_x(slot, E_WO2 + i, R[:, 4 * g:4 * g + 4, :].rearrange("p a b -> p (a b)"))

            dve.wait_ge(columns_in, 16)
            for j in range(MT):
                dve.wait_ge(rstd_done, j + 1)
                dve.tensor_scalar(MEM[:, j, :], MEM[:, j, :], RST[:, j:j + 1], None, ALU.mult).then_inc(mem_normed, 1)
            dve.wait_ge(w_hi, 1)
            lower(WL[0][:, 0:1024], RAW[0][:, 0:1024], WH[0][:, 0:1024]).then_inc(w_lo, 1)
            for c in range(KC):
                dve.wait_ge(t_hi, (c | 1) + 1)
                q = (c % 2) * NMEM
                ins = dve.scalar_tensor_tensor(MEML[:, c, :], bank[4 + c // 2][:, q:q + NMEM], col(C_MEMN + c),
                                               MEMH[:, c, :].bitcast(f32), ALU.mult, ALU.subtract)
                if c % 2:
                    free(ins, ("memT", c // 2))
            for n in range(ff1_0):
                split(n + 1)
                side(n)
                if n + 1 not in PAIRED:
                    stage(n)
                if n + 2 in PAIRED:
                    stage(n + 1)
                drain(n)

            def squares(m, group, more=0):
                for t in range(2):
                    dve.wait_ge(bank_free[t], more + (f0[t] + m + 1))
                    q = (2 * m + t) % 4 * S
                    f = F1[:, group, q:q + S]
                    dve.tensor_tensor(f, f, f, ALU.mult).then_inc(f1_done, 1)

            split(ff1_0 + 1)
            squares(0, 0)
            with dve.Fori(0, 7) as i:
                split(ff1_0 + 2, i * 2)
                squares(1, i, i * 2)
                split(ff1_0 + 3, i * 2)
                squares(2, i + 1, i * 2)
            split(ff2_0)
            split_x(0, E_FF2, F1[:, 0, :])
            squares(15, 7)

            for half in range(2):
                n0, e0 = ff2_0 + 8 * half, E_FF2 + 8 * half
                for g in (1, 2):
                    split(n0 + g)
                    split_x(g % 2, e0 + g, F1[:, g, :])
                with dve.Fori(0, 2) as i:
                    for g in (3, 4):
                        split(n0 + g, i * 2)
                        split_x(g % 2, e0 + g, F1[:, i * 2 + g, :], i * 2)
                if half == 1:
                    split_x(3, e0 + 7, F1[:, 7, :])
                    split(n0 + 7)
                else:
                    split(n0 + 7)
                    split_x(1, e0 + 7, F1[:, 7, :])
                    split(n0 + 8)
                    split_x(0, e0 + 8, F1[:, 0, :])
                    for j in range(TT):
                        add_half(n0, 0, ALPHA, j)
                        half_stats(RES, j, 0)
            dve.wait_ge(ln2_in, 32)
            for j in range(TT):
                center_rows(ff2_0 + 8, j, L2G, 2 * TT)
                scale_rows(j, MT + TT + H + 4 * TT, L2B, TT, h2_done, 2 if j == TT - 1 else 1)

        @block.gpsimd
        def _(pool):
            links, roots = [0], [0]

            def link(ins):
                links[0] += 1
                ins.then_inc(pool_chain, 1)
                pool.wait_ge(pool_chain, links[0])

            def rstd(dst, src, w, mean, eps):
                if roots[0]:
                    pool.wait_ge(rstd_done, roots[0])
                roots[0] += 1
                link(pool.tensor_scalar(RTMP[:, 0:w], src, mean, eps, ALU.mult, ALU.add))
                pool.tensor_tensor(dst, RTMP[:, 0:w], NHALF[:, 0:w], ALU.pow).then_inc(rstd_done, 1)

            def split_own(n):
                pool.wait_ge(w_hi, n + 1)
                pool.tensor_tensor(WL[2][:, :], RAW[n % 2][:, :], WH[2][:, :].bitcast(f32), ALU.subtract).then_inc(own_lo, 1)

            def load_all(dst, src, s):
                pool.dma_start(dst, src.partition_broadcast(P)).then_inc(s, 16)

            pool.memset(ONES[:, :], 1.0).then_inc(ones_set, 1)
            pool.memset(V[:, :, :, P:P + 1], 1.0).then_inc(ones_set, 1)
            link(pool.memset(NHALF[:, :], -0.5))
            for c in range(MT + TT):
                if c == MT:
                    pool.wait_ge(w0_hi, 1)
                    pool.tensor_tensor(WL[0][:, 1024:], RAW[0][:, 1024:], WH[0][:, 1024:].bitcast(f32), ALU.subtract).then_inc(w0_lo, 1)
                pool.wait_ge(squared, c + 1)
                rstd(RST[:, c:c + 1], SSQ[:, c:c + 1], 1, 1.0, RMS_EPS)
            pool.wait_ge(m_done, 1)
            pool.dma_start(m_spill, MROW[:, :]).then_inc(m_spilled, 16)
            pool.wait_ge(m_spilled, 16)
            pool.dma_start(MB[:, :, :], m_spill.partition_broadcast(P)).then_inc(mb_in, 16)
            for h in range(H):
                pool.wait_ge(ml_ss, h + 1)
                rstd(RST[:, 10:14], SSQ[:, 10:14], 4, 1 / P, RMS_EPS)
            pool.wait_ge(ml_h, H)
            pool.dma_start(POOLW[:, :, :], a["pool_w"][0].rearrange("g c d -> c g d")).then_inc(poolw_in, 16)
            full(pool, ("yc", TT - 1))
            load_all(BV[:, :], a["b_in_2"][0, 3 * D:4 * D], bv_in)
            load_all(BAV[:, :], a["b_in_2"][0, D:2 * D], bv_in)
            split_own(WO + 6)
            for j in range(TT):
                pool.wait_ge(squared, MT + TT + j + 1)
                rstd(RST[:, 6 + j:7 + j], SSQ[:, 6 + j:7 + j], 1, 1.0, RMS_EPS)
            pool.wait_ge(x1_done, TT)
            pool.dma_start(x1_spill.rearrange("(j p) n -> p j n", p=P), RES[:, :, :]).then_inc(x1_spilled, 16)
            for t in (SC[:, :, :], KE[:, :]):
                pool.memset(t, 0.0).then_inc(zeros_set, 1)
            pool.wait_ge(x1_spilled, 16)
            for i in range(2):
                drained(pool, ("x1T", TT - 1, i))
            pool.dma_start(WSR[:, :, :], a["sg_w_s_2"][0].rearrange("g t s -> t g s")).then_inc(ws_in, 16)
            full(pool, ("lg", TT - 1))
            load_all(SGG[:, :], a["sg_ln_g_2"][0], sg_in)
            load_all(SGB[:, :], a["sg_ln_b_2"][0], sg_in)
            for j in range(TT):
                drained(pool, ("tm", first["a_v"] + 2, j))
            load_all(BS[:, :, :], a["sg_b_s_2"][0], bs_in)
            pool.wait_ge(sg_in, 32)

            def v_gain(j):
                link(pool.tensor_tensor(VH[:, j, :], VH[:, j, :], SGG[:, :], ALU.mult))
                pool.tensor_tensor(VH[:, j, :], VH[:, j, :], SGB[:, :], ALU.add).then_inc(vh_ready, 1)

            for j in range(TT):
                pool.wait_ge(ln_var, j + 1)
                rstd(RST[:, j:j + 1], MV[:, j, 1:2], 1, 1.0, LN_EPS)
                if j:
                    pool.wait_ge(vhat_done, j)
                    v_gain(j - 1)
            pool.wait_ge(vhat_done, TT)
            v_gain(TT - 1)
            for j in range(TT):
                pool.wait_ge(squared, MT + 2 * TT + H * (j + 1))
                rstd(RST[:, 10:14], SSQ[:, 10:14], 4, 1.0, LN_EPS)
            pool.wait_ge(m_ready, KC)
            pool.dma_start(RES[:, :, :], x1_spill.rearrange("(j p) n -> p j n", p=P)).then_inc(x1_back, 16)
            load_all(L1G[:, :], a["ln1_g_2"][0], ln1_in)
            load_all(L1B[:, :], a["ln1_b_2"][0], ln1_in)
            load_all(L2G[:, :], a["ln2_g_2"][0], ln2_in)
            load_all(L2B[:, :], a["ln2_b_2"][0], ln2_in)
            split_own(ff1_0)
            for j in range(2 * TT):
                pool.wait_ge(ln_var, TT + j + 1)
                rstd(RST[:, j % TT:j % TT + 1], MV[:, j % TT, 1:2], 1, 1.0, LN_EPS)

        @block.sync
        def _(sp):
            def load(n, src, more=0):
                if n >= 2:
                    sp.wait_ge(w_lo, more + (n - 1))
                k, c = blocks[n][2].shape[1:]
                sp.dma_start(RAW[n % 2][:, 0:k * c].rearrange("p (k c) -> p k c", c=c), src).then_inc(w_loaded[n % 2], 16)

            for j in range(MT):
                sp.dma_start(MEM[:, j, :], a["mem"][0, j * P:j * P + P, :]).then_inc(mem_in[j], 16)
            for i, s in enumerate((w0_loaded, w_loaded[0])):
                k = slice(KC // 2 * i, KC // 2 * (i + 1))
                sp.dma_start(RAW[0][:, :].rearrange("p (k c) -> p k c", k=KC)[:, k, :], blocks[0][2][:, k, :]).then_inc(s, 16)
            load(1, blocks[1][2])
            for j in range(TT):
                sp.dma_start(RES[:, j, :], a["x"][0, j * P:j * P + P, :]).then_inc(x_in[j], 16)
            sp.wait_ge(w0_lo, 1)
            load(2, blocks[2][2])
            load(3, blocks[3][2])

            def thin_load(w, c):
                sp.dma_start(THIN_RAW[:, :, :], w[0].rearrange("(k p) n -> p k n", p=P)[:, :, c:c + THIN]).then_inc(thin_in, 16)

            thin_load(a["w_in"], 5 * GW)
            load(4, blocks[4][2])
            sp.dma_start(TRIU[:, :], a["c_triu"]).then_inc(tables_in, 16)
            sp.dma_start(PINV[:, :, :], a["c_pool_edge"].partition_broadcast(P)).then_inc(tables_in, 16)
            sp.dma_start(MASKF[:, :, :], a["c_masks"]).then_inc(masks_in, 16)
            sp.dma_start(FG[:, :], a["final_norm_g"].partition_broadcast(P)).then_inc(fg_in, 16)
            for i in range(STACK // THIN):
                sp.dma_start(WG2[THIN * i:THIN * (i + 1), :], a["gla_w_gate2_2"][0]).then_inc(wg2_in, 16)
            for n in range(5, ff1_0):
                load(n, blocks[n][2])
                if n == GATES + 5:
                    sp.wait_ge(thin_lo, 1)
                    thin_load(a["w_in_2"], 5 * D)
            up = a["w_ff1_2"][0].rearrange("(k p) (b c) -> b p k c", p=P, c=256)
            with sp.Fori(0, 8) as i:
                for b in range(2):
                    load(ff1_0 + b, up[i * 2 + b], i * 2)
            down = a["w_ff2_2"][0].rearrange("(g k p) (h c) -> h g p k c", p=P, k=4, h=2)
            for half in range(2):
                with sp.Fori(0, 4) as i:
                    for b in range(2):
                        load(ff2_0 + 8 * half + b, down[half, i * 2 + b], i * 2)
            for j in range(TT - 1):
                sp.wait_ge(h2_done, j + 1)
                sp.dma_start(out[0, j * P:j * P + P, :], RES[:, j, :]).then_inc(stored, 16)
            for i in range(2):
                sp.wait_ge(h2_done, TT + i)
                h = slice(i * D // 2, (i + 1) * D // 2)
                sp.dma_start(out[0, S - P:S, h], RES[:, TT - 1, h]).then_inc(stored, 16)
            sp.wait_ge(stored, 16 * (TT + 1))


def constants():
    s, t = np.arange(P)[:, None], np.arange(P)[None, :]
    masks = np.zeros((P, LEVELS + 1, P), np.float32)
    for l in range(LEVELS):
        half = P >> (l + 1)
        masks[:, l] = (s // (2 * half) == t // (2 * half)) & (s % (2 * half) < half) & (t % (2 * half) >= half)
    masks[:, LEVELS] = s == t
    edge = 1 / np.minimum(np.arange(1, 17)[None, :], np.array(WINDOWS)[:, None]).astype(np.float32)
    return {"c_ident": (s == t).astype(np.float32), "c_triu": (s <= t).astype(np.float32),
            "c_masks": masks, "c_pool_edge": edge.astype(np.float32)}


def vector_columns(i):
    b_in = i["b_in_2"][0]
    low = 5 * D
    b_low = np.concatenate([b_in[low:low + THIN], np.zeros(THIN, np.float32)] * 3 + [np.zeros(P - STACK, np.float32)])
    rows = [i["norm_g"][0], i["mem_norm_g"][0], i["conv_w"][0].reshape(-1), i["conv_b"][0], i["mlstm_norm_g"][0],
            i["pool_scale"][0], b_in[:low], b_in[low + 16:], i["gla_norm_g_2"][0], b_low, i["b_gates"][0], np.zeros(P - 2 * H, np.float32),
            i["gla_b_gate_2"][0]]
    rows = np.concatenate([np.asarray(r) for r in rows])
    return rows.reshape(-1, P).T


def kernel(**inputs):
    import concourse.bacc as bacc
    from concourse import mybir
    from concourse.bass_utils import run_bass_kernel_spmd

    nc = bacc.Bacc("TRN2", target_bir_lowering=False, num_devices=1)
    arrays = {f"in_{k}": np.ascontiguousarray(v) for k, v in inputs.items()}
    arrays["in_vector_columns"] = np.ascontiguousarray(vector_columns(inputs))
    arrays.update({f"in_{k}": v for k, v in constants().items()})
    a = {k[3:]: nc.dram_tensor(k, v.shape, mybir.dt.from_np(v.dtype), kind="ExternalInput").ap() for k, v in arrays.items()}
    out = nc.dram_tensor("out_0", (1, S, D), mybir.dt.float32, kind="ExternalOutput").ap()
    x1_spill = nc.dram_tensor("x1_spill", (S, D), mybir.dt.float32, kind="Internal").ap()
    m_spill = nc.dram_tensor("m_spill", (H, S), mybir.dt.float32, kind="Internal").ap()
    two_blocks(nc, a, out, x1_spill, m_spill)
    r = run_bass_kernel_spmd(nc, [arrays], core_ids=[0])
    return r.results[0]["out_0"]
```
